# Optimizing a Trainium2 kernel written in Bass

```python
import jax, jax.numpy as jnp
from jax import lax
import numpy as np

D_MODEL = 1024
BATCH = 1
SEQ = 512
DEPTH = 2

GRID_W = 64
CTX_LEN = 256
EPS = 1e-6
CONV_CH = 512
CONV_WIDTH = 31
N_HEADS = 8
QK_NOPE = 64
QK_ROPE = 32
V_HEAD = 64
Q_LORA = 256
KV_LORA = 128
ROPE_BASE = 10000.0
Q_BLOCK = 128
SC_CH = D_MODEL
SC_WIDTH = 3
N_EXPERTS = 64
TOP_K = 6
N_GROUPS = 8
TOPK_GROUPS = 4
D_EXPERT = 256
D_SHARED = 256
ROUTED_SCALE = 2.5
ROUTE_BLOCK = 128
N_EVEN = (DEPTH + 1) // 2
N_ODD = DEPTH // 2
IN_A = 2 * CONV_CH
IN_EVEN = IN_A + Q_LORA + KV_LORA + QK_ROPE
OUT_EVEN = CONV_CH + N_HEADS * V_HEAD

kernel_name = "hybrid_convmla_shortconv_moe_dit"

def rmsnorm(x, w):
    xf = x.astype(jnp.float32)
    y = xf * lax.rsqrt(jnp.mean(xf * xf, axis=-1, keepdims=True) + EPS)
    return (y * w.astype(jnp.float32)).astype(x.dtype)

def layernorm(x, w, b):
    xf = x.astype(jnp.float32)
    mu = jnp.mean(xf, axis=-1, keepdims=True)
    var = jnp.mean(jnp.square(xf - mu), axis=-1, keepdims=True)
    y = (xf - mu) * lax.rsqrt(var + EPS)
    return (y * w.astype(jnp.float32) + b.astype(jnp.float32)).astype(x.dtype)

def modulate(h, shift, scale):
    return h * (1 + scale) + shift

def axial_rope_tables(n):
    rows = n // GRID_W
    row = jnp.repeat(jnp.arange(rows), GRID_W).astype(jnp.float32)
    col = jnp.tile(jnp.arange(GRID_W), rows).astype(jnp.float32)
    half = QK_ROPE // 2
    inv = 1.0 / (ROPE_BASE ** (jnp.arange(0, half, 2, dtype=jnp.float32) / half))
    ang = jnp.stack([row[:, None] * inv, col[:, None] * inv], axis=1)
    return jnp.cos(ang), jnp.sin(ang)

def apply_rope(x, cos, sin):
    xr = x.reshape(x.shape[:-1] + (2, 2, QK_ROPE // 4))
    x1, x2 = xr[..., 0, :], xr[..., 1, :]
    out = jnp.stack([x1 * cos - x2 * sin, x2 * cos + x1 * sin], axis=-2)
    return out.reshape(x.shape).astype(x.dtype)

def dwconv(v, w):
    pad = w.shape[0] // 2
    return lax.conv_general_dilated(v, w.astype(v.dtype), (1,), [(pad, pad)],
                                    dimension_numbers=('NWC', 'WIO', 'NWC'),
                                    feature_group_count=v.shape[-1])

def conformer_conv(u, conv_w, conv_b, ln_w, ln_b):
    a, g = jnp.split(u, 2, axis=-1)
    y = dwconv(a * jax.nn.sigmoid(g), conv_w) + conv_b
    return jax.nn.silu(layernorm(y, ln_w, ln_b))

def mla_kv(ckv, k_rope, kv_norm_w, w_ukv, rope):
    kv = jnp.einsum('bnc,chd->bnhd', rmsnorm(ckv, kv_norm_w), w_ukv)
    k_nope, v = kv[..., :QK_NOPE], kv[..., QK_NOPE:]
    if rope is not None:
        k_rope = apply_rope(k_rope, rope[0], rope[1])
    k_rope = jnp.broadcast_to(k_rope[:, :, None, :], k_nope.shape[:-1] + (QK_ROPE,))
    return jnp.concatenate([k_nope, k_rope.astype(k_nope.dtype)], axis=-1), v

def mla_q(cq, q_norm_w, w_uq, rope):
    q = jnp.einsum('bnc,chd->bnhd', rmsnorm(cq, q_norm_w), w_uq)
    if rope is not None:
        q_rope = apply_rope(q[..., QK_NOPE:], rope[0][:, None], rope[1][:, None])
        q = jnp.concatenate([q[..., :QK_NOPE], q_rope], axis=-1)
    return q

def attend(q, k, v):
    scale = (QK_NOPE + QK_ROPE) ** -0.5
    s = jnp.einsum('bqhd,bkhd->bhqk', q, k).astype(jnp.float32) * scale
    p = jax.nn.softmax(s, axis=-1)
    return jnp.einsum('bhqk,bkhd->bqhd', p.astype(v.dtype), v)

def blocked_attention(q, k, v):
    B, n, H, dq = q.shape
    nb = n // Q_BLOCK
    qb = q.reshape(B, nb, Q_BLOCK, H, dq).transpose(1, 0, 2, 3, 4)
    out = lax.map(lambda qi: attend(qi, k, v), qb)
    return out.transpose(1, 0, 2, 3, 4).reshape(B, n, H, v.shape[-1])

def split_even(u):
    o1, o2, o3 = IN_A, IN_A + Q_LORA, IN_A + Q_LORA + KV_LORA
    return u[..., :o1], u[..., o1:o2], u[..., o2:o3], u[..., o3:]

def even_mixer(a, ac, w_in, conv_w, conv_b, ln_w, ln_b, q_norm_w, kv_norm_w, w_uq, w_ukv, w_out, rope, ctx_out):
    B, n, _ = a.shape
    u_a, cq, ckv, kr = split_even(a @ w_in)
    if ctx_out:
        uc_a, cq_c, ckv_c, kr_c = split_even(ac @ w_in)
    else:
        uc_kv = ac @ w_in[:, IN_A + Q_LORA:]
        ckv_c, kr_c = uc_kv[..., :KV_LORA], uc_kv[..., KV_LORA:]
    k_c, v_c = mla_kv(ckv_c, kr_c, kv_norm_w, w_ukv, None)
    k_l, v_l = mla_kv(ckv, kr, kv_norm_w, w_ukv, rope)
    q_l = mla_q(cq, q_norm_w, w_uq, rope)
    o_b = blocked_attention(q_l, jnp.concatenate([k_c, k_l], axis=1), jnp.concatenate([v_c, v_l], axis=1))
    o_a = conformer_conv(u_a, conv_w, conv_b, ln_w, ln_b)
    y = jnp.concatenate([o_a, o_b.reshape(B, n, N_HEADS * V_HEAD)], axis=-1) @ w_out
    if not ctx_out:
        return y, None
    o_bc = attend(mla_q(cq_c, q_norm_w, w_uq, None), k_c, v_c)
    o_ac = conformer_conv(uc_a, conv_w, conv_b, ln_w, ln_b)
    yc = jnp.concatenate([o_ac, o_bc.reshape(B, ac.shape[1], N_HEADS * V_HEAD)], axis=-1) @ w_out
    return y, yc

def short_conv_mixer(h, w_in, conv_w, w_out):
    b, cg, xt = jnp.split(h @ w_in, 3, axis=-1)
    return (b * dwconv(cg * xt, conv_w)) @ w_out

def moe_ffn(h, router_w, router_bias, w_gate, w_up, w_down, sw_gate, sw_up, sw_down):
    T, D = h.shape
    scores = jax.nn.sigmoid((h @ router_w).astype(jnp.float32))
    sel = scores + router_bias.astype(jnp.float32)
    gscore = lax.top_k(sel.reshape(T, N_GROUPS, N_EXPERTS // N_GROUPS), 2)[0].sum(-1)
    _, gidx = lax.top_k(gscore, TOPK_GROUPS)
    gmask = jnp.any(gidx[..., None] == jnp.arange(N_GROUPS), axis=1)
    emask = jnp.repeat(gmask, N_EXPERTS // N_GROUPS, axis=1)
    _, eidx = lax.top_k(jnp.where(emask, sel, -jnp.inf), TOP_K)
    wts = jnp.take_along_axis(scores, eidx, axis=1)
    wts = wts / jnp.sum(wts, axis=-1, keepdims=True) * ROUTED_SCALE
    TK = T * TOP_K
    flat_e = eidx.reshape(-1)
    flat_tok = jnp.arange(TK, dtype=jnp.int32) // TOP_K
    order = jnp.argsort(flat_e)
    se, stok, sw = flat_e[order], flat_tok[order], wts.reshape(-1)[order]
    counts = jnp.bincount(flat_e, length=N_EXPERTS)
    starts = jnp.cumsum(counts) - counts
    pcounts = ((counts + ROUTE_BLOCK - 1) // ROUTE_BLOCK) * ROUTE_BLOCK
    pends = jnp.cumsum(pcounts)
    pstarts = pends - pcounts
    dest = pstarts[se] + (jnp.arange(TK) - starts[se])
    NB = -(-TK // ROUTE_BLOCK) + N_EXPERTS
    P = NB * ROUTE_BLOCK
    row_tok = jnp.full((P,), T, dtype=jnp.int32).at[dest].set(stok)
    row_w = jnp.zeros((P,), dtype=h.dtype).at[dest].set(sw.astype(h.dtype))
    block_e = jnp.minimum(jnp.searchsorted(pends, jnp.arange(NB) * ROUTE_BLOCK, side='right'), N_EXPERTS - 1)
    h_pad = jnp.concatenate([h, jnp.zeros((1, D), h.dtype)], axis=0)

    def run_block(args):
        toks, bw, e = args
        xb = h_pad[toks]
        act = jax.nn.silu(xb @ w_gate[e]) * (xb @ w_up[e])
        return (act @ w_down[e]) * bw[:, None]

    yb = lax.map(run_block, (row_tok.reshape(NB, ROUTE_BLOCK), row_w.reshape(NB, ROUTE_BLOCK), block_e))
    routed = jax.ops.segment_sum(yb.reshape(P, D), row_tok, num_segments=T + 1)[:T]
    shared = (jax.nn.silu(h @ sw_gate) * (h @ sw_up)) @ sw_down
    return (routed + shared).astype(h.dtype)

def setup_inputs(seed: int = 0) -> dict:
    key = jax.random.key(seed)
    ks = iter(jax.random.split(key, 40))

    def nrm(shape, scale):
        return jax.random.normal(next(ks), shape, jnp.float32) * scale

    def gain(shape):
        return 1.0 + nrm(shape, 0.05)

    D = D_MODEL
    return {
        "x": nrm((BATCH, SEQ, D), 1.0),
        "c": nrm((BATCH, D), 1.0),
        "ctx": nrm((BATCH, CTX_LEN, D), 1.0),
        "c_ctx": nrm((D,), 1.0),
        "ada_w": nrm((DEPTH, D, 6 * D), 0.5 * D ** -0.5),
        "ada_b": nrm((DEPTH, 6 * D), 0.02),
        "norm_mix_w": gain((DEPTH, D)),
        "norm_ffn_w": gain((DEPTH, D)),
        "ev_w_in": nrm((N_EVEN, D, IN_EVEN), D ** -0.5),
        "ev_conv_w": nrm((N_EVEN, CONV_WIDTH, 1, CONV_CH), CONV_WIDTH ** -0.5),
        "ev_conv_b": nrm((N_EVEN, CONV_CH), 0.02),
        "ev_ln_w": gain((N_EVEN, CONV_CH)),
        "ev_ln_b": nrm((N_EVEN, CONV_CH), 0.02),
        "ev_q_norm_w": gain((N_EVEN, Q_LORA)),
        "ev_kv_norm_w": gain((N_EVEN, KV_LORA)),
        "ev_w_uq": nrm((N_EVEN, Q_LORA, N_HEADS, QK_NOPE + QK_ROPE), Q_LORA ** -0.5),
        "ev_w_ukv": nrm((N_EVEN, KV_LORA, N_HEADS, QK_NOPE + V_HEAD), KV_LORA ** -0.5),
        "ev_w_out": nrm((N_EVEN, OUT_EVEN, D), OUT_EVEN ** -0.5),
        "od_w_in": nrm((N_ODD, D, 3 * SC_CH), D ** -0.5),
        "od_conv_w": nrm((N_ODD, SC_WIDTH, 1, SC_CH), SC_WIDTH ** -0.5),
        "od_w_out": nrm((N_ODD, SC_CH, D), SC_CH ** -0.5),
        "router_w": nrm((DEPTH, D, N_EXPERTS), D ** -0.5),
        "router_bias": nrm((DEPTH, N_EXPERTS), 0.01),
        "exp_w_gate": nrm((DEPTH, N_EXPERTS, D, D_EXPERT), D ** -0.5),
        "exp_w_up": nrm((DEPTH, N_EXPERTS, D, D_EXPERT), D ** -0.5),
        "exp_w_down": nrm((DEPTH, N_EXPERTS, D_EXPERT, D), D_EXPERT ** -0.5),
        "sh_w_gate": nrm((DEPTH, D, D_SHARED), D ** -0.5),
        "sh_w_up": nrm((DEPTH, D, D_SHARED), D ** -0.5),
        "sh_w_down": nrm((DEPTH, D_SHARED, D), D_SHARED ** -0.5),
        "final_norm_w": gain((D,)),
    }

def reference(x, c, ctx, c_ctx, ada_w, ada_b, norm_mix_w, norm_ffn_w, ev_w_in, ev_conv_w, ev_conv_b, ev_ln_w,
              ev_ln_b, ev_q_norm_w, ev_kv_norm_w, ev_w_uq, ev_w_ukv, ev_w_out, od_w_in, od_conv_w, od_w_out,
              router_w, router_bias, exp_w_gate, exp_w_up, exp_w_down, sh_w_gate, sh_w_up, sh_w_down,
              final_norm_w):
    B, N, D = x.shape
    rope = axial_rope_tables(N)
    h, hc = x, ctx
    for i in range(DEPTH):
        reads_ctx = i % 2 == 0
        ctx_out = any(j % 2 == 0 for j in range(i + 1, DEPTH))
        m = jax.nn.silu(c) @ ada_w[i] + ada_b[i]
        sh1, sc1, g1, sh2, sc2, g2 = jnp.split(m[:, None, :], 6, axis=-1)
        a = modulate(rmsnorm(h, norm_mix_w[i]), sh1, sc1)
        if reads_ctx or ctx_out:
            mc = jax.nn.silu(c_ctx) @ ada_w[i] + ada_b[i]
            csh1, csc1, cg1, csh2, csc2, cg2 = jnp.split(mc, 6)
            ac = modulate(rmsnorm(hc, norm_mix_w[i]), csh1, csc1)
        if i % 2 == 0:
            e = i // 2
            y, yc = even_mixer(a, ac, ev_w_in[e], ev_conv_w[e], ev_conv_b[e], ev_ln_w[e], ev_ln_b[e],
                               ev_q_norm_w[e], ev_kv_norm_w[e], ev_w_uq[e], ev_w_ukv[e], ev_w_out[e], rope, ctx_out)
        else:
            o = i // 2
            y = short_conv_mixer(a, od_w_in[o], od_conv_w[o], od_w_out[o])
            yc = short_conv_mixer(ac, od_w_in[o], od_conv_w[o], od_w_out[o]) if ctx_out else None
        h = h + g1 * y
        f = modulate(rmsnorm(h, norm_ffn_w[i]), sh2, sc2)
        moe_args = (router_w[i], router_bias[i], exp_w_gate[i], exp_w_up[i], exp_w_down[i],
                    sh_w_gate[i], sh_w_up[i], sh_w_down[i])
        if ctx_out:
            hc = hc + cg1 * yc
            fc = modulate(rmsnorm(hc, norm_ffn_w[i]), csh2, csc2)
            nc = fc.shape[0] * fc.shape[1]
            out = moe_ffn(jnp.concatenate([fc.reshape(-1, D), f.reshape(-1, D)], axis=0), *moe_args)
            hc = hc + cg2 * out[:nc].reshape(hc.shape)
            h = h + g2 * out[nc:].reshape(h.shape)
        else:
            h = h + g2 * moe_ffn(f.reshape(-1, D), *moe_args).reshape(h.shape)
    return rmsnorm(h, final_norm_w)


_drawn_inputs = setup_inputs


def setup_inputs(seed=0):
    import zlib

    import numpy as np

    out = dict(_drawn_inputs(seed))
    spreads = {}
    factors = {'ev_q_norm_w': 2.899}
    for name, (base, spread) in spreads.items():
        noise = np.random.default_rng([zlib.crc32(name.encode()), seed]).standard_normal(out[name].shape)
        drawn = base * np.exp(spread * noise) if base else spread * noise
        out[name] = __import__('jax').numpy.asarray(drawn.astype(out[name].dtype))
    for name, factor in factors.items():
        out[name] = (out[name] * factor).astype(out[name].dtype)
    return out
```

```python
import concourse.bass as bass
from concourse import mybir
from contextlib import ExitStack
import numpy as np

P = 128
D = 1024
N = 512
NCTX = 256
KEYS = NCTX + N
KC = D // P
TT, TC = N // P, NCTX // P
CONV, TAPS = 512, 31
PAD = TAPS // 2
CC = CONV // P
HEADS, NOPE, ROPE, VH = 8, 64, 32, 64
QL, KVL = 256, 128
LAT = QL + KVL + ROPE
EXPERTS, TOPK, GROUPS, TOPG = 64, 6, 8, 4
GE = EXPERTS // GROUPS
DE = 256
ROUTED_SCALE = 2.5
EPS = 1e-6
ATT_SCALE = float(NOPE + ROPE) ** -0.5
SC = 1024
SCC = SC // P
MAXB = (N * TOPK + EXPERTS * (P - 1)) // P
MAXP = (MAXB + 1) // 2
COLS = 2 * MAXP + 4
EMPTY = 65536
HB = 512
DEPTH = 2


def build(nc, a, out, scratch):
    f32, i32, u32 = mybir.dt.float32, mybir.dt.int32, mybir.dt.uint32
    ALU, ACT, AX = mybir.AluOpType, mybir.ActivationFunctionType, mybir.AxisListType
    F_dram, Y_dram = scratch
    x, c, ctx_in, c_ctx = a["x"], a["c"], a["ctx"], a["c_ctx"]

    stack = ExitStack()
    with stack:
        sem = lambda name: stack.enter_context(nc.semaphore(name))
        both = lambda name: [sem(f"{name}_{b}") for b in range(2)]
        layers = lambda name: [sem(f"{name}_l{l}") for l in range(DEPTH)]
        keep = lambda name, shape, dt=f32: stack.enter_context(nc.sbuf_tensor(name, shape, dt))

        h = keep("h", [P, TT, D])
        ident = keep("ident", [P, P])
        ones = keep("ones", [P, P])
        before = keep("before", [P, P])
        iota_row = keep("iota_row", [P, P])
        iota_part = keep("iota_part", [P, 1])
        pair_val = keep("pair_val", [P, TT, 8])
        one_over = keep("one_over", [P, P])
        first_row = keep("first_row", [2, P])
        ccol = keep("ccol", [P, 2, KC])
        csil = keep("csil", [P, 2, KC])
        acol = keep("acol", [P, 2, KC, 2])
        g1b = keep("g1b", [P, D])
        g2b = keep("g2b", [P, D])
        a2b = keep("a2b", [P, D])
        b2b = keep("b2b", [P, D])
        nrow = keep("nrow", [2, D])
        mrow = keep("mrow", [2, 2, D])
        adab = keep("adab", [P, 2, HB])
        adaw = keep("adaw", [P, 2, KC, HB])
        ssq = keep("ssq", [P, 24])
        rstd = keep("rstd", [P, 24])
        rope = keep("rope", [P, N])
        cvw = keep("cvw", [P, CC, TAPS + 3])
        odw = keep("odw", [P, SCC, 3])
        qnw = keep("qnw", [P, 2])
        kvw = keep("kvw", [P, 1])

        def region():
            return ExitStack()

        r0 = region()
        m0 = lambda name, shape, dt=f32: r0.enter_context(nc.sbuf_tensor(name, shape, dt))
        aT = m0("aT", [P, KC, KEYS])
        wlat = m0("wlat", [P, KC, LAT + ROPE])
        wab = m0("wab", [P, 2, KC, 2, P])
        vv = wab.rearrange("p b k j n -> p (b k j n)")[:, 0:(TT + TC) * HEADS * VH].rearrange("p (t n) -> p t n", n=HEADS * VH)
        wuq = m0("wuq", [P, 2, HEADS, P])
        wukv = m0("wukv", [P, HEADS, NOPE + VH])
        r0e = region()
        m0e = lambda name, shape, dt=f32: r0e.enter_context(nc.sbuf_tensor(name, shape, dt))
        r0l = region()
        m0l = lambda name, shape, dt=f32: r0l.enter_context(nc.sbuf_tensor(name, shape, dt))
        crow = m0e("crow", [TAPS + 3, CONV])
        orow = m0e("orow", [3, D])
        rn = m0e("rn", [P, TT + TC, D])
        hc = m0e("hc", [P, TC, D])
        r0e.close()
        pe_ = m0l("pe_", [P, 2, KEYS])
        pT = m0l("pT", [P, 2, KEYS])
        kT = m0l("kT", [P, 2, KEYS])
        qT = m0l("qT", [P, 2, N])
        vpad = m0l("vpad", [P, CC, N + 2 * PAD])
        cy = m0l("cy", [P, CC, N])
        csg = m0l("csg", [P, 2, N])
        cqT = m0l("cqT", [P, 2, N])
        ckvT = m0l("ckvT", [P, KEYS])
        krT = m0l("krT", [P, KEYS])
        stat = m0l("stat", [P, 4, 3])
        r0l.close()
        r0q = region()
        cqs = r0q.enter_context(nc.sbuf_tensor("cqs", [P, TT + TC, QL + KVL], f32))
        r0q.close()
        r0.close()
        r0b = region()
        m0b = lambda name, shape, dt=f32: r0b.enter_context(nc.sbuf_tensor(name, shape, dt))
        catT = m0b("catT", [P, 2, CC, N])
        oo = m0b("oo", [P, TT, HEADS * VH])
        r0b.close()
        rt = adab
        wo0 = adaw

        r1 = region()
        m1 = lambda name, shape, dt=f32: r1.enter_context(nc.sbuf_tensor(name, shape, dt))
        rn1 = m1("rn1", [P, TT, D])
        aT1 = m1("aT1", [P, KC, N])
        w3 = m1("w3", [P, 3, KC, 3, P])
        zz = m1("zz", [P, 2, N + 2])
        cgs = m1("cgs", [P, 2, N])
        zt = m1("zt", [P, 2, N])
        oT1 = m1("oT1", [P, SCC, N])
        r1.close()
        wo1 = adaw

        rm = region()
        mm = lambda name, shape, dt=f32: rm.enter_context(nc.sbuf_tensor(name, shape, dt))
        wgu = mm("wgu", [P, 2, 2, KC, DE])
        wd = mm("wd", [P, 2, 2, D])
        fT = mm("fT", [P, KC, N])
        acc = mm("acc", [P, TT, D])
        xg = mm("xg", [P, 2, D])
        xT = mm("xT", [P, 2, KC, P])
        sg = mm("sg", [P, 2, DE])
        hh = mm("hh", [P, 2, DE])
        hT = mm("hT", [P, 2, 2, P])
        yo = mm("yo", [P, 2, D])
        score = mm("score", [P, TT, EXPERTS])
        sel = mm("sel", [P, TT, EXPERTS])
        g8 = mm("g8", [P, TT, GROUPS, 8])
        gsum = mm("gsum", [P, TT, GROUPS])
        top8 = mm("top8", [P, TT, 8])
        idx8 = mm("idx8", [P, TT, 8], u32)
        idxf = mm("idxf", [P, TT, 8])
        geq = mm("geq", [P, TT, GROUPS, TOPG])
        gmask = mm("gmask", [P, TT, GROUPS])
        wts = mm("wts", [P, TT, TOPK])
        wsum = mm("wsum", [P, TT])
        mask = mm("mask", [P, TT, EXPERTS])
        rbias = mm("rbias", [P, EXPERTS])
        rw = mm("rw", [P, KC, EXPERTS])
        nblk = mm("nblk", [P, EXPERTS])
        pend = mm("pend", [P, EXPERTS])
        bst = mm("bst", [P, EXPERTS])
        code = mm("code", [P, TT * TOPK])
        codei = mm("codei", [P, 2, TT * TOPK], i32)
        slotf = mm("slotf", [P, TT * TOPK])
        blkf = mm("blkf", [P, TT * TOPK])
        junk_e = mm("junk_e", [P, EXPERTS])
        becol = mm("becol", [P, 1])
        vtab = mm("vtab", [P, COLS], i32)
        ttab = mm("ttab", [P, COLS], i32)
        etab = mm("etab", [1, COLS], i32)
        npair = mm("npair", [1, 2], i32)
        xid = mm("xid", [P, 2], u32)
        yid = mm("yid", [P, 2], u32)
        rm.close()
        rr = region()
        mr = lambda name, shape, dt=f32: rr.enter_context(nc.sbuf_tensor(name, shape, dt))
        eq = mr("eq", [P, TT, TOPK, EXPERTS])
        eqw = mr("eqw", [P, TT, TOPK, EXPERTS])
        hot_s = mr("hot_s", [P, 4, P])
        hot_b = mr("hot_b", [P, 4, COLS])
        rr.close()
        ry = region()
        yl = ry.enter_context(nc.sbuf_tensor("yl", [P, 2, TOPK, D], f32))
        ry.close()

        pp = [stack.enter_context(nc.psum_tensor(f"pp{i}", [P, 2 * HB], f32)) for i in range(4)]
        bank = lambda i: pp[i // 2][:, (i % 2) * HB:(i % 2 + 1) * HB]

        c_in = sem("c_in"); x_in = sem("x_in"); hc_in = sem("hc_in"); const_in = sem("const_in"); rows_in = sem("rows_in")
        q_const = sem("q_const"); pool_set = sem("pool_set")
        ada_in = both("ada_in"); ada_ps = sem("ada_ps"); ada_row = sem("ada_row")
        ada_gain = sem("ada_gain"); ada_out_ps = sem("ada_out_ps"); ada_col = sem("ada_col"); ada_out = sem("ada_out"); nrow_in = sem("nrow_in")
        csil_ok = sem("csil_ok")
        sq_done = sem("sq_done"); var_done = sem("var_done"); std_done = sem("std_done"); rn_done = sem("rn_done")
        t_ps = sem("t_ps"); t_out = sem("t_out")
        cw_ps = sem("cw_ps"); cw_out = sem("cw_out")
        wlat_in = sem("wlat_in"); wlat_swap = sem("wlat_swap"); wab_in = both("wab_in"); wab_used = sem("wab_used")
        wu_in = sem("wu_in"); wu_swap = sem("wu_swap"); wo_in = sem("wo_in")
        lat_ps = sem("lat_ps"); lat_out = sem("lat_out"); lat_sq = sem("lat_sq"); lat_var = sem("lat_var"); lat_std = sem("lat_std")
        lat_n = sem("lat_n"); latT_ps = sem("latT_ps"); latT_out = sem("latT_out")
        kr_ps = sem("kr_ps"); kr_out = sem("kr_out"); krc_out = sem("krc_out")
        u_ps = sem("u_ps"); sg_out = sem("sg_out"); v_out = sem("v_out")
        cv_done = sem("cv_done"); mean_ps = sem("mean_ps"); d_done = sem("d_done"); dsq = sem("dsq"); varc_ps = sem("varc_ps")
        cvar = sem("cvar"); cstd = sem("cstd"); dn = sem("dn"); ca_out = sem("ca_out")
        v_ps = sem("v_ps"); vv_out = sem("vv_out")
        kn_ps = sem("kn_ps"); kn_out = sem("kn_out"); kr_copy = sem("kr_copy")
        q_ps = sem("q_ps"); qn_out = sem("qn_out"); qr_out = sem("qr_out")
        s_ps = sem("s_ps"); mx = sem("mx"); ex = sem("ex"); pt_ps = sem("pt_ps"); pt_out = sem("pt_out"); pv_ps = sem("pv_ps")
        o_out = sem("o_out"); oT_ps = sem("oT_ps"); oT_out = sem("oT_out")
        y_ps = sem("y_ps"); y_g = sem("y_g"); h_new = sem("h_new")
        w3_in = [sem(f"w3_in{i}") for i in range(3)]
        u3_ps = sem("u3_ps"); cg_out = sem("cg_out"); z_out = sem("z_out"); o1_out = sem("o1_out")
        PER = {"f_done": TT, "f_stored": 16 * TT, "fT_ps": KC, "fT_out": KC, "lg_ps": 1, "sc_out": 1, "rt": 1,
               "rk_in": 1, "rk_ps": 1, "hot": 2 * TT * TOPK, "hot_used": TT * TOPK, "tables": 4, "be_ps": 1, "rconst_in": 32,
               "sh_in": 48, "x_clear": 1, "y_clear": 1, "comb": TT * TOPK, "hfin": TT, "yl_in0": 16 * TT // 2, "yl_in1": 16 * TT // 2}
        L = {name: [sem(name)] * DEPTH for name in PER}
        at = lambda l, name, n: PER[name] * l + n
        for name in ("Wg_in Wd_in x_in xo yp ye yw").split():
            for b in range(2):
                L[f"{name}{b}"] = layers(f"{name}{b}")
        for name in "xp0 x_id x_used gu s hm hp ho y_id".split():
            L[name] = layers(name)
        L["fence"] = [sem("fence")] * DEPTH
        fin_o = sem("fin_o"); stored = sem("stored"); fw_in = sem("fw_in")

        block = stack.enter_context(nc.Block())

        Y3 = [y.rearrange("(t p e) d -> p t e d", p=P, e=8) for y in Y_dram]
        F3 = [f.rearrange("(t p) d -> p t d", p=P) for f in F_dram]
        adaw_d = [a["ada_w"][l].rearrange("(p k) n -> p k n", k=KC) for l in range(DEPTH)]
        win_d = a["ev_w_in"][0].rearrange("(p k) n -> p k n", k=KC)
        w3_d = a["od_w_in"][0].rearrange("(p k) (j n) -> p k j n", k=KC, j=3)
        NSEC = 6
        LAST_ROW = (1, 4)

        @block.sync
        def _(sp):
            sp.dma_start(ccol[:, 0, :], c.rearrange("a (p k) -> (a p) k", k=KC)).then_inc(c_in, 16)
            sp.dma_start(ccol[:, 1, :], c_ctx.rearrange("(p k) -> p k", k=KC)).then_inc(c_in, 16)
            sp.dma_start(h[:, :, :], x[0].rearrange("(t p) d -> p t d", p=P)).then_inc(x_in, 16)
            sp.dma_start(hc[:, :, :], ctx_in[0].rearrange("(t p) d -> p t d", p=P)).then_inc(hc_in, 16)

            def load_ada(l):
                def load_norm(name, which):
                    if which + 2 * l:
                        sp.wait_ge(ada_gain, which + 2 * l)
                    sp.dma_start(nrow[:, :], a[name][l:l + 1, :].partition_broadcast(2).rearrange("p a d -> p (a d)")).then_inc(nrow_in, 16)

                load_norm("norm_mix_w", 0)
                for n in range(2 * NSEC):
                    m = 2 * NSEC * l + n
                    if m >= 2:
                        sp.wait_ge(ada_row, m - 1)
                    if n == 8:
                        load_norm("norm_ffn_w", 1)
                    if l and n == 0:
                        sp.wait_ge(h_new, 2 * TT)
                    sp.dma_start(adaw[:, m % 2, :, :], adaw_d[l][:, :, n * HB:(n + 1) * HB]).then_inc(ada_in[m % 2], 16)
                    sp.dma_start(adab[0:2, m % 2, :], a["ada_b"][l:l + 1, n * HB:(n + 1) * HB].partition_broadcast(2).rearrange("p a d -> p (a d)")).then_inc(ada_in[m % 2], 16)

            load_ada(0)
            sp.dma_start(wlat[:, :, 0:LAT], win_d[:, :, 2 * CONV:]).then_inc(wlat_in, 16)
            for ci in range(CC):
                if ci >= 2:
                    sp.wait_ge(wab_used, ci - 1)
                for j in range(2):
                    sp.dma_start(wab[:, ci % 2, :, j, :], win_d[:, :, j * CONV + ci * P:j * CONV + (ci + 1) * P]).then_inc(wab_in[ci % 2], 16)
                if ci == 1:
                    sp.dma_start(wuq[:, :, :, 0:NOPE + ROPE], a["ev_w_uq"][0].rearrange("(p j) h d -> p j h d", j=2)).then_inc(wu_in, 16)
                    sp.dma_start(wukv[:, :, :], a["ev_w_ukv"][0]).then_inc(wu_in, 16)
            sp.wait_ge(ada_row, 2 * NSEC)
            wo0v = wo0.rearrange("p b k n -> p (b k n)").rearrange("p (c n) -> p c n", n=D)
            sp.dma_start(wo0v[:, 0:CC, :], a["ev_w_out"][0, 0:CONV, :].rearrange("(c p) n -> p c n", p=P)).then_inc(wo_in, 16)
            sp.dma_start(wo0v[:, CC:2 * CC, :], a["ev_w_out"][0, CONV:, :].rearrange("(p c) n -> p c n", c=CC)).then_inc(wo_in, 16)

            def load_short_conv():
                for ci in range(SCC):
                    if ci < 3:
                        if ci == 0:
                            sp.wait_ge(L["hfin"][0], TT)
                    else:
                        sp.wait_ge(u3_ps, 3 * (ci - 2))
                    for j in range(3):
                        sp.dma_start(w3[:, ci % 3, :, j, :], w3_d[:, :, j, ci * P:(ci + 1) * P]).then_inc(w3_in[ci % 3], 16)
                sp.wait_ge(ada_row, 4 * NSEC)
                wo1v = wo1.rearrange("p b k n -> p (b k n)").rearrange("p (c n) -> p c n", n=D)
                sp.dma_start(wo1v, a["od_w_out"][0].rearrange("(c p) n -> p c n", p=P)).then_inc(wo_in, 16)

            def experts(l):
                s = {k: v[l] for k, v in L.items()}
                sp.wait_ge(h_new, 2 * TT * (l + 1))
                sp.dma_start(rw[:, :, :], a["router_w"][l].rearrange("(p k) e -> p k e", k=KC)).then_inc(s["rconst_in"], 16)
                sp.dma_start(rbias[:, :], a["router_bias"][l:l + 1, :].partition_broadcast(P).rearrange("p a d -> p (a d)")).then_inc(s["rconst_in"], 16)
                for j, name in enumerate(("sh_w_gate", "sh_w_up")):
                    sp.dma_start(wgu[:, 1, j, :, :], a[name][l].rearrange("(p k) n -> p k n", k=KC)).then_inc(s["sh_in"], 16)
                sp.dma_start(wd[:, 1, :, :], a["sh_w_down"][l].rearrange("(p j) n -> p j n", j=2)).then_inc(s["sh_in"], 16)
                for t in range(TT):
                    sp.wait_ge(s["f_done"], at(l, "f_done", t + 1))
                    sp.dma_start(F3[l][:, t, :], acc[:, t, :]).then_inc(s["f_stored"], 16)
                sp.wait_ge(s["tables"], at(l, "tables", 4))
                pairs = sp.value_load(npair[0:1, 0:1], min_val=1, max_val=MAXP)

                def load(b, e):
                    for j, name in enumerate(("exp_w_gate", "exp_w_up")):
                        sp.dma_start(wgu[:, b, j:j + 1, :, :], a[name][l][bass.ds(e, 1), :, :].rearrange("a (p k) n -> p a k n", k=KC)).then_inc(s[f"Wg_in{b}"], 16)

                def load_down(b, e):
                    sp.dma_start(wd[:, b, :, :], a["exp_w_down"][l][bass.ds(e, 1), :, :].rearrange("a (p j) n -> p (a j) n", j=2)).then_inc(s[f"Wd_in{b}"], 16)

                for b in range(2):
                    e = sp.value_load(etab[0:1, b:b + 1], min_val=0, max_val=EXPERTS - 1)
                    if b == 1:
                        sp.wait_ge(s["gu"], TT)
                    load(b, e)
                    if b == 1:
                        sp.wait_ge(s["yp1"], TT)
                    load_down(b, e)
                with sp.Fori(1, pairs) as i:
                    for b in range(2):
                        e = sp.value_load(etab[0:1, bass.ds(2 * i + b, 1)], min_val=0, max_val=EXPERTS - 1)
                        sp.wait_ge(s["gu"], TT + 2 * i - 1 + b)
                        load(b, e)
                        sp.wait_ge(s["yp1"], TT + 2 * i - 1 + b)
                        load_down(b, e)
                for b in range(2):
                    sp.wait_ge(s[f"yw{b}"], 16 * pairs + 16)
                    sp.sem_inc(s["fence"], 1)
                sp.wait_ge(s["yp1"], TT + 2 * pairs)
                sp.sem_inc(s["fence"], 1)
                for t in range(TT):
                    if t >= 2:
                        sp.wait_ge(s["comb"], at(l, "comb", TOPK * (t - 1)))
                    sp.dma_start(yl[:, t % 2, :, :], Y3[l][:, t, 0:TOPK, :]).then_inc(s[f"yl_in{t % 2}"], 16)

            experts(0)
            load_ada(1)
            load_short_conv()
            experts(1)
            sp.wait_ge(L["hfin"][1], 2 * TT)
            sp.dma_start(b2b[:, :], a["final_norm_w"].rearrange("(a n) -> a n", a=1).partition_broadcast(P).rearrange("p a d -> p (a d)")).then_inc(fw_in, 16)
            for t in range(TT):
                sp.wait_ge(fin_o, t + 1)
                sp.dma_start(out[0].rearrange("(t p) d -> p t d", p=P)[:, t, :], h[:, t, :]).then_inc(stored, 16)
            sp.wait_ge(stored, 16 * TT)

        @block.gpsimd
        def _(pool):
            for dst, name in ((ident, "k_ident"), (before, "k_before"), (rope, "k_rope")):
                pool.dma_start(dst[:, :], a[name]).then_inc(const_in, 16)
            pool.dma_start(first_row[:, :], a["k_first"]).then_inc(const_in, 16)
            pool.dma_start(crow[0:TAPS, :], a["ev_conv_w"][0].rearrange("t a n -> t (a n)")).then_inc(rows_in, 16)
            for j, name in enumerate(("ev_conv_b", "ev_ln_w", "ev_ln_b")):
                pool.dma_start(crow[TAPS + j:TAPS + j + 1, :], a[name]).then_inc(rows_in, 16)
            pool.dma_start(orow[:, :], a["od_conv_w"][0].rearrange("t a n -> t (a n)")).then_inc(rows_in, 16)
            pool.dma_start(qnw[:, :], a["ev_q_norm_w"].rearrange("a (p j) -> p (a j)", j=2)).then_inc(q_const, 16)
            pool.dma_start(kvw[:, :], a["ev_kv_norm_w"].rearrange("a p -> p a")).then_inc(q_const, 16)
            nc.gpsimd.memset(ones[:, :], 1.0).then_inc(pool_set, 1)
            nc.gpsimd.memset(one_over[:, :], 1.0 / CONV).then_inc(pool_set, 1)
            nc.gpsimd.iota(iota_row[:, :], pattern=[[1, P]], base=0, channel_multiplier=0, allow_small_or_imprecise_dtypes=True).then_inc(pool_set, 1)
            nc.gpsimd.iota(iota_part[:, :], pattern=[[0, 1]], base=0, channel_multiplier=1, allow_small_or_imprecise_dtypes=True).then_inc(pool_set, 1)
            nc.gpsimd.iota(pair_val[:, :, :], pattern=[[8 * P, TT], [1, 8]], base=-EMPTY, channel_multiplier=8, allow_small_or_imprecise_dtypes=True).then_inc(pool_set, 1)
            pool.wait_ge(wlat_in, 16)
            q8 = ROPE // 4
            for ax in range(2):
                for half in range(2):
                    d0, s0 = LAT + (2 * ax + half) * q8, QL + KVL + (2 * ax + 1 - half) * q8
                    nc.gpsimd.tensor_copy(wlat[:, :, d0:d0 + q8], wlat[:, :, s0:s0 + q8]).then_inc(wlat_swap, 1)
            pool.wait_ge(wu_in, 32)
            wuqv = wuq.rearrange("p j h d -> p (j h) d")
            for ax in range(2):
                for half in range(2):
                    d0, s0 = NOPE + ROPE + (2 * ax + half) * q8, NOPE + (2 * ax + 1 - half) * q8
                    nc.gpsimd.tensor_copy(wuqv[:, :, d0:d0 + q8], wuqv[:, :, s0:s0 + q8]).then_inc(wu_swap, 1)
            pool.wait_ge(t_ps, 2 * KC)
            nc.gpsimd.memset(vpad[:, :, :], 0.0).then_inc(pool_set, 1)
            pool.wait_ge(kr_out, 1)
            pool.wait_ge(krc_out, 1)
            pool.wait_ge(wu_swap, 4)
            pool.wait_ge(pool_set, 6)
            for b in range(2):
                if b:
                    pool.wait_ge(kr_copy, b)
                nc.gpsimd.tensor_copy(kT[NOPE:NOPE + ROPE, b, :], krT[NOPE:NOPE + ROPE, :]).then_inc(kr_copy, 1)

            def experts(l):
                s = {k: v[l] for k, v in L.items()}
                pool.wait_ge(h_new, 2 * TT * (l + 1))
                pool.wait_ge(kr_copy, 2)
                nc.gpsimd.memset(yo[:, :, :], 0.0).then_inc(s["y_clear"], 1)
                nc.gpsimd.memset(xg[:, :, :], 0.0).then_inc(s["x_clear"], 1)
                pool.wait_ge(s["tables"], at(l, "tables", 4))
                pool.wait_ge(s["f_stored"], at(l, "f_stored", 16 * TT))
                pool.wait_ge(s["x_clear"], at(l, "x_clear", 1))
                pool.wait_ge(s["y_clear"], at(l, "y_clear", 1))
                pairs = pool.value_load(npair[0:1, 0:1], min_val=1, max_val=MAXP)

                def gather(b):
                    nc.gpsimd.indirect_dma_start(
                        xg[:, b, :], None, F_dram[l][:, :], bass.IndirectOffsetOnAxis(ap=xid[:, b:b + 1], axis=0),
                        bounds_check=N - 1, oob_is_err=False).then_inc(s[f"x_in{b}"], 16)

                for b in range(2):
                    nc.gpsimd.tensor_copy(xid[:, b:b + 1], ttab[:, b:b + 1]).then_inc(s["x_id"], 1)
                for b in range(2):
                    pool.wait_ge(s["x_id"], b + 1)
                    gather(b)

                def scatter(b):
                    nc.gpsimd.indirect_dma_start(
                        Y_dram[l][:, :], bass.IndirectOffsetOnAxis(ap=yid[:, b:b + 1], axis=0), yo[:, b, :], None,
                        bounds_check=N * 8 - 1, oob_is_err=False).then_inc(s[f"yw{b}"], 16)

                for b in range(2):
                    nc.gpsimd.tensor_copy(yid[:, b:b + 1], vtab[:, COLS - 1:COLS]).then_inc(s["y_id"], 1)
                for b in range(2):
                    pool.wait_ge(s["y_id"], b + 1)
                    scatter(b)
                with pool.Fori(0, pairs) as i:
                    for b in range(2):
                        pool.wait_ge(s["x_used"], 2 * i + b + 1)
                        pool.sem_inc(s["fence"], 1)
                        nc.gpsimd.tensor_copy(xid[:, b:b + 1], ttab[:, bass.ds(2 * i + 2 + b, 1)]).then_inc(s["x_id"], 1)
                        pool.wait_ge(s["x_id"], 2 * i + b + 3)
                        pool.sem_inc(s["fence"], 1)
                        gather(b)
                    for b in range(2):
                        pool.wait_ge(s[f"yw{b}"], 16 * i + 16)
                        pool.sem_inc(s["fence"], 1)
                        nc.gpsimd.tensor_copy(yid[:, b:b + 1], vtab[:, bass.ds(2 * i + b, 1)]).then_inc(s["y_id"], 1)
                        pool.wait_ge(s["y_id"], 2 * i + b + 3)
                        pool.sem_inc(s["fence"], 1)
                        pool.wait_ge(s["ye0"], TT + 2 * i + b + 1)
                        pool.sem_inc(s["fence"], 1)
                        pool.wait_ge(s["ye1"], TT + 2 * i + b + 1)
                        pool.sem_inc(s["fence"], 1)
                        scatter(b)
                for b in range(2):
                    pool.wait_ge(s[f"x_in{b}"], 16 * (pairs + 1))
                    pool.sem_inc(s["fence"], 1)

            experts(0)
            experts(1)

        @block.tensor
        def _(pe):
            mmul = nc.tensor.matmul

            def ada(l):
                for sct in range(NSEC):
                    for half in range(2):
                        m = 2 * NSEC * l + 2 * sct + half
                        pe.wait_ge(ada_in[m % 2], 32 * (m // 2 + 1))
                        if m >= 2:
                            pe.wait_ge(ada_row, m - 1)
                        for k in range(KC):
                            ins = mmul(bank(m % 2)[0:2, :], csil[:, :, k], adaw[:, m % 2, k, :], start=(k == 0), stop=(k == KC - 1))
                        ins.then_inc(ada_ps, 1)
                    m = NSEC * l + sct
                    g = 2 * l + sum(q <= sct for q in LAST_ROW)
                    pe.wait_ge(ada_gain, g) if sct in LAST_ROW else pe.wait_ge(ada_row, 2 * (m + 1))
                    if sct < 2:
                        if l or sct:
                            pe.wait_ge(ada_col, 2 * l + sct)
                        for k in range(KC):
                            ins = mmul(bank(2)[:, 2 * k:2 * k + 2], mrow[:, m % 2, k:D:KC], ident[0:2, 0:2], start=True, stop=True)
                        ins.then_inc(ada_out_ps, 1)
                    else:
                        for half in range(2):
                            n = 8 * l + 2 * (sct - 2) + half
                            if n >= 2:
                                pe.wait_ge(ada_out, n - 1)
                            ins = mmul(bank(4 + half), first_row[:, :], mrow[:, m % 2, half * HB:(half + 1) * HB], start=True, stop=True)
                            ins.then_inc(ada_out_ps, 1)

            pe.wait_ge(const_in, 64)
            pe.wait_ge(rows_in, 80)
            for ci in range(CC):
                ins = nc.tensor.transpose(bank(6)[:, ci * 40:ci * 40 + TAPS + 3], crow[:, ci * P:(ci + 1) * P], ident[0:TAPS + 3, 0:TAPS + 3])
            for ci in range(SCC):
                ins = nc.tensor.transpose(bank(6)[:, 256 + ci * 4:256 + ci * 4 + 3], orow[:, ci * P:(ci + 1) * P], ident[0:3, 0:3])
            ins.then_inc(cw_ps, 1)
            pe.wait_ge(csil_ok, 1)
            ada(0)

            for k in range(KC):
                for part in range(2):
                    n = 2 * k + part
                    if n == 0:
                        pe.wait_ge(rn_done, TT + TC)
                    if n >= 2:
                        pe.wait_ge(t_out, n - 1)
                    for t in range(TT if part == 0 else TC):
                        ins = nc.tensor.transpose(bank(n % 2)[:, t * P:(t + 1) * P], rn[:, t + (TT if part else 0), k:D:KC], ident[:, :])
                    ins.then_inc(t_ps, 1)

            pe.wait_ge(t_out, 2 * KC)
            pe.wait_ge(wlat_in, 16)
            for t in range(TT + TC):
                if t >= 2:
                    pe.wait_ge(lat_out, t - 1)
                w = QL + KVL if t < TT else KVL
                key0 = NCTX + t * P if t < TT else (t - TT) * P
                for k in range(KC):
                    ins = mmul(bank(2 + t % 2)[:, 0:w], aT[:, k, key0:key0 + P], wlat[:, k, QL + KVL - w:QL + KVL], start=(k == 0), stop=(k == KC - 1))
                ins.then_inc(lat_ps, 1)
            pe.wait_ge(wlat_swap, 4)
            for j, (k0, kn) in enumerate(((NCTX, N), (0, NCTX))):
                for k in range(KC):
                    ins = mmul(bank(4 + j)[:, 0:kn], wlat[:, k, LAT - ROPE - NOPE:LAT + ROPE], aT[:, k, k0:k0 + kn], start=(k == 0), stop=(k == KC - 1))
                ins.then_inc(kr_ps, 1)
            pe.wait_ge(cw_out, 2)
            for ci in range(CC):
                pe.wait_ge(wab_in[ci % 2], 32 * (ci // 2 + 1))
                if ci >= 1:
                    pe.wait_ge(v_out, ci)
                for j in range(2):
                    for k in range(KC):
                        ins = mmul(bank(6 + j), wab[:, ci % 2, k, j, :], aT[:, k, NCTX:], start=(k == 0), stop=(k == KC - 1))
                    ins.then_inc(u_ps if j == 0 else wab_used, 1)
            pe.wait_ge(lat_n, 2 * TT + TC)
            for j in range(2):
                for t in range(TT):
                    ins = nc.tensor.transpose(bank(j)[:, t * P:(t + 1) * P], cqs[:, t, j:QL:2], ident[:, :])
                ins.then_inc(latT_ps, 1)
            pe.wait_ge(lat_out, TT + TC)
            for t in range(TC):
                ins = nc.tensor.transpose(bank(2)[:, t * P:(t + 1) * P], cqs[:, TT + t, QL:], ident[:, :])
            ins.then_inc(latT_ps, 1)
            for t in range(TT):
                ins = nc.tensor.transpose(bank(3)[:, t * P:(t + 1) * P], cqs[:, t, QL:], ident[:, :])
            ins.then_inc(latT_ps, 1)
            pe.wait_ge(wu_in, 32)
            pe.wait_ge(latT_out, 4)
            pe.wait_ge(kr_out, 1)
            pe.wait_ge(krc_out, 1)
            for t in range(TT + TC):
                if t >= 2:
                    pe.wait_ge(vv_out, t - 1)
                mmul(bank(4 + t % 2), ckvT[:, t * P:(t + 1) * P], wukv[:, :, NOPE:], start=True, stop=True).then_inc(v_ps, 1)
            pe.wait_ge(wu_swap, 4)
            pe.wait_ge(kr_copy, 2)
            pe.wait_ge(vv_out, TT + TC)
            pe.wait_ge(v_out, CC)
            S = [pp[0], pp[1]]
            for hd in range(HEADS):
                if hd >= 1:
                    pe.wait_ge(pt_out, TT * hd)
                for n0, nn in ((0, HB), (HB, KEYS - HB)):
                    ins = mmul(pp[3][0:NOPE, n0:n0 + nn], wukv[:, hd, 0:NOPE], ckvT[:, n0:n0 + nn], start=True, stop=True)
                ins.then_inc(kn_ps, 1)
                for j in range(2):
                    ins = mmul(bank(5), wuq[:, j, hd, :], cqT[:, j, :], start=(j == 0), stop=(j == 1))
                ins.then_inc(q_ps, 1)
                pe.wait_ge(kn_out, hd + 1)
                pe.wait_ge(qn_out, hd + 1)
                pe.wait_ge(qr_out, hd + 1)

                def scores(t):
                    n = hd * TT + t
                    if n >= 2:
                        pe.wait_ge(ex, n - 1)
                    for n0, nn in ((0, HB), (HB, KEYS - HB)):
                        ins = mmul(S[n % 2][:, n0:n0 + nn], qT[0:NOPE + ROPE, hd % 2, t * P:(t + 1) * P], kT[0:NOPE + ROPE, hd % 2, n0:n0 + nn], start=True, stop=True)
                    ins.then_inc(s_ps, 1)

                scores(0)
                for t in range(TT):
                    n = hd * TT + t
                    if t + 1 < TT:
                        scores(t + 1)
                    pe.wait_ge(ex, n + 1)
                    if n >= 1:
                        pe.wait_ge(pt_out, n)
                    for j in range(KEYS // P):
                        ins = nc.tensor.transpose(pp[3][:, j * P:(j + 1) * P], pe_[:, n % 2, j * P:(j + 1) * P], ident[:, :])
                    ins.then_inc(pt_ps, 1)
                    pe.wait_ge(pt_out, n + 1)
                    if n >= 1:
                        pe.wait_ge(o_out, n)
                    for j in range(KEYS // P):
                        ins = mmul(bank(4)[:, 0:VH], pT[:, n % 2, j * P:(j + 1) * P], vv[:, j, hd * VH:(hd + 1) * VH], start=(j == 0), stop=(j == KEYS // P - 1))
                    ins.then_inc(pv_ps, 1)
            pe.wait_ge(cv_done, CC)
            pe.wait_ge(ex, TT * HEADS)
            for ci in range(CC):
                ins = mmul(bank(0), one_over[:, :], cy[:, ci, :], start=(ci == 0), stop=(ci == CC - 1))
            ins.then_inc(mean_ps, 1)
            pe.wait_ge(o_out, TT * HEADS)
            for ci in range(CC):
                if ci >= 2:
                    pe.wait_ge(oT_out, ci - 1)
                for t in range(TT):
                    ins = nc.tensor.transpose(bank(2 + ci % 2)[:, t * P:(t + 1) * P], oo[:, t, ci:HEADS * VH:CC], ident[:, :])
                ins.then_inc(oT_ps, 1)
            for ci in range(CC):
                pe.wait_ge(dsq, ci + 1)
                ins = mmul(bank(1), one_over[:, :], csg[:, ci % 2, :], start=(ci == 0), stop=(ci == CC - 1))
                ins.then_inc(varc_ps, 1)

            def mix_out(l, left, n_chunks, wv, base):
                for n in range(2 * TT):
                    t, half = n // 2, n % 2
                    if n >= 2:
                        pe.wait_ge(y_g, 2 * TT * l + n - 1)
                    for k in range(n_chunks):
                        ins = mmul(bank(base + n % 2), left(k, t), wv[:, k, half * HB:(half + 1) * HB], start=(k == 0), stop=(k == n_chunks - 1))
                    ins.then_inc(y_ps, 1)

            pe.wait_ge(wo_in, 32)
            pe.wait_ge(ca_out, CC)
            pe.wait_ge(oT_out, CC)
            wo0v = wo0.rearrange("p b k n -> p (b k n)").rearrange("p (c n) -> p c n", n=D)
            mix_out(0, lambda k, t: catT[:, k // CC, k % CC, t * P:(t + 1) * P], 2 * CC, wo0v, 4)

            def experts(l):
                s = {k: v[l] for k, v in L.items()}
                pe.wait_ge(s["f_done"], at(l, "f_done", TT))
                for k in range(KC):
                    if k >= 2:
                        pe.wait_ge(s["fT_out"], at(l, "fT_out", k - 1))
                    for t in range(TT):
                        ins = nc.tensor.transpose(bank(k % 2)[:, t * P:(t + 1) * P], acc[:, t, k:D:KC], ident[:, :])
                    ins.then_inc(s["fT_ps"], 1)
                pe.wait_ge(s["rconst_in"], at(l, "rconst_in", 32))
                pe.wait_ge(s["fT_out"], at(l, "fT_out", KC))
                for t in range(TT):
                    for k in range(KC):
                        ins = mmul(bank(0)[:, t * EXPERTS:(t + 1) * EXPERTS], fT[:, k, t * P:(t + 1) * P], rw[:, k, :], start=(k == 0), stop=(k == KC - 1))
                ins.then_inc(s["lg_ps"], 1)
                pe.wait_ge(s["rk_in"], at(l, "rk_in", 1))
                for t in range(TT):
                    for q in range(t + 1):
                        ins = mmul(bank(1)[:, t * EXPERTS:(t + 1) * EXPERTS], before[:, :] if q == t else ones[:, :], mask[:, q, :], start=(q == 0), stop=(q == t))
                for q in range(TT):
                    ins = mmul(bank(2)[:, 0:EXPERTS], ones[:, :], mask[:, q, :], start=(q == 0), stop=(q == TT - 1))
                ins.then_inc(s["rk_ps"], 1)
                pe.wait_ge(s["rt"], at(l, "rt", 1))
                mmul(bank(2)[0:1, 128:128 + COLS], becol[0:COLS, :], ident[0:COLS, 0:COLS], start=True, stop=True).then_inc(s["be_ps"], 1)
                for n in range(TT * TOPK):
                    pe.wait_ge(s["hot"], at(l, "hot", 2 * (n + 1)))
                    mmul(bank(0)[:, 0:COLS], hot_s[:, n % 4, :], hot_b[:, n % 4, :], start=(n == 0), stop=(n == TT * TOPK - 1)).then_inc(s["hot_used"], 1)

                def gate_up(b, left, ready):
                    for k in range(KC):
                        ins = mmul(bank(2 + b), left(k), wgu[:, ready, :, k, :], start=(k == 0), stop=(k == KC - 1))
                    ins.then_inc(s["gu"], 1)

                def hidden_T(b):
                    for j in range(2):
                        ins = nc.tensor.transpose(bank(4 + b)[:, j * P:(j + 1) * P], hh[:, b, j:DE:2], ident[:, :])
                    ins.then_inc(s["hp"], 1)

                def down(b, w):
                    for half in range(2):
                        for j in range(2):
                            ins = mmul(bank(6 + half), hT[:, b, j, :], wd[:, w, j, half * HB:(half + 1) * HB], start=(j == 0), stop=(j == 1))
                        ins.then_inc(s[f"yp{half}"], 1)

                pe.wait_ge(s["sh_in"], at(l, "sh_in", 48))
                pe.wait_ge(s["tables"], at(l, "tables", 4))
                for pr in range(TT // 2):
                    for b in range(2):
                        t = 2 * pr + b
                        gate_up(b, lambda k, t=t: fT[:, k, t * P:(t + 1) * P], 1)
                    for b in range(2):
                        t = 2 * pr + b
                        pe.wait_ge(s["hm"], t + 1)
                        hidden_T(b)
                        pe.wait_ge(s["ho"], t + 1)
                        if t:
                            pe.wait_ge(s["ye0"], t)
                            pe.wait_ge(s["ye1"], t)
                        down(b, 1)
                pairs = pe.value_load(npair[0:1, 0:1], min_val=1, max_val=MAXP)
                with pe.Fori(0, pairs) as i:
                    for b in range(2):
                        pe.wait_ge(s[f"x_in{b}"], 16 * i + 16)
                        for g in range(2):
                            for k in range(KC // 2):
                                kk = g * KC // 2 + k
                                ins = nc.tensor.transpose(bank(g)[:, k * P:(k + 1) * P], xg[:, b, kk:D:KC], ident[:, :])
                            ins.then_inc(s["xp0"] if g == 0 else s["x_used"], 1)
                        pe.wait_ge(s["xo0"], 2 * i + b + 1)
                        pe.wait_ge(s["xo1"], 2 * i + b + 1)
                        pe.wait_ge(s[f"Wg_in{b}"], 32 * i + 32)
                        gate_up(b, lambda k, b=b: xT[:, b, k, :], b)
                    for b in range(2):
                        pe.wait_ge(s["hm"], TT + 2 * i + b + 1)
                        hidden_T(b)
                        pe.wait_ge(s["ho"], TT + 2 * i + b + 1)
                        pe.wait_ge(s[f"Wd_in{b}"], 16 * i + 16)
                        pe.wait_ge(s["ye0"], TT + 2 * i + b)
                        pe.wait_ge(s["ye1"], TT + 2 * i + b)
                        down(b, b)

            experts(0)
            ada(1)
            for k in range(KC):
                if k == 0:
                    pe.wait_ge(rn_done, TT + TC + TT)
                if k >= 2:
                    pe.wait_ge(t_out, 2 * KC + k - 1)
                for t in range(TT):
                    ins = nc.tensor.transpose(bank(k % 2)[:, t * P:(t + 1) * P], rn1[:, t, k:D:KC], ident[:, :])
                ins.then_inc(t_ps, 1)
            pe.wait_ge(t_out, 3 * KC)
            for ci in range(SCC):
                pe.wait_ge(w3_in[ci % 3], 48 * (ci // 3 + 1))
                if ci >= 2:
                    pe.wait_ge(o1_out, ci - 1)
                for j in (1, 2, 0):
                    for k in range(KC):
                        ins = mmul(bank(2 + 3 * (ci % 2) + j), w3[:, ci % 3, k, j, :], aT1[:, k, :], start=(k == 0), stop=(k == KC - 1))
                    ins.then_inc(u3_ps, 1)
            pe.wait_ge(wo_in, 48)
            pe.wait_ge(o1_out, SCC)
            wo1v = wo1.rearrange("p b k n -> p (b k n)").rearrange("p (c n) -> p c n", n=D)
            mix_out(1, lambda k, t: oT1[:, k, t * P:(t + 1) * P], SCC, wo1v, 0)
            experts(1)

        @block.scalar
        def _(act):
            act.wait_ge(c_in, 32)
            nc.scalar.activation(csil[:, :, :], ccol[:, :, :], ACT.Silu).then_inc(csil_ok, 1)

            def squares(src, n0, cols):
                for n, (row, junk) in enumerate(src):
                    nc.scalar.activation(junk, row, ACT.Square, accum_out=ssq[:, n0 + n:n0 + n + 1]).then_inc(sq_done, 1)

            def ada(l):
                for n in range(8):
                    dst = (g1b, b2b, a2b, g2b)[n // 2]
                    act.wait_ge(ada_out_ps, 10 * l + 2 + n + 1)
                    nc.scalar.activation(dst[:, (n % 2) * HB:(n % 2 + 1) * HB], bank(4 + n % 2), ACT.Copy).then_inc(ada_out, 1)

            act.wait_ge(x_in, 16)
            act.wait_ge(hc_in, 16)
            squares([(h[:, t, :], rn[:, t, :]) for t in range(TT)] + [(hc[:, t, :], rn[:, TT + t, :]) for t in range(TC)], 0, D)
            act.wait_ge(var_done, 1)
            nc.scalar.activation(rstd[:, 0:TT + TC], rstd[:, 0:TT + TC], ACT.Sqrt).then_inc(std_done, 1)
            ada(0)

            def modulate_T(k0, ks, parts, dst, n0):
                for k in range(ks):
                    for part in range(parts):
                        n = n0 + parts * k + part
                        act.wait_ge(t_ps, n + 1)
                        if n == n0:
                            act.wait_ge(ada_col, 2 * (n0 > 0) + 2)
                        o = dst[:, k, NCTX:] if parts == 2 and part == 0 else (dst[:, k, 0:NCTX] if part else dst[:, k, :])
                        nc.scalar.activation(o, bank(n % 2)[:, 0:(NCTX if part else N)], ACT.Identity,
                                             scale=acol[:, 1, k, part:part + 1], bias=acol[:, 0, k, part:part + 1]).then_inc(t_out, 1)

            modulate_T(0, KC, 2, aT, 0)
            for t in range(TT + TC):
                act.wait_ge(lat_ps, t + 1)
                w = QL + KVL if t < TT else KVL
                nc.scalar.activation(cqs[:, t, QL + KVL - w:], bank(2 + t % 2)[:, 0:w], ACT.Copy).then_inc(lat_out, 1)
            act.wait_ge(lat_out, TT + TC)
            cyf = cy.rearrange("p c n -> p (c n)")
            for t in range(TT + TC):
                nc.scalar.activation(cyf[:, t * KVL:(t + 1) * KVL], cqs[:, t, QL:], ACT.Square, accum_out=ssq[:, 8 + TT + t:9 + TT + t]).then_inc(lat_sq, 1)
                if t < TT:
                    nc.scalar.activation(cyf[:, 768 + t * QL:768 + (t + 1) * QL], cqs[:, t, 0:QL], ACT.Square, accum_out=ssq[:, 8 + t:9 + t]).then_inc(lat_sq, 1)
            act.wait_ge(kr_ps, 2)
            nc.scalar.activation(krT[NOPE:NOPE + ROPE, 0:NCTX], bank(5)[NOPE:NOPE + ROPE, 0:NCTX], ACT.Copy).then_inc(krc_out, 1)
            act.wait_ge(lat_var, 1)
            nc.scalar.activation(rstd[:, 8:8 + 2 * TT + TC], rstd[:, 8:8 + 2 * TT + TC], ACT.Sqrt).then_inc(lat_std, 1)
            for ci in range(CC):
                act.wait_ge(wab_used, ci + 1)
                if ci >= 2:
                    act.wait_ge(v_out, ci - 1)
                nc.scalar.activation(csg[:, ci % 2, :], bank(7), ACT.Sigmoid).then_inc(sg_out, 1)
            act.wait_ge(q_const, 32)
            for j in range(2):
                act.wait_ge(latT_ps, j + 1)
                nc.scalar.activation(cqT[:, j, :], bank(j), ACT.Copy, scale=qnw[:, j:j + 1]).then_inc(latT_out, 1)
            act.wait_ge(latT_ps, 4)
            nc.scalar.activation(ckvT[:, 0:NCTX], bank(2)[:, 0:NCTX], ACT.Copy, scale=kvw[:, 0:1]).then_inc(latT_out, 1)
            nc.scalar.activation(ckvT[:, NCTX:], bank(3), ACT.Copy, scale=kvw[:, 0:1]).then_inc(latT_out, 1)
            for t in range(TT + TC):
                act.wait_ge(v_ps, t + 1)
                nc.scalar.activation(vv[:, t, :], bank(4 + t % 2), ACT.Copy).then_inc(vv_out, 1)
            for hd in range(HEADS):
                act.wait_ge(kn_ps, hd + 1)
                nc.scalar.activation(kT[0:NOPE, hd % 2, :], pp[3][0:NOPE, 0:KEYS], ACT.Copy).then_inc(kn_out, 1)
                act.wait_ge(q_ps, hd + 1)
                nc.scalar.activation(qT[0:NOPE, hd % 2, :], bank(5)[0:NOPE, :], ACT.Copy, scale=ATT_SCALE).then_inc(qn_out, 1)
                for t in range(TT):
                    n = hd * TT + t
                    act.wait_ge(mx, n + 1)
                    if n >= 2:
                        act.wait_ge(pt_ps, n - 1)
                    nc.scalar.activation(pe_[:, n % 2, :], pp[n % 2][:, 0:KEYS], ACT.Exp, bias=stat[:, n % 4, 0:1],
                                         accum_out=stat[:, n % 4, 1:2]).then_inc(ex, 1)
                    act.wait_ge(pt_ps, n + 1)
                    if n >= 2:
                        act.wait_ge(pv_ps, n - 1)
                    nc.scalar.activation(pT[:, n % 2, :], pp[3][:, 0:KEYS], ACT.Copy).then_inc(pt_out, 1)
            for ci in range(CC):
                act.wait_ge(oT_ps, ci + 1)
                nc.scalar.activation(catT[:, 1, ci, :], bank(2 + ci % 2), ACT.Copy).then_inc(oT_out, 1)
            for ci in range(CC):
                act.wait_ge(d_done, ci + 1)
                if ci >= 2:
                    act.wait_ge(varc_ps, ci - 1)
                nc.scalar.activation(csg[:, ci % 2, :], cy[:, ci, :], ACT.Square).then_inc(dsq, 1)
            act.wait_ge(cvar, 2)
            nc.scalar.activation(csg[:, 0, :], csg[:, 0, :], ACT.Sqrt).then_inc(cstd, 1)
            for ci in range(CC):
                act.wait_ge(dn, ci + 1)
                nc.scalar.activation(catT[:, 0, ci, :], cy[:, ci, :], ACT.Silu, scale=cvw[:, ci, TAPS + 1:TAPS + 2],
                                     bias=cvw[:, ci, TAPS + 2:TAPS + 3]).then_inc(ca_out, 1)

            def experts(l):
                s = {k: v[l] for k, v in L.items()}
                for t in range(TT):
                    act.wait_ge(h_new, 2 * (TT * l + t + 1))
                    nc.scalar.activation(fT[:, 2 * t:2 * t + 2, :].rearrange("p k n -> p (k n)"), h[:, t, :], ACT.Square, accum_out=ssq[:, t:t + 1]).then_inc(sq_done, 1)
                act.wait_ge(var_done, 2 + 2 * l)
                nc.scalar.activation(rstd[:, 0:TT], rstd[:, 0:TT], ACT.Sqrt).then_inc(std_done, 1)
                for k in range(0, KC, 2):
                    act.wait_ge(s["fT_ps"], at(l, "fT_ps", k + 1))
                    nc.scalar.activation(fT[:, k, :], bank(0), ACT.Copy).then_inc(s["fT_out"], 1)
                    act.wait_ge(s["fT_ps"], at(l, "fT_ps", k + 2))
                    nc.scalar.activation(fT[:, k + 1, :], bank(1), ACT.Copy).then_inc(s["fT_out"], 1)
                act.wait_ge(s["lg_ps"], at(l, "lg_ps", 1))
                nc.scalar.activation(score.rearrange("p t e -> p (t e)"), bank(0)[:, 0:TT * EXPERTS], ACT.Sigmoid).then_inc(s["sc_out"], 1)

                for pr in range(TT // 2):
                    for b in range(2):
                        act.wait_ge(s["gu"], 2 * pr + b + 1)
                        nc.scalar.activation(sg[:, b, :], bank(2 + b)[:, 0:DE], ACT.Silu).then_inc(s["s"], 1)
                    for b in range(2):
                        t = 2 * pr + b
                        act.wait_ge(s["yp0"], t + 1)
                        if t == 0:
                            act.wait_ge(s["f_stored"], at(l, "f_stored", 16 * TT))
                        nc.scalar.activation(acc[:, t, 0:HB], bank(6), ACT.Copy).then_inc(s["ye0"], 1)
                pairs = act.value_load(npair[0:1, 0:1], min_val=1, max_val=MAXP)
                with act.Fori(0, pairs) as i:
                    for b in range(2):
                        act.wait_ge(s["xp0"], 2 * i + b + 1)
                        nc.scalar.activation(xT[:, b, 0:KC // 2, :].rearrange("p k n -> p (k n)"), bank(0), ACT.Copy).then_inc(s["xo0"], 1)
                        act.wait_ge(s["gu"], TT + 2 * i + b + 1)
                        nc.scalar.activation(sg[:, b, :], bank(2 + b)[:, 0:DE], ACT.Silu).then_inc(s["s"], 1)
                    for b in range(2):
                        act.wait_ge(s[f"yw{b}"], 16 * i + 16)
                        act.wait_ge(s["yp0"], TT + 2 * i + b + 1)
                        nc.scalar.activation(yo[:, b, 0:HB], bank(6), ACT.Copy).then_inc(s["ye0"], 1)

            experts(0)
            for t in range(TT):
                act.wait_ge(L["hfin"][0], TT)
                nc.scalar.activation(rn1[:, t, :], h[:, t, :], ACT.Square, accum_out=ssq[:, t:t + 1]).then_inc(sq_done, 1)
            act.wait_ge(var_done, 3)
            nc.scalar.activation(rstd[:, 0:TT], rstd[:, 0:TT], ACT.Sqrt).then_inc(std_done, 1)
            ada(1)
            modulate_T(0, KC, 1, aT1, 2 * KC)
            for ci in range(SCC):
                act.wait_ge(u3_ps, 3 * ci + 1)
                if ci >= 2:
                    act.wait_ge(z_out, ci - 1)
                nc.scalar.activation(cgs[:, ci % 2, :], bank(2 + 3 * (ci % 2) + 1), ACT.Copy).then_inc(cg_out, 1)
            experts(1)
            for t in range(TT):
                act.wait_ge(L["hfin"][1], 2 * TT)
                nc.scalar.activation(acc[:, t, :], h[:, t, :], ACT.Square, accum_out=ssq[:, t:t + 1]).then_inc(sq_done, 1)
            act.wait_ge(var_done, 5)
            nc.scalar.activation(rstd[:, 0:TT], rstd[:, 0:TT], ACT.Sqrt).then_inc(std_done, 1)

        @block.vector
        def _(dve):
            chain, steps = sem("dve_step"), [0]

            def mark(ins):
                steps[0] += 1
                ins.then_inc(chain, 1)

            def link(ins):
                mark(ins)
                dve.wait_ge(chain, steps[0])

            V = nc.vector
            cum = (1, 2, 4, 6, 8, 10)

            def stats(n0, n1, width, squares, done):
                if squares:
                    dve.wait_ge(sq_done, squares)
                link(V.tensor_scalar(rstd[:, n0:n1], ssq[:, n0:n1], 1.0 / width, EPS, ALU.mult, ALU.add))
                V.reciprocal(rstd[:, n0:n1], rstd[:, n0:n1]).then_inc(done, 1)

            def ada(l):
                for sct in range(NSEC):
                    sg_ = NSEC * l + sct
                    if sg_ >= 2:
                        dve.wait_ge(ada_out_ps, 10 * l + cum[sct - 2] if sct >= 2 else 10 * (l - 1) + cum[sct + 4])
                    for half in range(2):
                        m = 2 * sg_ + half
                        dve.wait_ge(ada_ps, m + 1)
                        V.scalar_tensor_tensor(mrow[:, sg_ % 2, half * HB:(half + 1) * HB], bank(m % 2)[0:2, :], 1.0 if sct in LAST_ROW else 0.0,
                                               adab[0:2, m % 2, :], ALU.add, ALU.add).then_inc(ada_row, 1)
                    if sct in LAST_ROW:
                        dve.wait_ge(ada_row, 2 * sg_ + 2)
                        dve.wait_ge(nrow_in, 16 * (2 * l + LAST_ROW.index(sct) + 1))
                        V.tensor_tensor(mrow[:, sg_ % 2, :], mrow[:, sg_ % 2, :], nrow[:, :], ALU.mult).then_inc(ada_gain, 1)
                    if sct < 2:
                        dve.wait_ge(ada_out_ps, 10 * l + sct + 1)
                        V.tensor_copy(acol[:, sct, :, :], bank(2)[:, 0:2 * KC].rearrange("p (k j) -> p k j", j=2)).then_inc(ada_col, 1)

            stats(0, TT + TC, D, TT + TC, var_done)
            dve.wait_ge(std_done, 1)
            for t in range(TT + TC):
                V.tensor_scalar(rn[:, t, :], h[:, t, :] if t < TT else hc[:, t - TT, :], rstd[:, t:t + 1], None, ALU.mult).then_inc(rn_done, 1)
            dve.wait_ge(cw_ps, 1)
            V.tensor_copy(cvw[:, :, :], bank(6)[:, 0:CC * 40].rearrange("p (c n) -> p c n", n=40)[:, :, 0:TAPS + 3]).then_inc(cw_out, 1)
            V.tensor_copy(odw[:, :, :], bank(6)[:, 256:256 + SCC * 4].rearrange("p (c n) -> p c n", n=4)[:, :, 0:3]).then_inc(cw_out, 1)
            ada(0)

            dve.wait_ge(lat_sq, 2 * TT + TC)
            q0, k0 = 8, 8 + TT
            mark(V.tensor_scalar(rstd[:, q0:k0], ssq[:, q0:k0], 1.0 / QL, EPS, ALU.mult, ALU.add))
            link(V.tensor_scalar(rstd[:, k0:k0 + TT + TC], ssq[:, k0:k0 + TT + TC], 1.0 / KVL, EPS, ALU.mult, ALU.add))
            V.reciprocal(rstd[:, q0:k0 + TT + TC], rstd[:, q0:k0 + TT + TC]).then_inc(lat_var, 1)
            dve.wait_ge(lat_std, 1)
            for t in range(TT + TC):
                V.tensor_scalar(cqs[:, t, QL:], cqs[:, t, QL:], rstd[:, k0 + t:k0 + t + 1], None, ALU.mult).then_inc(lat_n, 1)
                if t < TT:
                    V.tensor_scalar(cqs[:, t, 0:QL], cqs[:, t, 0:QL], rstd[:, q0 + t:q0 + t + 1], None, ALU.mult).then_inc(lat_n, 1)
            dve.wait_ge(kr_ps, 2)
            R0, R1, R2 = NOPE, NOPE + ROPE, NOPE + 2 * ROPE
            mark(V.tensor_tensor(rt[R0:R1, 0, :], bank(4)[R0:R1, :], rope[R0:R1, :], ALU.mult))
            link(V.tensor_tensor(rt[R0:R1, 1, :], bank(4)[R1:R2, :], rope[R1:R2, :], ALU.mult))
            V.tensor_tensor(krT[R0:R1, NCTX:], rt[R0:R1, 0, :], rt[R0:R1, 1, :], ALU.add).then_inc(kr_out, 1)
            dve.wait_ge(pool_set, 6)
            for ci in range(CC):
                dve.wait_ge(sg_out, ci + 1)
                V.tensor_tensor(vpad[:, ci, PAD:PAD + N], bank(6), csg[:, ci % 2, :], ALU.mult).then_inc(v_out, 1)

            def conv_steps():
                for ci in range(CC):
                    dve.wait_ge(v_out, ci + 1)
                    link(V.tensor_scalar(cy[:, ci, :], vpad[:, ci, 0:N], cvw[:, ci, 0:1], cvw[:, ci, TAPS:TAPS + 1], ALU.mult, ALU.add))
                    yield
                    for tap in range(1, TAPS):
                        ins = V.scalar_tensor_tensor(cy[:, ci, :], vpad[:, ci, tap:tap + N], cvw[:, ci, tap:tap + 1], cy[:, ci, :], ALU.mult, ALU.add)
                        if tap < TAPS - 1:
                            link(ins)
                        else:
                            ins.then_inc(cv_done, 1)
                        yield

            conv = conv_steps()
            for hd in range(HEADS):
                dve.wait_ge(q_ps, hd + 1)
                mark(V.scalar_tensor_tensor(rt[R0:R1, 0, :], bank(5)[R0:R1, :], ATT_SCALE, rope[R0:R1, :], ALU.mult, ALU.mult))
                link(V.scalar_tensor_tensor(rt[R0:R1, 1, :], bank(5)[R1:R2, :], ATT_SCALE, rope[R1:R2, :], ALU.mult, ALU.mult))
                V.tensor_tensor(qT[R0:R1, hd % 2, :], rt[R0:R1, 0, :], rt[R0:R1, 1, :], ALU.add).then_inc(qr_out, 1)

                def head_max(t):
                    n = hd * TT + t
                    dve.wait_ge(s_ps, n + 1)
                    V.tensor_reduce(stat[:, n % 4, 0:1], pp[n % 2][:, 0:KEYS], AX.X, ALU.max, negate=True).then_inc(mx, 1)

                head_max(0)
                for t in range(TT):
                    n = hd * TT + t
                    if t + 1 < TT:
                        head_max(t + 1)
                    for _ in range(4):
                        next(conv, None)
                    dve.wait_ge(ex, n + 1)
                    link(V.reciprocal(stat[:, n % 4, 2:3], stat[:, n % 4, 1:2]))
                    dve.wait_ge(pv_ps, n + 1)
                    V.tensor_scalar(oo[:, t, hd * VH:(hd + 1) * VH], bank(4)[:, 0:VH], stat[:, n % 4, 2:3], None, ALU.mult).then_inc(o_out, 1)
            for _ in conv:
                pass
            dve.wait_ge(mean_ps, 1)
            dve.wait_ge(cv_done, CC)
            for ci in range(CC):
                V.tensor_tensor(cy[:, ci, :], cy[:, ci, :], bank(0), ALU.subtract).then_inc(d_done, 1)
            dve.wait_ge(varc_ps, CC)
            V.tensor_scalar(csg[:, 0, :], bank(1), EPS, None, ALU.add).then_inc(cvar, 1)
            dve.wait_ge(cvar, 1)
            V.reciprocal(csg[:, 0, :], csg[:, 0, :]).then_inc(cvar, 1)
            dve.wait_ge(cstd, 1)
            dve.wait_ge(d_done, CC)
            for ci in range(CC):
                V.tensor_tensor(cy[:, ci, :], cy[:, ci, :], csg[:, 0, :], ALU.mult).then_inc(dn, 1)

            def residual(l, tmp, base):
                dve.wait_ge(ada_out, 8 * l + 2)
                for n in range(2 * TT):
                    t, cols = n // 2, slice(n % 2 * HB, (n % 2 + 1) * HB)
                    dve.wait_ge(y_ps, 2 * TT * l + n + 1)
                    V.tensor_tensor(tmp[:, n % 2, :], bank(base + n % 2), g1b[:, cols], ALU.mult).then_inc(y_g, 1)
                    dve.wait_ge(y_g, 2 * TT * l + n + 1)
                    V.tensor_tensor(h[:, t, cols], h[:, t, cols], tmp[:, n % 2, :], ALU.add).then_inc(h_new, 1)

            residual(0, rt, 4)

            def bc(ap, shape):
                return ap.to_broadcast(shape)

            def experts(l):
                s = {k: v[l] for k, v in L.items()}
                stats(0, TT, D, TT + TC + TT + 2 * TT * l, var_done)
                dve.wait_ge(std_done, 2 + 2 * l)
                dve.wait_ge(ada_out, 8 * l + 8)
                dve.wait_ge(h_new, 2 * TT * (l + 1))
                for t in range(TT):
                    link(V.scalar_tensor_tensor(acc[:, t, :], h[:, t, :], rstd[:, t:t + 1], a2b[:, :], ALU.mult, ALU.mult))
                    V.tensor_tensor(acc[:, t, :], acc[:, t, :], b2b[:, :], ALU.add).then_inc(s["f_done"], 1)
                dve.wait_ge(s["rconst_in"], at(l, "rconst_in", 32))
                dve.wait_ge(s["sc_out"], at(l, "sc_out", 1))
                link(V.tensor_tensor(sel[:, :, :], score[:, :, :], bc(rbias[:, :].unsqueeze(1), [P, TT, EXPERTS]), ALU.add))
                for t in range(TT):
                    for g in range(GROUPS):
                        ins = V.max(out=g8[:, t, g, :], in_=sel[:, t, g * GE:(g + 1) * GE])
                link(ins)
                link(V.tensor_tensor(gsum[:, :, :], g8[:, :, :, 0], g8[:, :, :, 1], ALU.add))
                for t in range(TT):
                    ins = V.max(out=top8[:, t, :], in_=gsum[:, t, :])
                link(ins)
                for t in range(TT):
                    ins = V.max_index(out=idx8[:, t, :], in_max=top8[:, t, :], in_values=gsum[:, t, :])
                link(ins)
                link(V.tensor_copy(idxf[:, :, :], idx8[:, :, :]))
                link(V.tensor_tensor(geq[:, :, :, :], bc(iota_row[:, 0:GROUPS].unsqueeze(1).unsqueeze(3), [P, TT, GROUPS, TOPG]),
                                     bc(idxf[:, :, 0:TOPG].unsqueeze(2), [P, TT, GROUPS, TOPG]), ALU.is_equal))
                link(V.tensor_reduce(gmask[:, :, :], geq[:, :, :, :], AX.X, ALU.add))
                link(V.tensor_scalar(gmask[:, :, :], gmask[:, :, :], -1.0, 3.0e38, ALU.add, ALU.mult))
                sel4 = sel.rearrange("p t (g e) -> p (t g) e", e=GE)
                link(V.tensor_tensor(sel4, sel4, bc(gmask.rearrange("p t g -> p (t g)").unsqueeze(2), [P, TT * GROUPS, GE]), ALU.add))
                for t in range(TT):
                    ins = V.max(out=top8[:, t, :], in_=sel[:, t, :])
                link(ins)
                for t in range(TT):
                    ins = V.max_index(out=idx8[:, t, :], in_max=top8[:, t, :], in_values=sel[:, t, :])
                link(ins)
                link(V.tensor_copy(idxf[:, :, :], idx8[:, :, :]))
                full = [P, TT, TOPK, EXPERTS]
                for t in range(TT):
                    ins = V.tensor_tensor(eq[:, t, :, :], bc(iota_row[:, 0:EXPERTS].unsqueeze(1), full[:1] + full[2:]),
                                          bc(idxf[:, t, 0:TOPK].unsqueeze(2), full[:1] + full[2:]), ALU.is_equal)
                link(ins)
                for t in range(TT):
                    ins = V.tensor_reduce(mask[:, t, :], eq[:, t, :, :].rearrange("p k e -> p e k"), AX.X, ALU.add)
                ins.then_inc(s["rk_in"], 1)
                for t in range(TT):
                    ins = V.tensor_tensor(eqw[:, t, :, :], eq[:, t, :, :], bc(score[:, t, :].unsqueeze(1), full[:1] + full[2:]), ALU.mult)
                link(ins)
                link(V.tensor_reduce(wts[:, :, :], eqw[:, :, :, :], AX.X, ALU.add))
                link(V.tensor_reduce(wsum[:, :], wts[:, :, :], AX.X, ALU.add))
                link(V.reciprocal(wsum[:, :], wsum[:, :]))
                link(V.tensor_scalar(wsum[:, :], wsum[:, :], ROUTED_SCALE, None, ALU.mult))
                link(V.tensor_tensor(wts[:, :, :], wts[:, :, :], bc(wsum[:, :].unsqueeze(2), [P, TT, TOPK]), ALU.mult))
                dve.wait_ge(s["rk_ps"], at(l, "rk_ps", 1))
                cnt = bank(2)[:, 0:EXPERTS]
                link(V.tensor_copy(pend[:, :], cnt))
                link(V.tensor_scalar(nblk[:, :], pend[:, :], 0.0, None, ALU.is_gt))
                for q in range(1, TT):
                    link(V.scalar_tensor_tensor(nblk[:, :], pend[:, :], float(q * P), nblk[:, :], ALU.is_gt, ALU.add))
                link(V.tensor_tensor_scan(pend[:, :], ones[:, 0:EXPERTS], nblk[:, :], 0.0, ALU.mult, ALU.add))
                link(V.tensor_scalar(junk_e[:, :], pend[:, :], iota_part[:, 0:1], None, ALU.is_le, ALU.add, accum_out=becol[:, :]))
                V.tensor_tensor(bst[:, :], pend[:, :], nblk[:, :], ALU.subtract).then_inc(s["rt"], 1)
                dve.wait_ge(s["rt"], at(l, "rt", 1))
                link(V.tensor_scalar(bst[:, :], bst[:, :], float(P), None, ALU.mult))
                link(V.tensor_tensor(sel[:, :, :], bank(1)[:, 0:TT * EXPERTS].rearrange("p (t e) -> p t e", e=EXPERTS),
                                     bc(bst[:, :].unsqueeze(1), [P, TT, EXPERTS]), ALU.add))
                for t in range(TT):
                    ins = V.tensor_tensor(eqw[:, t, :, :], eq[:, t, :, :], bc(sel[:, t, :].unsqueeze(1), full[:1] + full[2:]), ALU.mult)
                link(ins)
                link(V.tensor_reduce(code[:, :].rearrange("p (t k) -> p t k", k=TOPK), eqw[:, :, :, :], AX.X, ALU.add))
                link(V.tensor_copy(codei[:, 0, :], code[:, :]))
                link(V.tensor_scalar(codei[:, 1, :], codei[:, 0, :], P - 1, None, ALU.bitwise_and))
                link(V.tensor_copy(slotf[:, :], codei[:, 1, :]))
                link(V.tensor_scalar(codei[:, 1, :], codei[:, 0, :], 7, None, ALU.logical_shift_right))
                link(V.tensor_copy(blkf[:, :], codei[:, 1, :]))
                for n in range(TT * TOPK):
                    if n >= 4:
                        dve.wait_ge(s["hot_used"], at(l, "hot_used", n - 3))
                    t, k = n // TOPK, n % TOPK
                    V.tensor_scalar(hot_s[:, n % 4, :], iota_row[:, :], slotf[:, n:n + 1], None, ALU.is_equal).then_inc(s["hot"], 1)
                    V.tensor_scalar(hot_b[:, n % 4, :], iota_row[:, 0:COLS], blkf[:, n:n + 1], pair_val[:, t, k:k + 1], ALU.is_equal, ALU.mult).then_inc(s["hot"], 1)
                dve.wait_ge(s["be_ps"], at(l, "be_ps", 1))
                V.tensor_scalar(etab[:, :], bank(2)[0:1, 128:128 + COLS], float(EXPERTS - 1), None, ALU.min).then_inc(s["tables"], 1)
                link(V.tensor_scalar(npair[:, 1:2], pend[0:1, EXPERTS - 1:EXPERTS], 1.0, None, ALU.add))
                V.tensor_scalar(npair[:, 0:1], npair[:, 1:2], 1, None, ALU.logical_shift_right).then_inc(s["tables"], 1)
                dve.wait_ge(s["hot_used"], at(l, "hot_used", TT * TOPK))
                V.tensor_scalar(vtab[:, :], bank(0)[:, 0:COLS], float(EMPTY), None, ALU.add).then_inc(s["tables"], 1)
                dve.wait_ge(s["tables"], at(l, "tables", 3))
                V.tensor_scalar(ttab[:, :], vtab[:, :], 3, None, ALU.logical_shift_right).then_inc(s["tables"], 1)

                def hidden(b, n):
                    dve.wait_ge(s["s"], n)
                    V.tensor_tensor(hh[:, b, :], bank(2 + b)[:, DE:2 * DE], sg[:, b, :], ALU.mult).then_inc(s["hm"], 1)

                def hidden_T(b, n):
                    dve.wait_ge(s["hp"], n)
                    V.tensor_copy(hT[:, b, :, :].rearrange("p j n -> p (j n)"), bank(4 + b)[:, 0:2 * P]).then_inc(s["ho"], 1)

                for pr in range(TT // 2):
                    for b in range(2):
                        hidden(b, 2 * pr + b + 1)
                    for b in range(2):
                        t = 2 * pr + b
                        hidden_T(b, t + 1)
                        dve.wait_ge(s["yp1"], t + 1)
                        if t == 0:
                            dve.wait_ge(s["f_stored"], at(l, "f_stored", 16 * TT))
                        V.tensor_copy(acc[:, t, HB:], bank(7)).then_inc(s["ye1"], 1)
                dve.wait_ge(s["tables"], at(l, "tables", 4))
                pairs = dve.value_load(npair[0:1, 0:1], min_val=1, max_val=MAXP)
                with dve.Fori(0, pairs) as i:
                    for b in range(2):
                        dve.wait_ge(s["x_used"], 2 * i + b + 1)
                        V.tensor_copy(xT[:, b, KC // 2:, :].rearrange("p k n -> p (k n)"), bank(1)).then_inc(s["xo1"], 1)
                        hidden(b, TT + 2 * i + b + 1)
                    for b in range(2):
                        hidden_T(b, TT + 2 * i + b + 1)
                        dve.wait_ge(s[f"yw{b}"], 16 * i + 16)
                        dve.wait_ge(s["yp1"], TT + 2 * i + b + 1)
                        V.tensor_copy(yo[:, b, HB:], bank(7)).then_inc(s["ye1"], 1)
                dve.wait_ge(s["ye0"], TT)
                for t in range(TT):
                    dve.wait_ge(s[f"yl_in{t % 2}"], at(l, f"yl_in{t % 2}", 16 * (t // 2 + 1)))
                    for k in range(TOPK):
                        V.scalar_tensor_tensor(acc[:, t, :], yl[:, t % 2, k, :], wts[:, t, k:k + 1], acc[:, t, :], ALU.mult, ALU.add).then_inc(s["comb"], 1)
                        dve.wait_ge(s["comb"], at(l, "comb", TOPK * t + k + 1))
                    link(V.tensor_tensor(acc[:, t, :], acc[:, t, :], g2b[:, :], ALU.mult))
                    V.tensor_tensor(h[:, t, :], h[:, t, :], acc[:, t, :], ALU.add).then_inc(s["hfin"], 1)

            experts(0)
            stats(0, TT, D, 3 * TT + TC, var_done)
            dve.wait_ge(std_done, 3)
            for t in range(TT):
                V.tensor_scalar(rn1[:, t, :], h[:, t, :], rstd[:, t:t + 1], None, ALU.mult).then_inc(rn_done, 1)
            ada(1)
            link(V.memset(zz[:, :, :], 0.0))
            for ci in range(SCC):
                b = ci % 2
                dve.wait_ge(cg_out, ci + 1)
                dve.wait_ge(u3_ps, 3 * ci + 2)
                V.tensor_tensor(zz[:, b, 1:N + 1], bank(2 + 3 * b + 2), cgs[:, b, :], ALU.mult).then_inc(z_out, 1)
                dve.wait_ge(z_out, ci + 1)
                link(V.tensor_scalar(zt[:, b, :], zz[:, b, 0:N], odw[:, ci, 0:1], None, ALU.mult))
                for tap in (1, 2):
                    link(V.scalar_tensor_tensor(zt[:, b, :], zz[:, b, tap:tap + N], odw[:, ci, tap:tap + 1], zt[:, b, :], ALU.mult, ALU.add))
                dve.wait_ge(u3_ps, 3 * ci + 3)
                V.tensor_tensor(oT1[:, ci, :], bank(2 + 3 * b), zt[:, b, :], ALU.mult).then_inc(o1_out, 1)
            residual(1, zt, 0)
            experts(1)
            stats(0, TT, D, 5 * TT + TC, var_done)
            dve.wait_ge(std_done, 5)
            dve.wait_ge(fw_in, 16)
            for t in range(TT):
                V.scalar_tensor_tensor(h[:, t, :], h[:, t, :], rstd[:, t:t + 1], b2b[:, :], ALU.mult, ALU.mult).then_inc(fin_o, 1)


NAMES = ["x", "c", "ctx", "c_ctx", "ada_w", "ada_b", "norm_mix_w", "norm_ffn_w", "ev_w_in", "ev_conv_w", "ev_conv_b", "ev_ln_w",
         "ev_ln_b", "ev_q_norm_w", "ev_kv_norm_w", "ev_w_uq", "ev_w_ukv", "ev_w_out", "od_w_in", "od_conv_w", "od_w_out",
         "router_w", "router_bias", "exp_w_gate", "exp_w_up", "exp_w_down", "sh_w_gate", "sh_w_up", "sh_w_down", "final_norm_w"]
GRID_W, ROPE_BASE = 64, 10000.0


def constants():
    half = ROPE // 2
    inv = (1.0 / (np.float32(ROPE_BASE) ** (np.arange(0, half, 2, dtype=np.float32) / np.float32(half)))).astype(np.float32)
    n = np.arange(N)
    pos = np.stack([n // GRID_W, n % GRID_W]).astype(np.float32)
    ang = (pos[:, None, :] * inv[None, :, None]).astype(np.float32)
    cos, sin = np.cos(ang), np.sin(ang)
    rope = np.zeros((P, N), np.float32)
    rope[NOPE:NOPE + ROPE] = np.stack([cos, cos], 1).reshape(ROPE, N)
    rope[NOPE + ROPE:] = np.stack([-sin, sin], 1).reshape(ROPE, N)
    first = np.zeros((2, P), np.float32)
    first[0] = 1.0
    return {"k_ident": np.eye(P, dtype=np.float32), "k_before": np.triu(np.ones((P, P), np.float32), 1),
            "k_rope": rope, "k_first": first}


def kernel(**inputs):
    import concourse.bacc as bacc
    from concourse.bass_utils import run_bass_kernel_spmd

    nc = bacc.Bacc("TRN2", target_bir_lowering=False, num_devices=1)
    arrays = {name: np.ascontiguousarray(inputs[name]) for name in NAMES}
    arrays.update(constants())
    aps = {name: nc.dram_tensor(f"in_{name}", v.shape, mybir.dt.from_np(v.dtype), kind="ExternalInput").ap() for name, v in arrays.items()}
    out = nc.dram_tensor("out", (1, N, D), mybir.dt.float32, kind="ExternalOutput").ap()
    scratch = [[nc.dram_tensor(f"{name}{l}", (rows, D), mybir.dt.float32, kind="Internal").ap() for l in range(DEPTH)]
               for name, rows in (("rows_for_experts", N), ("rows_of_experts", N * 8))]
    build(nc, aps, out, scratch)
    result = run_bass_kernel_spmd(nc, [{f"in_{name}": v for name, v in arrays.items()}], core_ids=[0])
    return result.results[0]["out"]
```

```python
import concourse.bass as bass
from concourse import mybir
from contextlib import ExitStack
import numpy as np

P = 128
D = 1024
N = 512
NCTX = 256
KEYS = NCTX + N
KC = D // P
TT, TC = N // P, NCTX // P
CONV, TAPS = 512, 31
PAD = TAPS // 2
CC = CONV // P
HEADS, NOPE, ROPE, VH = 8, 64, 32, 64
QL, KVL = 256, 128
LAT = QL + KVL + ROPE
EXPERTS, TOPK, GROUPS, TOPG = 64, 6, 8, 4
GE = EXPERTS // GROUPS
DE = 256
ROUTED_SCALE = 2.5
EPS = 1e-6
ATT_SCALE = float(NOPE + ROPE) ** -0.5
SC = 1024
SCC = SC // P
MAXB = (N * TOPK + EXPERTS * (P - 1)) // P
MAXP = (MAXB + 1) // 2
COLS = 2 * MAXP + 4
EMPTY = 65536
HB = 512
DEPTH = 2
UNIT = KC // 2 * 2 * DE


def build(nc, a, out, scratch):
    f32, f32r, i32, u32 = mybir.dt.float32, mybir.dt.float32r, mybir.dt.int32, mybir.dt.uint32
    ALU, ACT, AX = mybir.AluOpType, mybir.ActivationFunctionType, mybir.AxisListType
    F_dram, Y_dram, M_dram = scratch
    x, c, ctx_in, c_ctx = a["x"], a["c"], a["ctx"], a["c_ctx"]

    stack = ExitStack()
    with stack:
        sem = lambda name: stack.enter_context(nc.semaphore(name))
        both = lambda name: [sem(f"{name}_{b}") for b in range(2)]
        layers = lambda name: [sem(f"{name}_l{l}") for l in range(DEPTH)]
        keep = lambda name, shape, dt=f32: stack.enter_context(nc.sbuf_tensor(name, shape, dt))

        h = keep("h", [P, TT, D])
        ident = keep("ident", [P, P])
        ones = keep("ones", [P, P])
        before = keep("before", [P, P])
        iota_row = keep("iota_row", [P, P])
        iota_part = keep("iota_part", [P, 1])
        pair_val = keep("pair_val", [P, TT, 8])
        one_over = keep("one_over", [P, P])
        ccol = keep("ccol", [P, 2, KC])
        csil = keep("csil", [P, 2, KC])
        acol = keep("acol", [P, 2, 2, KC])
        nwcol = keep("nwcol", [P, DEPTH, KC])
        g1b = keep("g1b", [P, D])
        g2b = keep("g2b", [P, D])
        a2b = keep("a2b", [P, D])
        b2b = keep("b2b", [P, D])
        def region():
            return ExitStack()

        rr = region()
        mr = lambda name, shape, dt=f32: rr.enter_context(nc.sbuf_tensor(name, shape, dt))
        score = mr("score", [P, TT, EXPERTS])
        sel = mr("sel", [P, TT, EXPERTS])
        g8 = mr("g8", [P, TT, GROUPS, 8])
        gsum = mr("gsum", [P, TT, GROUPS])
        top8 = mr("top8", [P, TT, 8])
        idx8 = mr("idx8", [P, TT, 8], u32)
        idxf = mr("idxf", [P, TT, 8])
        geq = mr("geq", [P, TT, GROUPS, TOPG])
        gmask = mr("gmask", [P, TT, GROUPS])
        wsum = mr("wsum", [P, TT])
        mask = mr("mask", [P, TT, EXPERTS])
        rbias = mr("rbias", [P, EXPERTS])
        nblk = mr("nblk", [P, EXPERTS])
        pend = mr("pend", [P, EXPERTS])
        bst = mr("bst", [P, EXPERTS])
        code = mr("code", [P, TT * TOPK])
        codei = mr("codei", [P, 2, TT * TOPK], i32)
        slotf = mr("slotf", [P, TT * TOPK])
        blkf = mr("blkf", [P, TT * TOPK])
        junk_e = mr("junk_e", [P, EXPERTS])
        rr.close()
        nrow = keep("nrow", [P, D])
        mrow = keep("mrow", [2, 2, HB])
        adab = keep("adab", [2, 2, HB])
        rt = keep("rt", [P, 2, HB])
        adaw = keep("adaw", [P, 2, KC, HB])
        last_loop_pair = keep("last_loop_pair", [1, 2 * DEPTH], i32)
        ssq = keep("ssq", [P, 24])
        rstd = keep("rstd", [P, 24])
        rope = keep("rope", [P, N])
        cvw = keep("cvw", [P, CC, TAPS + 3])
        odw = keep("odw", [P, SCC, 3])
        qnw = keep("qnw", [P, 2])
        kvw = keep("kvw", [P, 1])

        r0 = region()
        m0 = lambda name, shape, dt=f32: r0.enter_context(nc.sbuf_tensor(name, shape, dt))
        aT = m0("aT", [P, KC, KEYS])
        wlat = m0("wlat", [P, KC, LAT + ROPE])
        wab = m0("wab", [P, 2, KC, 2, P])
        vv = wab.rearrange("p b k j n -> p (b k j n)")[:, 0:(TT + TC) * HEADS * VH].rearrange("p (t n) -> p t n", n=HEADS * VH)
        wuq = m0("wuq", [P, 2, HEADS, P])
        wukv = m0("wukv", [P, HEADS, NOPE + VH])
        r0e = region()
        m0e = lambda name, shape, dt=f32: r0e.enter_context(nc.sbuf_tensor(name, shape, dt))
        r0l = region()
        m0l = lambda name, shape, dt=f32: r0l.enter_context(nc.sbuf_tensor(name, shape, dt))
        crow = m0e("crow", [TAPS + 3, CONV])
        orow = m0e("orow", [3, D])
        rn = m0e("rn", [P, TT + TC, D])
        hc = m0e("hc", [P, TC, D])
        r0e.close()
        pe_ = m0l("pe_", [P, 2, KEYS])
        pT = m0l("pT", [P, 2, KEYS])
        kT = m0l("kT", [P, 2, KEYS])
        qT = m0l("qT", [P, 2, N])
        vpad = m0l("vpad", [P, CC, N + 2 * PAD])
        cy = m0l("cy", [P, CC, N])
        csg = m0l("csg", [P, 2, N])
        cqT = m0l("cqT", [P, 2, N])
        ckvT = m0l("ckvT", [P, KEYS])
        krT = m0l("krT", [P, KEYS])
        stat = m0l("stat", [P, 4, 3])
        r0l.close()
        r0q = region()
        cqs = r0q.enter_context(nc.sbuf_tensor("cqs", [P, TT + TC, QL + KVL], f32))
        r0q.close()
        r0.close()
        r0b = region()
        m0b = lambda name, shape, dt=f32: r0b.enter_context(nc.sbuf_tensor(name, shape, dt))
        catT = m0b("catT", [P, 2, CC, N])
        oo = m0b("oo", [P, TT, HEADS * VH])
        r0b.close()
        wo0 = adaw

        r1 = region()
        m1 = lambda name, shape, dt=f32: r1.enter_context(nc.sbuf_tensor(name, shape, dt))
        rn1 = m1("rn1", [P, TT, D])
        aT1 = m1("aT1", [P, KC, N])
        zz = m1("zz", [P, 2, N + 2])
        cgs = m1("cgs", [P, 2, N])
        zt = m1("zt", [P, 2, N])
        oT1 = m1("oT1", [P, SCC, N])
        gap1 = m1("gap1", [P, D - 4])
        w3 = m1("w3", [P, 3, KC, 3, P])
        r1.close()
        wo1 = adaw

        rm = region()
        mm = lambda name, shape, dt=f32: rm.enter_context(nc.sbuf_tensor(name, shape, dt))
        wh = mm("wh", [P, 3, UNIT], f32r)
        wl = mm("wl", [P, 3, UNIT], f32r)
        acc = mm("acc", [P, TT, D])
        rr = region()
        mr = lambda name, shape, dt=f32: rr.enter_context(nc.sbuf_tensor(name, shape, dt))
        eq = mr("eq", [P, TT, TOPK, EXPERTS])
        eqw = mr("eqw", [P, TT, TOPK, EXPERTS])
        hot_s = mr("hot_s", [P, 4, P])
        hot_b = mr("hot_b", [P, 4, COLS])
        rr.close()
        xg = mm("xg", [P, 2, D])
        yo = mm("yo", [P, 2, D])
        rf = region()
        fTl = rf.enter_context(nc.sbuf_tensor("fTl", [P, KC, N], f32r))
        rf.close()
        xTh = mm("xTh", [P, 2, KC, P], f32r)
        xTl = mm("xTl", [P, 2, KC, P], f32r)
        rf = region()
        fTh = rf.enter_context(nc.sbuf_tensor("fTh", [P, KC, N], f32r))
        rf.close()
        raw45 = mm("raw45", [P, 2, UNIT])
        rf = region()
        rw = rf.enter_context(nc.sbuf_tensor("rw", [P, KC, EXPERTS], f32))
        rwh = rf.enter_context(nc.sbuf_tensor("rwh", [P, KC, EXPERTS], f32r))
        rwl = rf.enter_context(nc.sbuf_tensor("rwl", [P, KC, EXPERTS], f32r))
        rf.close()
        sg = mm("sg", [P, 2, DE])
        hTh = mm("hTh", [P, 2, 2, P], f32r)
        hTl = mm("hTl", [P, 2, 2, P], f32r)
        hh = mm("hh", [P, 2, DE])
        wts = mm("wts", [P, TT, TOPK])
        becol = mm("becol", [P, 1])
        vtab = mm("vtab", [P, COLS], i32)
        ttab = mm("ttab", [P, COLS], i32)
        etab = mm("etab", [1, COLS], i32)
        xid = mm("xid", [P, 2], u32)
        yid = mm("yid", [P, 2], u32)
        rm.close()
        ry = region()
        yl = ry.enter_context(nc.sbuf_tensor("yl", [P, 2, TOPK, D], f32))
        ry.close()

        raw4 = adaw.rearrange("p b k n -> p (b k n)").rearrange("p (r n) -> p r n", n=UNIT)
        raw = lambda r: raw4[:, r, :] if r < 4 else raw45[:, r - 4, :]

        pp = [stack.enter_context(nc.psum_tensor(f"pp{i}", [P, 2 * HB], f32)) for i in range(4)]
        bank = lambda i: pp[i // 2][:, (i % 2) * HB:(i % 2 + 1) * HB]

        c_in = sem("c_in"); x_in = sem("x_in"); hc_in = sem("hc_in"); const_in = sem("const_in"); rows_in = sem("rows_in")
        q_const = sem("q_const"); pool_set = sem("pool_set")
        ada_in = both("ada_in"); ada_ps = sem("ada_ps"); ada_row = sem("ada_row")
        mod_st = both("mod_st"); acol_in = sem("acol_in"); ada_col = sem("ada_col"); g1_in = sem("g1_in"); ab_in = sem("ab_in"); g2_in = sem("g2_in")
        csil_ok = sem("csil_ok")
        sq_done = sem("sq_done"); var_done = sem("var_done"); std_done = sem("std_done"); rn_done = sem("rn_done")
        t_ps = sem("t_ps"); t_out = sem("t_out")
        cw_ps = sem("cw_ps"); cw_out = sem("cw_out")
        wlat_in = sem("wlat_in"); wlat_swap = sem("wlat_swap"); wab_in = both("wab_in"); wab_used = sem("wab_used")
        wu_in = sem("wu_in"); wu_swap = sem("wu_swap"); wo_in = sem("wo_in")
        lat_ps = sem("lat_ps"); lat_out = sem("lat_out"); lat_sq = sem("lat_sq"); lat_var = sem("lat_var"); lat_std = sem("lat_std")
        lat_n = sem("lat_n"); latT_ps = sem("latT_ps"); latT_out = sem("latT_out")
        kr_ps = sem("kr_ps"); kr_out = sem("kr_out"); krc_out = sem("krc_out")
        u_ps = sem("u_ps"); sg_out = sem("sg_out"); v_out = sem("v_out")
        cv_done = sem("cv_done"); mean_ps = sem("mean_ps"); d_done = sem("d_done"); dsq = sem("dsq"); varc_ps = sem("varc_ps")
        cvar = sem("cvar"); cstd = sem("cstd"); dn = sem("dn"); ca_out = sem("ca_out")
        v_ps = sem("v_ps"); vv_out = sem("vv_out")
        kn_ps = sem("kn_ps"); kn_out = sem("kn_out"); kr_copy = sem("kr_copy")
        q_ps = sem("q_ps"); qn_out = sem("qn_out"); qr_out = sem("qr_out")
        s_ps = sem("s_ps"); mx = sem("mx"); ex = sem("ex"); pt_ps = sem("pt_ps"); pt_out = sem("pt_out"); pv_ps = sem("pv_ps")
        o_out = sem("o_out"); oT_ps = sem("oT_ps"); oT_out = sem("oT_out")
        y_ps = sem("y_ps"); y_g = sem("y_g"); h_new = sem("h_new")
        w3_in = [sem(f"w3_in{i}") for i in range(3)]
        u3_ps = sem("u3_ps"); cg_out = sem("cg_out"); z_out = sem("z_out"); o1_out = sem("o1_out")
        PER = {"f_done": TT, "f_stored": 16 * TT, "fT_ps": KC, "fT_out": KC, "lg_ps": 1, "sc_out": 1, "rt": 1,
               "rk_in": 1, "rk_ps": 1, "places": 1, "hot": 2 * TT * TOPK, "hot_used": TT * TOPK, "tables": 4, "be_ps": 1, "rconst_in": 32,
               "rw_hi": 1, "rw_lo": 1, "fT_hi": KC, "comb": TT * TOPK, "hfin": TT, "yl_in0": 16 * TT // 2, "yl_in1": 16 * TT // 2}
        L = {name: [sem(name)] * DEPTH for name in PER}
        at = lambda l, name, n: PER[name] * l + n
        for name in ("w_in0 w_in1 w_in2 w_in3 w_in4 w_in5 x_in0 x_in1 yw0 yw1 ye0 ye1 yp0 yp1 xp0 x_used x_hi x_lo x_id y_id "
                     "gu_h gu s hm hp h_hi ho whg whd w_gu w_d fence").split():
            L[name] = [sem(name)] * DEPTH
        fin_o = sem("fin_o"); stored = sem("stored"); fw_in = sem("fw_in")

        block = stack.enter_context(nc.Block())

        class Counts:

            def __init__(self, eng, l):
                self.l = l
                self.off = eng.value_load(last_loop_pair[0:1, 0:1], min_val=10, max_val=MAXP - 2) + 2 if l else 0

            def n(self, b, i):
                return 2 * (i + self.off) + b

            def tile(self, t):
                return TT * self.l + 2 * self.off + t + 1

            def block(self, b, i):
                return TT * (self.l + 1) + self.n(b, i) + 1

            def arrived(self, b, i, u):
                return (16 if u == 2 else 32) * (i + self.off + 1 + (self.l + 1 if b == 0 else 0))

            def shared_arrived(self, u):
                return (16 if u == 2 else 32) * (self.off + self.l + 1)

            def split(self, b, i, u):
                return (self.l + 1) + self.n(b, i) + 1 if u == 2 else 2 * (self.l + 1) + 2 * self.n(b, i) + u + 1

            def shared_split(self, u):
                return self.l + 2 * self.off + 1 if u == 2 else 2 * self.l + 4 * self.off + u + 1

        def run_blocks(eng, last, step):
            for b in range(2):
                step(b, 0, first=(b == 0))
            with eng.Fori(1, last) as i:
                for b in range(2):
                    step(b, i)
            for b in range(2):
                step(b, last, last=(b == 1), last_pair=True)

        after = lambda b, i: (1, i) if b == 0 else (0, i + 1)
        prior = lambda b, i: (1, i - 1) if b == 0 else (0, i)

        Y3 = [y.rearrange("(t p e) d -> p t e d", p=P, e=8) for y in Y_dram]
        F3 = [f.rearrange("(t p) d -> p t d", p=P) for f in F_dram]
        adaw_d = [a["ada_w"][l].rearrange("(p k) n -> p k n", k=KC) for l in range(DEPTH)]
        win_d = a["ev_w_in"][0].rearrange("(p k) n -> p k n", k=KC)
        w3_d = a["od_w_in"][0].rearrange("(p k) (j n) -> p k j n", k=KC, j=3)
        NSEC = 6
        SH1, SC1, G1, SH2, SC2, G2 = range(NSEC)
        CHUNKS = 2 * NSEC
        FIRST = 4
        MID = 4

        @block.sync
        def _(sp):
            sp.dma_start(ccol[:, 0, :], c.rearrange("a (p k) -> (a p) k", k=KC)).then_inc(c_in, 16)
            sp.dma_start(ccol[:, 1, :], c_ctx.rearrange("(p k) -> p k", k=KC)).then_inc(c_in, 16)
            sp.dma_start(h[:, :, :], x[0].rearrange("(t p) d -> p t d", p=P)).then_inc(x_in, 16)
            sp.dma_start(hc[:, :, :], ctx_in[0].rearrange("(t p) d -> p t d", p=P)).then_inc(hc_in, 16)

            def load_ada(m):
                l, n = m // CHUNKS, m % CHUNKS
                if m >= 2:
                    sp.wait_ge(ada_row, m - 1)
                sp.dma_start(adaw[:, m % 2, :, :], adaw_d[l][:, :, n * HB:(n + 1) * HB]).then_inc(ada_in[m % 2], 16)
                sp.dma_start(adab[:, m % 2, :], a["ada_b"][l:l + 1, n * HB:(n + 1) * HB].partition_broadcast(2).rearrange("p a d -> p (a d)")).then_inc(ada_in[m % 2], 16)

            for m in range(FIRST):
                load_ada(m)
            sp.dma_start(wlat[:, :, 0:LAT], win_d[:, :, 2 * CONV:]).then_inc(wlat_in, 16)
            for ci in range(CC):
                if ci >= 2:
                    sp.wait_ge(wab_used, ci - 1)
                for j in range(2):
                    sp.dma_start(wab[:, ci % 2, :, j, :], win_d[:, :, j * CONV + ci * P:j * CONV + (ci + 1) * P]).then_inc(wab_in[ci % 2], 16)
                if ci == 1:
                    sp.dma_start(wuq[:, :, :, 0:NOPE + ROPE], a["ev_w_uq"][0].rearrange("(p j) h d -> p j h d", j=2)).then_inc(wu_in, 16)
                    sp.dma_start(wukv[:, :, :], a["ev_w_ukv"][0]).then_inc(wu_in, 16)
                    load_ada(FIRST)
                    load_ada(FIRST + 1)
            for m in range(FIRST + 2, DEPTH * CHUNKS):
                load_ada(m)
            wo0v = wo0.rearrange("p b k n -> p (b k n)").rearrange("p (c n) -> p c n", n=D)
            sp.wait_ge(ada_row, DEPTH * CHUNKS - 1)
            sp.dma_start(wo0v[:, 0:CC, :], a["ev_w_out"][0, 0:CONV, :].rearrange("(c p) n -> p c n", p=P)).then_inc(wo_in, 16)
            sp.wait_ge(ada_row, DEPTH * CHUNKS)
            sp.dma_start(wo0v[:, CC:2 * CC, :], a["ev_w_out"][0, CONV:, :].rearrange("(p c) n -> p c n", c=CC)).then_inc(wo_in, 16)

            def load_wo():
                wo1v = wo1.rearrange("p b k n -> p (b k n)").rearrange("p (c n) -> p c n", n=D)
                sp.dma_start(wo1v, a["od_w_out"][0].rearrange("(c p) n -> p c n", p=P)).then_inc(wo_in, 16)

            def load_short_conv():
                for ci in range(SCC):
                    if ci == 3:
                        load_wo()
                    if ci >= 3:
                        sp.wait_ge(u3_ps, 3 * (ci - 2))
                    for j in range(3):
                        sp.dma_start(w3[:, ci % 3, :, j, :], w3_d[:, :, j, ci * P:(ci + 1) * P]).then_inc(w3_in[ci % 3], 16)

            def experts(l):
                s = {k: v[l] for k, v in L.items()}
                sp.wait_ge(h_new, 2 * TT * (l + 1))
                sp.dma_start(rw[:, :, :], a["router_w"][l].rearrange("(p k) e -> p k e", k=KC)).then_inc(s["rconst_in"], 16)
                for b in range(2):
                    sp.wait_ge(mod_st[b], 16 * CHUNKS * DEPTH // 2)
                sp.dma_start(rbias[:, :], a["router_bias"][l:l + 1, :].partition_broadcast(P).rearrange("p a d -> p (a d)")).then_inc(s["rconst_in"], 16)

                def half(r, name, j, u, src):
                    sp.dma_start(raw(r)[:, j * (UNIT // 2):(j + 1) * (UNIT // 2)].rearrange("p (k n) -> p k n", n=DE),
                                 src.rearrange("(p k) n -> p k n", k=KC)[:, u * KC // 2:(u + 1) * KC // 2, :]).then_inc(s[f"w_in{r}"], 16)

                for u in range(2):
                    for j, name in enumerate(("sh_w_gate", "sh_w_up")):
                        half(u, name, j, u, a[name][l])
                sp.dma_start(raw(2), a["sh_w_down"][l].rearrange("(p j) n -> p (j n)", j=2)).then_inc(s["w_in2"], 16)
                for t in range(TT):
                    sp.wait_ge(s["f_done"], at(l, "f_done", t + 1))
                    sp.dma_start(F3[l][:, t, :], acc[:, t, :]).then_inc(s["f_stored"], 16)
                sp.wait_ge(s["tables"], at(l, "tables", 4))
                last = sp.value_load(last_loop_pair[0:1, 2 * l:2 * l + 1], min_val=10, max_val=MAXP - 2) + 1
                cn = Counts(sp, l)

                def load(b, i, u, e, behind):
                    r = 3 * b + u
                    if behind:
                        sp.wait_ge(s["w_d" if u == 2 else "w_gu"], cn.split(b, i - 1, u))
                    elif b == 0:
                        sp.wait_ge(s["w_d" if u == 2 else "w_gu"], cn.shared_split(u))
                    elif u:
                        sp.wait_ge(s["gu"], cn.tile(TT - 1))
                    if u == 2:
                        sp.dma_start(raw(r).rearrange("p (a n) -> p a n", a=1),
                                     a["exp_w_down"][l][bass.ds(e, 1), :, :].rearrange("a (p j) n -> p a (j n)", j=2)).then_inc(s[f"w_in{r}"], 16)
                    else:
                        for j, name in enumerate(("exp_w_gate", "exp_w_up")):
                            sp.dma_start(raw(r)[:, j * (UNIT // 2):(j + 1) * (UNIT // 2)].rearrange("p (a k n) -> p a k n", a=1, n=DE),
                                         a[name][l][bass.ds(e, 1), :, :].rearrange("a (p k) n -> p a k n", k=KC)[:, :, u * KC // 2:(u + 1) * KC // 2, :]).then_inc(s[f"w_in{r}"], 16)

                def expert(b, i):
                    return sp.value_load(etab[0:1, bass.ds(2 * i + b, 1)], min_val=0, max_val=EXPERTS - 1)

                def step(b, i, first=False, last=False, last_pair=False):
                    here = type(i) is int and i == 0
                    if not last:
                        nb, ni = after(b, i)
                        e = expert(nb, ni)
                        for u in range(2):
                            load(nb, ni, u, e, behind=not (here and b == 0))
                    load(b, i, 2, expert(b, i), behind=not here)

                e = expert(0, 0)
                for u in range(2):
                    load(0, 0, u, e, behind=False)
                run_blocks(sp, last, step)
                for b in range(2):
                    sp.wait_ge(s[f"yw{b}"], 16 * (last + 1 + cn.off))
                    sp.sem_inc(s["fence"], 1)
                sp.wait_ge(s["yp1"], TT * (l + 1) + 2 * (last + 1 + cn.off))
                sp.sem_inc(s["fence"], 1)
                for t in range(TT):
                    if t >= 2:
                        sp.wait_ge(s["comb"], at(l, "comb", TOPK * (t - 1)))
                    sp.dma_start(yl[:, t % 2, :, :], Y3[l][:, t, 0:TOPK, :]).then_inc(s[f"yl_in{t % 2}"], 16)

            experts(0)
            load_short_conv()
            experts(1)
            sp.wait_ge(L["hfin"][1], 2 * TT)
            sp.dma_start(b2b[:, :], a["final_norm_w"].rearrange("(a n) -> a n", a=1).partition_broadcast(P).rearrange("p a d -> p (a d)")).then_inc(fw_in, 16)
            for t in range(TT):
                sp.wait_ge(fin_o, t + 1)
                sp.dma_start(out[0].rearrange("(t p) d -> p t d", p=P)[:, t, :], h[:, t, :]).then_inc(stored, 16)
            sp.wait_ge(stored, 16 * TT)

        @block.gpsimd
        def _(pool):
            for dst, name in ((ident, "k_ident"), (before, "k_before"), (rope, "k_rope")):
                pool.dma_start(dst[:, :], a[name]).then_inc(const_in, 16)
            pool.dma_start(crow[0:TAPS, :], a["ev_conv_w"][0].rearrange("t a n -> t (a n)")).then_inc(rows_in, 16)
            for j, name in enumerate(("ev_conv_b", "ev_ln_w", "ev_ln_b")):
                pool.dma_start(crow[TAPS + j:TAPS + j + 1, :], a[name]).then_inc(rows_in, 16)
            pool.dma_start(orow[:, :], a["od_conv_w"][0].rearrange("t a n -> t (a n)")).then_inc(rows_in, 16)
            pool.dma_start(qnw[:, :], a["ev_q_norm_w"].rearrange("a (p j) -> p (a j)", j=2)).then_inc(q_const, 16)
            pool.dma_start(kvw[:, :], a["ev_kv_norm_w"].rearrange("a p -> p a")).then_inc(q_const, 16)
            pool.dma_start(nwcol[:, :, :], a["norm_mix_w"].rearrange("l (p k) -> p l k", k=KC)).then_inc(q_const, 16)
            nc.gpsimd.memset(ones[:, :], 1.0).then_inc(pool_set, 1)
            nc.gpsimd.memset(one_over[:, :], 1.0 / CONV).then_inc(pool_set, 1)
            nc.gpsimd.iota(iota_row[:, :], pattern=[[1, P]], base=0, channel_multiplier=0, allow_small_or_imprecise_dtypes=True).then_inc(pool_set, 1)
            nc.gpsimd.iota(iota_part[:, :], pattern=[[0, 1]], base=0, channel_multiplier=1, allow_small_or_imprecise_dtypes=True).then_inc(pool_set, 1)
            nc.gpsimd.iota(pair_val[:, :, :], pattern=[[8 * P, TT], [1, 8]], base=-EMPTY, channel_multiplier=8, allow_small_or_imprecise_dtypes=True).then_inc(pool_set, 1)

            def store_rows(m0, m1):
                for m in range(m0, m1):
                    pool.wait_ge(ada_row, m + 1)
                    n = m % CHUNKS
                    pool.dma_start(M_dram[m // CHUNKS][:, n * HB:(n + 1) * HB], mrow[:, m % 2, :]).then_inc(mod_st[m % 2], 16)

            def rows_stored(m):
                for b in range(2):
                    pool.wait_ge(mod_st[b], 16 * m // 2)

            def load_columns(l):
                for sct in (SH1, SC1):
                    pool.dma_start(acol[:, sct, :, :], M_dram[l][:, sct * D:(sct + 1) * D].rearrange("r (p k) -> p r k", k=KC)).then_inc(acol_in, 16)

            def load_row(l, sct, dst, signal):
                pool.dma_start(dst[:, :], M_dram[l][0:1, sct * D:(sct + 1) * D].partition_broadcast(P).rearrange("p a d -> p (a d)")).then_inc(signal, 16)

            def load_ffn_rows(l):
                load_row(l, SH2, b2b, ab_in)
                load_row(l, SC2, a2b, ab_in)
                pool.dma_start(nrow[:, :], a["norm_ffn_w"][l:l + 1, :].partition_broadcast(P).rearrange("p a d -> p (a d)")).then_inc(ab_in, 16)

            store_rows(0, FIRST)
            rows_stored(FIRST)
            load_columns(0)
            pool.wait_ge(wlat_in, 16)
            q8 = ROPE // 4
            for ax in range(2):
                for half in range(2):
                    d0, s0 = LAT + (2 * ax + half) * q8, QL + KVL + (2 * ax + 1 - half) * q8
                    nc.gpsimd.tensor_copy(wlat[:, :, d0:d0 + q8], wlat[:, :, s0:s0 + q8]).then_inc(wlat_swap, 1)
            pool.wait_ge(wu_in, 32)
            wuqv = wuq.rearrange("p j h d -> p (j h) d")
            for ax in range(2):
                for half in range(2):
                    d0, s0 = NOPE + ROPE + (2 * ax + half) * q8, NOPE + (2 * ax + 1 - half) * q8
                    nc.gpsimd.tensor_copy(wuqv[:, :, d0:d0 + q8], wuqv[:, :, s0:s0 + q8]).then_inc(wu_swap, 1)
            pool.wait_ge(t_ps, 2 * KC)
            nc.gpsimd.memset(vpad[:, :, :], 0.0).then_inc(pool_set, 1)
            pool.wait_ge(kr_out, 1)
            pool.wait_ge(krc_out, 1)
            pool.wait_ge(wu_swap, 4)
            pool.wait_ge(pool_set, 6)
            for b in range(2):
                if b:
                    pool.wait_ge(kr_copy, b)
                nc.gpsimd.tensor_copy(kT[NOPE:NOPE + ROPE, b, :], krT[NOPE:NOPE + ROPE, :]).then_inc(kr_copy, 1)

            store_rows(FIRST, CHUNKS)
            rows_stored(CHUNKS)
            load_row(0, G1, g1b, g1_in)
            load_ffn_rows(0)
            load_row(0, G2, g2b, g2_in)
            store_rows(CHUNKS, DEPTH * CHUNKS)
            rows_stored(DEPTH * CHUNKS)
            pool.wait_ge(t_out, 2 * KC)
            load_columns(1)

            def experts(l):
                s = {k: v[l] for k, v in L.items()}
                pool.wait_ge(h_new, 2 * TT * (l + 1))
                if l + 1 < DEPTH:
                    load_row(l + 1, G1, g1b, g1_in)
                pool.wait_ge(kr_copy, 2)
                pool.wait_ge(s["tables"], at(l, "tables", 4))
                pool.wait_ge(s["f_stored"], at(l, "f_stored", 16 * TT))
                last = pool.value_load(last_loop_pair[0:1, 2 * l:2 * l + 1], min_val=10, max_val=MAXP - 2) + 1
                cn = Counts(pool, l)

                def settled(name, value):
                    pool.wait_ge(s[name], value)
                    pool.sem_inc(s["fence"], 1)

                def by_fill(b, i, move):
                    token = pool.value_load(ttab[P // 2:P // 2 + 1, bass.ds(2 * i + b, 1)], min_val=0, max_val=EMPTY // 8)
                    with pool.If(token < N):
                        move(P)
                    with pool.Else():
                        move(P // 2)

                def gather(b, i, behind):
                    if behind:
                        settled("x_used", cn.n(b, i - 1) + 1)
                    nc.gpsimd.tensor_copy(xid[:, b:b + 1], ttab[:, bass.ds(2 * i + b, 1)]).then_inc(s["x_id"], 1)
                    settled("x_id", cn.n(b, i) + 1)

                    def rows(n):
                        nc.gpsimd.indirect_dma_start(
                            xg[0:n, b, :], None, F_dram[l][:, :], bass.IndirectOffsetOnAxis(ap=xid[0:n, b:b + 1], axis=0),
                            bounds_check=N - 1, oob_is_err=False).then_inc(s[f"x_in{b}"], 16)

                    if type(i) is int:
                        rows(P)
                    else:
                        by_fill(b, i, rows)

                def scatter(b, i, behind):
                    if behind:
                        settled(f"yw{b}", 16 * (i + cn.off))
                    nc.gpsimd.tensor_copy(yid[:, b:b + 1], vtab[:, bass.ds(2 * i + b, 1)]).then_inc(s["y_id"], 1)
                    settled("y_id", cn.n(b, i) + 1)
                    settled("ye0", cn.block(b, i))
                    settled("ye1", cn.block(b, i))
                    by_fill(b, i, lambda n: nc.gpsimd.indirect_dma_start(
                        Y_dram[l][:, :], bass.IndirectOffsetOnAxis(ap=yid[0:n, b:b + 1], axis=0), yo[0:n, b, :], None,
                        bounds_check=N * 8 - 1, oob_is_err=False).then_inc(s[f"yw{b}"], 16))

                def step(b, i, first=False, last=False, last_pair=False):
                    if not last_pair:
                        gather(b, i + 1, True)
                    if not first:
                        pb, pi = prior(b, i)
                        scatter(pb, pi, behind=not (type(pi) is int and pi == 0) if pb else not (type(pi) is int and pi == 0))

                for b in range(2):
                    gather(b, 0, False)
                run_blocks(pool, last, step)
                scatter(1, last, True)

            experts(0)
            load_ffn_rows(1)
            pool.wait_ge(L["hfin"][0], TT)
            load_row(1, G2, g2b, g2_in)
            experts(1)

        @block.tensor
        def _(pe):
            mmul = nc.tensor.matmul

            def split_mm(o, lh, ll, rh, rl, start, stop):
                mmul(o, lh, rh, start=start, stop=False)
                mmul(o, lh, rl, start=False, stop=False)
                return mmul(o, ll, rh, start=False, stop=stop)

            def ada_part(m, k0, k1, o):
                if k0 == 0:
                    pe.wait_ge(ada_in[m % 2], 32 * (m // 2 + 1))
                for k in range(k0, k1):
                    ins = mmul(o[0:2, :], csil[:, :, k], adaw[:, m % 2, k, :], start=(k == 0), stop=(k == KC - 1))
                if k1 == KC:
                    ins.then_inc(ada_ps, 1)

            pe.wait_ge(const_in, 48)
            pe.wait_ge(rows_in, 80)
            for ci in range(CC):
                ins = nc.tensor.transpose(bank(6)[:, ci * 40:ci * 40 + TAPS + 3], crow[:, ci * P:(ci + 1) * P], ident[0:TAPS + 3, 0:TAPS + 3])
            for ci in range(SCC):
                ins = nc.tensor.transpose(bank(6)[:, 256 + ci * 4:256 + ci * 4 + 3], orow[:, ci * P:(ci + 1) * P], ident[0:3, 0:3])
            ins.then_inc(cw_ps, 1)
            pe.wait_ge(csil_ok, 1)
            for m in range(FIRST):
                if m >= 2:
                    pe.wait_ge(ada_row, m - 1)
                ada_part(m, 0, KC, bank(m % 2))
            pe.wait_ge(ada_row, FIRST)

            for k in range(KC):
                for part in range(2):
                    n = 2 * k + part
                    if n == 0:
                        pe.wait_ge(rn_done, TT + TC)
                    if n >= 2:
                        pe.wait_ge(t_out, n - 1)
                    for t in range(TT if part == 0 else TC):
                        ins = nc.tensor.transpose(bank(n % 2)[:, t * P:(t + 1) * P], rn[:, t + (TT if part else 0), k:D:KC], ident[:, :])
                    ins.then_inc(t_ps, 1)

            pe.wait_ge(t_out, 2 * KC)
            pe.wait_ge(wlat_in, 16)
            for t in range(TT + TC):
                if t >= 2:
                    pe.wait_ge(lat_out, t - 1)
                w = QL + KVL if t < TT else KVL
                key0 = NCTX + t * P if t < TT else (t - TT) * P
                for k in range(KC):
                    ins = mmul(bank(2 + t % 2)[:, 0:w], aT[:, k, key0:key0 + P], wlat[:, k, QL + KVL - w:QL + KVL], start=(k == 0), stop=(k == KC - 1))
                ins.then_inc(lat_ps, 1)
            pe.wait_ge(wlat_swap, 4)
            for j, (k0, kn) in enumerate(((NCTX, N), (0, NCTX))):
                for k in range(KC):
                    ins = mmul(bank(4 + j)[:, 0:kn], wlat[:, k, LAT - ROPE - NOPE:LAT + ROPE], aT[:, k, k0:k0 + kn], start=(k == 0), stop=(k == KC - 1))
                ins.then_inc(kr_ps, 1)
            pe.wait_ge(cw_out, 2)
            for ci in range(CC):
                pe.wait_ge(wab_in[ci % 2], 32 * (ci // 2 + 1))
                if ci >= 1:
                    pe.wait_ge(v_out, ci)
                for j in range(2):
                    for k in range(KC):
                        ins = mmul(bank(6 + j), wab[:, ci % 2, k, j, :], aT[:, k, NCTX:], start=(k == 0), stop=(k == KC - 1))
                    ins.then_inc(u_ps if j == 0 else wab_used, 1)
            pe.wait_ge(kr_out, 1)
            pe.wait_ge(krc_out, 1)
            for m in range(FIRST, FIRST + MID):
                if m >= FIRST + 2:
                    pe.wait_ge(ada_row, m - 1)
                ada_part(m, 0, KC, bank(4 + m % 2))
            pe.wait_ge(lat_n, 2 * TT + TC)
            for j in range(2):
                for t in range(TT):
                    ins = nc.tensor.transpose(bank(j)[:, t * P:(t + 1) * P], cqs[:, t, j:QL:2], ident[:, :])
                ins.then_inc(latT_ps, 1)
            pe.wait_ge(lat_out, TT + TC)
            for t in range(TC):
                ins = nc.tensor.transpose(bank(2)[:, t * P:(t + 1) * P], cqs[:, TT + t, QL:], ident[:, :])
            ins.then_inc(latT_ps, 1)
            for t in range(TT):
                ins = nc.tensor.transpose(bank(3)[:, t * P:(t + 1) * P], cqs[:, t, QL:], ident[:, :])
            ins.then_inc(latT_ps, 1)
            pe.wait_ge(wu_in, 32)
            pe.wait_ge(latT_out, 4)
            pe.wait_ge(ada_row, FIRST + MID)
            for t in range(TT + TC):
                if t >= 2:
                    pe.wait_ge(vv_out, t - 1)
                mmul(bank(4 + t % 2), ckvT[:, t * P:(t + 1) * P], wukv[:, :, NOPE:], start=True, stop=True).then_inc(v_ps, 1)
            pe.wait_ge(wu_swap, 4)
            pe.wait_ge(kr_copy, 2)
            pe.wait_ge(vv_out, TT + TC)
            pe.wait_ge(v_out, CC)
            S = [pp[0], pp[1]]
            for hd in range(HEADS):
                if hd >= 1:
                    pe.wait_ge(pt_out, TT * hd)
                for n0, nn in ((0, HB), (HB, KEYS - HB)):
                    ins = mmul(pp[3][0:NOPE, n0:n0 + nn], wukv[:, hd, 0:NOPE], ckvT[:, n0:n0 + nn], start=True, stop=True)
                ins.then_inc(kn_ps, 1)
                pe.wait_ge(ada_row, FIRST + MID + 2 * hd)
                for j in range(2):
                    ins = mmul(bank(5), wuq[:, j, hd, :], cqT[:, j, :], start=(j == 0), stop=(j == 1))
                ins.then_inc(q_ps, 1)
                pe.wait_ge(kn_out, hd + 1)
                pe.wait_ge(qn_out, hd + 1)
                pe.wait_ge(qr_out, hd + 1)

                def scores(t):
                    n = hd * TT + t
                    if n >= 2:
                        pe.wait_ge(ex, n - 1)
                    for n0, nn in ((0, HB), (HB, KEYS - HB)):
                        ins = mmul(S[n % 2][:, n0:n0 + nn], qT[0:NOPE + ROPE, hd % 2, t * P:(t + 1) * P], kT[0:NOPE + ROPE, hd % 2, n0:n0 + nn], start=True, stop=True)
                    ins.then_inc(s_ps, 1)

                scores(0)
                for t in range(TT):
                    n = hd * TT + t
                    if t + 1 < TT:
                        scores(t + 1)
                    m, k0 = FIRST + MID + n // 2, n % 2 * KC // 2
                    if n % 2 == 0:
                        pe.wait_ge(ada_row, m)
                    ada_part(m, k0, k0 + KC // 4, bank(5))
                    pe.wait_ge(ex, n + 1)
                    if n >= 1:
                        pe.wait_ge(pt_out, n)
                    for j in range(KEYS // P):
                        ins = nc.tensor.transpose(pp[3][:, j * P:(j + 1) * P], pe_[:, n % 2, j * P:(j + 1) * P], ident[:, :])
                    ins.then_inc(pt_ps, 1)
                    ada_part(m, k0 + KC // 4, k0 + KC // 2, bank(5))
                    pe.wait_ge(pt_out, n + 1)
                    if n >= 1:
                        pe.wait_ge(o_out, n)
                    for j in range(KEYS // P):
                        ins = mmul(bank(4)[:, 0:VH], pT[:, n % 2, j * P:(j + 1) * P], vv[:, j, hd * VH:(hd + 1) * VH], start=(j == 0), stop=(j == KEYS // P - 1))
                    ins.then_inc(pv_ps, 1)
            pe.wait_ge(cv_done, CC)
            pe.wait_ge(ex, TT * HEADS)
            for ci in range(CC):
                ins = mmul(bank(0), one_over[:, :], cy[:, ci, :], start=(ci == 0), stop=(ci == CC - 1))
            ins.then_inc(mean_ps, 1)
            pe.wait_ge(o_out, TT * HEADS)
            for ci in range(CC):
                if ci >= 2:
                    pe.wait_ge(oT_out, ci - 1)
                for t in range(TT):
                    ins = nc.tensor.transpose(bank(2 + ci % 2)[:, t * P:(t + 1) * P], oo[:, t, ci:HEADS * VH:CC], ident[:, :])
                ins.then_inc(oT_ps, 1)
            for ci in range(CC):
                pe.wait_ge(dsq, ci + 1)
                ins = mmul(bank(1), one_over[:, :], csg[:, ci % 2, :], start=(ci == 0), stop=(ci == CC - 1))
                ins.then_inc(varc_ps, 1)

            def mix_out(l, left, n_chunks, wv, base):
                for n in range(2 * TT):
                    t, half = n // 2, n % 2
                    if n >= 2:
                        pe.wait_ge(y_g, 2 * TT * l + n - 1)
                    for k in range(n_chunks):
                        ins = mmul(bank(base + n % 2), left(k, t), wv[:, k, half * HB:(half + 1) * HB], start=(k == 0), stop=(k == n_chunks - 1))
                    ins.then_inc(y_ps, 1)

            pe.wait_ge(wo_in, 32)
            pe.wait_ge(ca_out, CC)
            pe.wait_ge(oT_out, CC)
            wo0v = wo0.rearrange("p b k n -> p (b k n)").rearrange("p (c n) -> p c n", n=D)
            mix_out(0, lambda k, t: catT[:, k // CC, k % CC, t * P:(t + 1) * P], 2 * CC, wo0v, 4)

            def experts(l):
                s = {k: v[l] for k, v in L.items()}
                pe.wait_ge(s["f_done"], at(l, "f_done", TT))
                for k in range(KC):
                    if k >= 2:
                        pe.wait_ge(s["fT_out"], at(l, "fT_out", k - 1))
                    for t in range(TT):
                        ins = nc.tensor.transpose(bank(k % 2)[:, t * P:(t + 1) * P], acc[:, t, k:D:KC], ident[:, :])
                    ins.then_inc(s["fT_ps"], 1)
                pe.wait_ge(s["rw_lo"], at(l, "rw_lo", 1))
                pe.wait_ge(s["fT_out"], at(l, "fT_out", KC))
                for t in range(TT):
                    for k in range(KC):
                        ins = split_mm(bank(0)[:, t * EXPERTS:(t + 1) * EXPERTS], fTh[:, k, t * P:(t + 1) * P], fTl[:, k, t * P:(t + 1) * P],
                                       rwh[:, k, :], rwl[:, k, :], k == 0, k == KC - 1)
                ins.then_inc(s["lg_ps"], 1)
                cn = Counts(pe, l)

                def gate_up(b, left, split, signal=None):
                    for u in range(2):
                        pe.wait_ge(s["w_gu"], split(u))
                        for k in range(KC // 2):
                            hi, lo = left(u * KC // 2 + k)
                            cols = lambda w: w[:, u, :].rearrange("p (j k n) -> p j k n", j=2, n=DE)[:, :, k, :]
                            ins = split_mm(bank(2 + b), hi, lo, cols(wh), cols(wl), u + k == 0, u == 1 and k == KC // 2 - 1)
                        ins.then_inc(s["gu" if u else "gu_h"], 1)

                def hidden_T(b, n):
                    pe.wait_ge(s["hm"], n)
                    for j in range(2):
                        ins = nc.tensor.transpose(bank(4 + b)[:, j * P:(j + 1) * P], hh[:, b, j:DE:2], ident[:, :])
                    ins.then_inc(s["hp"], 1)

                def down(b, n, split, behind=True):
                    pe.wait_ge(s["ho"], n)
                    pe.wait_ge(s["w_d"], split)
                    if behind:
                        pe.wait_ge(s["ye0"], n - 1)
                        pe.wait_ge(s["ye1"], n - 1)
                    for half in range(2):
                        for j in range(2):
                            cols = lambda w: w[:, 2, j * D + half * HB:j * D + (half + 1) * HB]
                            ins = split_mm(bank(6 + half), hTh[:, b, j, :], hTl[:, b, j, :], cols(wh), cols(wl), j == 0, j == 1)
                        ins.then_inc(s[f"yp{half}"], 1)

                tile_gu = lambda t: gate_up(t % 2, lambda k: (fTh[:, k, t * P:(t + 1) * P], fTl[:, k, t * P:(t + 1) * P]), cn.shared_split)

                def tile_down(t):
                    hidden_T(t % 2, cn.tile(t))
                    down(t % 2, cn.tile(t), cn.shared_split(2), behind=l > 0 or t > 0)

                tile_gu(0)
                tile_gu(1)
                pe.wait_ge(s["rk_in"], at(l, "rk_in", 1))
                for t in range(TT):
                    for q in range(t + 1):
                        ins = mmul(bank(1)[:, t * EXPERTS:(t + 1) * EXPERTS], before[:, :] if q == t else ones[:, :], mask[:, q, :], start=(q == 0), stop=(q == t))
                for q in range(TT):
                    ins = mmul(bank(0)[:, 0:EXPERTS], ones[:, :], mask[:, q, :], start=(q == 0), stop=(q == TT - 1))
                ins.then_inc(s["rk_ps"], 1)
                tile_down(0)
                tile_down(1)
                pe.wait_ge(s["places"], at(l, "places", 1))
                mmul(bank(1)[0:1, 256:256 + COLS], becol[0:COLS, :], ident[0:COLS, 0:COLS], start=True, stop=True).then_inc(s["be_ps"], 1)
                tile_gu(2)
                tile_gu(3)
                for n in range(TT * TOPK):
                    pe.wait_ge(s["hot"], at(l, "hot", 2 * (n + 1)))
                    mmul(bank(0)[:, 0:COLS], hot_s[:, n % 4, :], hot_b[:, n % 4, :], start=(n == 0), stop=(n == TT * TOPK - 1)).then_inc(s["hot_used"], 1)
                tile_down(2)
                tile_down(3)
                pe.wait_ge(s["tables"], at(l, "tables", 4))
                last = pe.value_load(last_loop_pair[0:1, 2 * l:2 * l + 1], min_val=10, max_val=MAXP - 2) + 1

                def rows_T(b, i):
                    pe.wait_ge(s[f"x_in{b}"], 16 * (i + cn.off + 1))
                    for g in range(2):
                        for k in range(KC // 2):
                            kk = g * KC // 2 + k
                            ins = nc.tensor.transpose(bank(g)[:, k * P:(k + 1) * P], xg[:, b, kk:D:KC], ident[:, :])
                        ins.then_inc(s["x_used" if g else "xp0"], 1)

                def step(b, i, first=False, last=False, last_pair=False):
                    if not first:
                        hidden_T(prior(b, i)[0], cn.block(*prior(b, i)))
                    pe.wait_ge(s["x_lo"], 2 * cn.n(b, i) + 2)
                    gate_up(b, lambda k: (xTh[:, b, k, :], xTl[:, b, k, :]), lambda u: cn.split(b, i, u))
                    if not last:
                        rows_T(*after(b, i))
                    if not first:
                        down(prior(b, i)[0], cn.block(*prior(b, i)), cn.split(*prior(b, i), 2))

                rows_T(0, 0)
                run_blocks(pe, last, step)
                hidden_T(1, cn.block(1, last))
                down(1, cn.block(1, last), cn.split(1, last, 2))

            experts(0)
            for k in range(KC):
                if k == 0:
                    pe.wait_ge(rn_done, TT + TC + TT)
                if k >= 2:
                    pe.wait_ge(t_out, 2 * KC + k - 1)
                for t in range(TT):
                    ins = nc.tensor.transpose(bank(k % 2)[:, t * P:(t + 1) * P], rn1[:, t, k:D:KC], ident[:, :])
                ins.then_inc(t_ps, 1)
            pe.wait_ge(t_out, 3 * KC)
            for ci in range(SCC):
                pe.wait_ge(w3_in[ci % 3], 48 * (ci // 3 + 1))
                if ci >= 2:
                    pe.wait_ge(o1_out, ci - 1)
                for j in (1, 2, 0):
                    for k in range(KC):
                        ins = mmul(bank(2 + 3 * (ci % 2) + j), w3[:, ci % 3, k, j, :], aT1[:, k, :], start=(k == 0), stop=(k == KC - 1))
                    ins.then_inc(u3_ps, 1)
            pe.wait_ge(wo_in, 48)
            pe.wait_ge(o1_out, SCC)
            wo1v = wo1.rearrange("p b k n -> p (b k n)").rearrange("p (c n) -> p c n", n=D)
            mix_out(1, lambda k, t: oT1[:, k, t * P:(t + 1) * P], SCC, wo1v, 0)
            experts(1)

        @block.scalar
        def _(act):
            act.wait_ge(c_in, 32)
            nc.scalar.activation(csil[:, :, :], ccol[:, :, :], ACT.Silu).then_inc(csil_ok, 1)

            def squares(src, n0, cols):
                for n, (row, junk) in enumerate(src):
                    nc.scalar.activation(junk, row, ACT.Square, accum_out=ssq[:, n0 + n:n0 + n + 1]).then_inc(sq_done, 1)

            act.wait_ge(x_in, 16)
            act.wait_ge(hc_in, 16)
            squares([(h[:, t, :], rn[:, t, :]) for t in range(TT)] + [(hc[:, t, :], rn[:, TT + t, :]) for t in range(TC)], 0, D)
            act.wait_ge(var_done, 1)
            nc.scalar.activation(rstd[:, 0:TT + TC], rstd[:, 0:TT + TC], ACT.Sqrt).then_inc(std_done, 1)

            def modulate_T(k0, ks, parts, dst, n0):
                for k in range(ks):
                    for part in range(parts):
                        n = n0 + parts * k + part
                        act.wait_ge(t_ps, n + 1)
                        if n == n0:
                            act.wait_ge(acol_in, 64 if n0 else 32)
                            act.wait_ge(ada_col, 2 if n0 else 1)
                        o = dst[:, k, NCTX:] if parts == 2 and part == 0 else (dst[:, k, 0:NCTX] if part else dst[:, k, :])
                        nc.scalar.activation(o, bank(n % 2)[:, 0:(NCTX if part else N)], ACT.Identity,
                                             scale=acol[:, 1, part, k:k + 1], bias=acol[:, 0, part, k:k + 1]).then_inc(t_out, 1)

            modulate_T(0, KC, 2, aT, 0)
            for t in range(TT + TC):
                act.wait_ge(lat_ps, t + 1)
                w = QL + KVL if t < TT else KVL
                nc.scalar.activation(cqs[:, t, QL + KVL - w:], bank(2 + t % 2)[:, 0:w], ACT.Copy).then_inc(lat_out, 1)
            act.wait_ge(lat_out, TT + TC)
            cyf = cy.rearrange("p c n -> p (c n)")
            for t in range(TT + TC):
                nc.scalar.activation(cyf[:, t * KVL:(t + 1) * KVL], cqs[:, t, QL:], ACT.Square, accum_out=ssq[:, 8 + TT + t:9 + TT + t]).then_inc(lat_sq, 1)
                if t < TT:
                    nc.scalar.activation(cyf[:, 768 + t * QL:768 + (t + 1) * QL], cqs[:, t, 0:QL], ACT.Square, accum_out=ssq[:, 8 + t:9 + t]).then_inc(lat_sq, 1)
            act.wait_ge(kr_ps, 2)
            nc.scalar.activation(krT[NOPE:NOPE + ROPE, 0:NCTX], bank(5)[NOPE:NOPE + ROPE, 0:NCTX], ACT.Copy).then_inc(krc_out, 1)
            act.wait_ge(lat_var, 1)
            nc.scalar.activation(rstd[:, 8:8 + 2 * TT + TC], rstd[:, 8:8 + 2 * TT + TC], ACT.Sqrt).then_inc(lat_std, 1)
            for ci in range(CC):
                act.wait_ge(wab_used, ci + 1)
                if ci >= 2:
                    act.wait_ge(v_out, ci - 1)
                nc.scalar.activation(csg[:, ci % 2, :], bank(7), ACT.Sigmoid).then_inc(sg_out, 1)
            act.wait_ge(q_const, 48)
            for j in range(2):
                act.wait_ge(latT_ps, j + 1)
                nc.scalar.activation(cqT[:, j, :], bank(j), ACT.Copy, scale=qnw[:, j:j + 1]).then_inc(latT_out, 1)
            act.wait_ge(latT_ps, 4)
            nc.scalar.activation(ckvT[:, 0:NCTX], bank(2)[:, 0:NCTX], ACT.Copy, scale=kvw[:, 0:1]).then_inc(latT_out, 1)
            nc.scalar.activation(ckvT[:, NCTX:], bank(3), ACT.Copy, scale=kvw[:, 0:1]).then_inc(latT_out, 1)
            for t in range(TT + TC):
                act.wait_ge(v_ps, t + 1)
                nc.scalar.activation(vv[:, t, :], bank(4 + t % 2), ACT.Copy).then_inc(vv_out, 1)
            for hd in range(HEADS):
                act.wait_ge(kn_ps, hd + 1)
                nc.scalar.activation(kT[0:NOPE, hd % 2, :], pp[3][0:NOPE, 0:KEYS], ACT.Copy).then_inc(kn_out, 1)
                act.wait_ge(q_ps, hd + 1)
                nc.scalar.activation(qT[0:NOPE, hd % 2, :], bank(5)[0:NOPE, :], ACT.Copy, scale=ATT_SCALE).then_inc(qn_out, 1)
                for t in range(TT):
                    n = hd * TT + t
                    act.wait_ge(mx, n + 1)
                    if n >= 2:
                        act.wait_ge(pt_ps, n - 1)
                    nc.scalar.activation(pe_[:, n % 2, :], pp[n % 2][:, 0:KEYS], ACT.Exp, bias=stat[:, n % 4, 0:1],
                                         accum_out=stat[:, n % 4, 1:2]).then_inc(ex, 1)
                    act.wait_ge(pt_ps, n + 1)
                    if n >= 2:
                        act.wait_ge(pv_ps, n - 1)
                    nc.scalar.activation(pT[:, n % 2, :], pp[3][:, 0:KEYS], ACT.Copy).then_inc(pt_out, 1)
            for ci in range(CC):
                act.wait_ge(oT_ps, ci + 1)
                nc.scalar.activation(catT[:, 1, ci, :], bank(2 + ci % 2), ACT.Copy).then_inc(oT_out, 1)
            for ci in range(CC):
                act.wait_ge(d_done, ci + 1)
                if ci >= 2:
                    act.wait_ge(varc_ps, ci - 1)
                nc.scalar.activation(csg[:, ci % 2, :], cy[:, ci, :], ACT.Square).then_inc(dsq, 1)
            act.wait_ge(cvar, 2)
            nc.scalar.activation(csg[:, 0, :], csg[:, 0, :], ACT.Sqrt).then_inc(cstd, 1)
            for ci in range(CC):
                act.wait_ge(dn, ci + 1)
                nc.scalar.activation(catT[:, 0, ci, :], cy[:, ci, :], ACT.Silu, scale=cvw[:, ci, TAPS + 1:TAPS + 2],
                                     bias=cvw[:, ci, TAPS + 2:TAPS + 3]).then_inc(ca_out, 1)

            def experts(l):
                s = {k: v[l] for k, v in L.items()}
                for t in range(TT):
                    act.wait_ge(h_new, 2 * (TT * l + t + 1))
                    nc.scalar.activation(yl[:, 0, t, :] if l else yl[:, 1, 2 + t, :], h[:, t, :], ACT.Square, accum_out=ssq[:, t:t + 1]).then_inc(sq_done, 1)
                act.wait_ge(var_done, 2 + 2 * l)
                nc.scalar.activation(rstd[:, 0:TT], rstd[:, 0:TT], ACT.Sqrt).then_inc(std_done, 1)
                act.wait_ge(s["rconst_in"], at(l, "rconst_in", 32))
                nc.scalar.activation(rwh[:, :, :], rw[:, :, :], ACT.Copy).then_inc(s["rw_hi"], 1)
                cn = Counts(act, l)

                def split(r, u, arrived, free):
                    act.wait_ge(s[f"w_in{r}"], arrived)
                    if free is not None:
                        act.wait_ge(s[("gu_h", "gu", "yp1")[u]], free)
                    for piece in range(2):
                        cols = slice(piece * UNIT // 2, (piece + 1) * UNIT // 2)
                        nc.scalar.activation(wh[:, u, cols], raw(r)[:, cols], ACT.Copy).then_inc(s["whd" if u == 2 else "whg"], 1)

                for u in range(3):
                    split(u, u, cn.shared_arrived(u), None)
                for k in range(KC):
                    act.wait_ge(s["fT_ps"], at(l, "fT_ps", k + 1))
                    nc.scalar.activation(fTh[:, k, :], bank(k % 2), ACT.Copy).then_inc(s["fT_hi"], 1)
                act.wait_ge(s["lg_ps"], at(l, "lg_ps", 1))
                nc.scalar.activation(score.rearrange("p t e -> p (t e)"), bank(0)[:, 0:TT * EXPERTS], ACT.Sigmoid).then_inc(s["sc_out"], 1)

                def silu(b, n):
                    act.wait_ge(s["gu"], n)
                    nc.scalar.activation(sg[:, b, :], bank(2 + b)[:, 0:DE], ACT.Silu).then_inc(s["s"], 1)

                def hidden_hi(b, n):
                    act.wait_ge(s["hp"], n)
                    nc.scalar.activation(hTh[:, b, :, :].rearrange("p j n -> p (j n)"), bank(4 + b)[:, 0:2 * P], ACT.Copy).then_inc(s["h_hi"], 1)

                for pr in range(TT // 2):
                    for b in range(2):
                        silu(b, cn.tile(2 * pr + b))
                    for b in range(2):
                        t = 2 * pr + b
                        hidden_hi(b, cn.tile(t))
                        act.wait_ge(s["yp0"], cn.tile(t))
                        if t == 0:
                            act.wait_ge(s["f_stored"], at(l, "f_stored", 16 * TT))
                        nc.scalar.activation(acc[:, t, 0:HB], bank(6), ACT.Copy).then_inc(s["ye0"], 1)
                act.wait_ge(s["tables"], at(l, "tables", 4))
                last = act.value_load(last_loop_pair[0:1, 2 * l:2 * l + 1], min_val=10, max_val=MAXP - 2) + 1

                def rows_hi(b, i):
                    for g in range(2):
                        act.wait_ge(s["x_used" if g else "xp0"], cn.n(b, i) + 1)
                        nc.scalar.activation(xTh[:, b, g * KC // 2:(g + 1) * KC // 2, :].rearrange("p k n -> p (k n)"), bank(g), ACT.Copy).then_inc(s["x_hi"], 1)

                def out_half(b, i):
                    if not (type(i) is int and i == 0):
                        act.wait_ge(s[f"yw{b}"], 16 * (i + cn.off))
                    act.wait_ge(s["yp0"], cn.block(b, i))
                    nc.scalar.activation(yo[:, b, 0:HB], bank(6), ACT.Copy).then_inc(s["ye0"], 1)

                def unit(b, i, u):
                    split(3 * b + u, u, cn.arrived(b, i, u), cn.block(b, i) - 1)

                def step(b, i, first=False, last=False, last_pair=False):
                    if not first:
                        hidden_hi(prior(b, i)[0], cn.block(*prior(b, i)))
                    if not last:
                        unit(*after(b, i), 0)
                        rows_hi(*after(b, i))
                    silu(b, cn.block(b, i))
                    if not last:
                        unit(*after(b, i), 1)
                    if not first:
                        out_half(*prior(b, i))
                    unit(b, i, 2)

                rows_hi(0, 0)
                for u in range(2):
                    unit(0, 0, u)
                run_blocks(act, last, step)
                hidden_hi(1, cn.block(1, last))
                out_half(1, last)

            experts(0)
            for t in range(TT):
                act.wait_ge(L["hfin"][0], TT)
                nc.scalar.activation(rn1[:, t, :], h[:, t, :], ACT.Square, accum_out=ssq[:, t:t + 1]).then_inc(sq_done, 1)
            act.wait_ge(var_done, 3)
            nc.scalar.activation(rstd[:, 0:TT], rstd[:, 0:TT], ACT.Sqrt).then_inc(std_done, 1)
            modulate_T(0, KC, 1, aT1, 2 * KC)
            for ci in range(SCC):
                act.wait_ge(u3_ps, 3 * ci + 1)
                if ci >= 2:
                    act.wait_ge(z_out, ci - 1)
                nc.scalar.activation(cgs[:, ci % 2, :], bank(2 + 3 * (ci % 2) + 1), ACT.Copy).then_inc(cg_out, 1)
            experts(1)
            for t in range(TT):
                act.wait_ge(L["hfin"][1], 2 * TT)
                nc.scalar.activation(acc[:, t, :], h[:, t, :], ACT.Square, accum_out=ssq[:, t:t + 1]).then_inc(sq_done, 1)
            act.wait_ge(var_done, 5)
            nc.scalar.activation(rstd[:, 0:TT], rstd[:, 0:TT], ACT.Sqrt).then_inc(std_done, 1)

        @block.vector
        def _(dve):
            chain, steps = sem("dve_step"), [0]

            def mark(ins):
                steps[0] += 1
                ins.then_inc(chain, 1)

            def link(ins):
                mark(ins)
                dve.wait_ge(chain, steps[0])

            V = nc.vector

            def stats(n0, n1, width, squares, done):
                if squares:
                    dve.wait_ge(sq_done, squares)
                link(V.tensor_scalar(rstd[:, n0:n1], ssq[:, n0:n1], 1.0 / width, EPS, ALU.mult, ALU.add))
                V.reciprocal(rstd[:, n0:n1], rstd[:, n0:n1]).then_inc(done, 1)

            def ada_row_of(m, src):
                dve.wait_ge(ada_ps, m + 1)
                if m >= 2:
                    dve.wait_ge(mod_st[m % 2], 16 * (m // 2))
                V.tensor_tensor(mrow[:, m % 2, :], src[0:2, :], adab[:, m % 2, :], ALU.add).then_inc(ada_row, 1)

            def column_gains(l):
                dve.wait_ge(q_const, 48)
                dve.wait_ge(acol_in, 32 * (l + 1))
                for r in range(2):
                    ins = V.scalar_tensor_tensor(acol[:, SC1, r, :], acol[:, SC1, r, :], 1.0, nwcol[:, l, :], ALU.add, ALU.mult)
                ins.then_inc(ada_col, 1)

            stats(0, TT + TC, D, TT + TC, var_done)
            dve.wait_ge(std_done, 1)
            for t in range(TT + TC):
                V.tensor_scalar(rn[:, t, :], h[:, t, :] if t < TT else hc[:, t - TT, :], rstd[:, t:t + 1], None, ALU.mult).then_inc(rn_done, 1)
            dve.wait_ge(cw_ps, 1)
            V.tensor_copy(cvw[:, :, :], bank(6)[:, 0:CC * 40].rearrange("p (c n) -> p c n", n=40)[:, :, 0:TAPS + 3]).then_inc(cw_out, 1)
            V.tensor_copy(odw[:, :, :], bank(6)[:, 256:256 + SCC * 4].rearrange("p (c n) -> p c n", n=4)[:, :, 0:3]).then_inc(cw_out, 1)
            for m in range(FIRST):
                ada_row_of(m, bank(m % 2))
            column_gains(0)

            dve.wait_ge(lat_sq, 2 * TT + TC)
            q0, k0 = 8, 8 + TT
            mark(V.tensor_scalar(rstd[:, q0:k0], ssq[:, q0:k0], 1.0 / QL, EPS, ALU.mult, ALU.add))
            link(V.tensor_scalar(rstd[:, k0:k0 + TT + TC], ssq[:, k0:k0 + TT + TC], 1.0 / KVL, EPS, ALU.mult, ALU.add))
            V.reciprocal(rstd[:, q0:k0 + TT + TC], rstd[:, q0:k0 + TT + TC]).then_inc(lat_var, 1)
            dve.wait_ge(lat_std, 1)
            for t in range(TT + TC):
                V.tensor_scalar(cqs[:, t, QL:], cqs[:, t, QL:], rstd[:, k0 + t:k0 + t + 1], None, ALU.mult).then_inc(lat_n, 1)
                if t < TT:
                    V.tensor_scalar(cqs[:, t, 0:QL], cqs[:, t, 0:QL], rstd[:, q0 + t:q0 + t + 1], None, ALU.mult).then_inc(lat_n, 1)
            dve.wait_ge(kr_ps, 2)
            R0, R1, R2 = NOPE, NOPE + ROPE, NOPE + 2 * ROPE
            mark(V.tensor_tensor(rt[R0:R1, 0, :], bank(4)[R0:R1, :], rope[R0:R1, :], ALU.mult))
            link(V.tensor_tensor(rt[R0:R1, 1, :], bank(4)[R1:R2, :], rope[R1:R2, :], ALU.mult))
            V.tensor_tensor(krT[R0:R1, NCTX:], rt[R0:R1, 0, :], rt[R0:R1, 1, :], ALU.add).then_inc(kr_out, 1)
            dve.wait_ge(pool_set, 6)
            for ci in range(CC):
                dve.wait_ge(sg_out, ci + 1)
                V.tensor_tensor(vpad[:, ci, PAD:PAD + N], bank(6), csg[:, ci % 2, :], ALU.mult).then_inc(v_out, 1)
            for m in range(FIRST, FIRST + MID):
                ada_row_of(m, bank(4 + m % 2))

            def conv_steps():
                for ci in range(CC):
                    dve.wait_ge(v_out, ci + 1)
                    link(V.tensor_scalar(cy[:, ci, :], vpad[:, ci, 0:N], cvw[:, ci, 0:1], cvw[:, ci, TAPS:TAPS + 1], ALU.mult, ALU.add))
                    yield
                    for tap in range(1, TAPS):
                        ins = V.scalar_tensor_tensor(cy[:, ci, :], vpad[:, ci, tap:tap + N], cvw[:, ci, tap:tap + 1], cy[:, ci, :], ALU.mult, ALU.add)
                        if tap < TAPS - 1:
                            link(ins)
                        else:
                            ins.then_inc(cv_done, 1)
                        yield

            conv = conv_steps()
            for hd in range(HEADS):
                dve.wait_ge(q_ps, hd + 1)
                mark(V.scalar_tensor_tensor(rt[R0:R1, 0, :], bank(5)[R0:R1, :], ATT_SCALE, rope[R0:R1, :], ALU.mult, ALU.mult))
                link(V.scalar_tensor_tensor(rt[R0:R1, 1, :], bank(5)[R1:R2, :], ATT_SCALE, rope[R1:R2, :], ALU.mult, ALU.mult))
                V.tensor_tensor(qT[R0:R1, hd % 2, :], rt[R0:R1, 0, :], rt[R0:R1, 1, :], ALU.add).then_inc(qr_out, 1)

                def head_max(t):
                    n = hd * TT + t
                    dve.wait_ge(s_ps, n + 1)
                    V.tensor_reduce(stat[:, n % 4, 0:1], pp[n % 2][:, 0:KEYS], AX.X, ALU.max, negate=True).then_inc(mx, 1)

                head_max(0)
                for t in range(TT):
                    n = hd * TT + t
                    if t + 1 < TT:
                        head_max(t + 1)
                    for _ in range(4):
                        next(conv, None)
                    dve.wait_ge(ex, n + 1)
                    link(V.reciprocal(stat[:, n % 4, 2:3], stat[:, n % 4, 1:2]))
                    if n % 2:
                        ada_row_of(FIRST + MID + n // 2, bank(5))
                    dve.wait_ge(pv_ps, n + 1)
                    V.tensor_scalar(oo[:, t, hd * VH:(hd + 1) * VH], bank(4)[:, 0:VH], stat[:, n % 4, 2:3], None, ALU.mult).then_inc(o_out, 1)
            for _ in conv:
                pass
            dve.wait_ge(mean_ps, 1)
            dve.wait_ge(cv_done, CC)
            for ci in range(CC):
                V.tensor_tensor(cy[:, ci, :], cy[:, ci, :], bank(0), ALU.subtract).then_inc(d_done, 1)
            dve.wait_ge(varc_ps, CC)
            V.tensor_scalar(csg[:, 0, :], bank(1), EPS, None, ALU.add).then_inc(cvar, 1)
            dve.wait_ge(cvar, 1)
            V.reciprocal(csg[:, 0, :], csg[:, 0, :]).then_inc(cvar, 1)
            dve.wait_ge(cstd, 1)
            dve.wait_ge(d_done, CC)
            for ci in range(CC):
                V.tensor_tensor(cy[:, ci, :], cy[:, ci, :], csg[:, 0, :], ALU.mult).then_inc(dn, 1)

            def residual(l, tmp, base):
                dve.wait_ge(g1_in, 16 * (l + 1))
                for n in range(2 * TT):
                    t, cols = n // 2, slice(n % 2 * HB, (n % 2 + 1) * HB)
                    dve.wait_ge(y_ps, 2 * TT * l + n + 1)
                    V.tensor_tensor(tmp[:, n % 2, :], bank(base + n % 2), g1b[:, cols], ALU.mult).then_inc(y_g, 1)
                    dve.wait_ge(y_g, 2 * TT * l + n + 1)
                    V.tensor_tensor(h[:, t, cols], h[:, t, cols], tmp[:, n % 2, :], ALU.add).then_inc(h_new, 1)

            residual(0, rt, 4)

            def bc(ap, shape):
                return ap.to_broadcast(shape)

            def experts(l):
                s = {k: v[l] for k, v in L.items()}
                dve.wait_ge(ab_in, 48 * (l + 1))
                link(V.scalar_tensor_tensor(a2b[:, :], a2b[:, :], 1.0, nrow[:, :], ALU.add, ALU.mult))
                stats(0, TT, D, TT + TC + TT + 2 * TT * l, var_done)
                dve.wait_ge(std_done, 2 + 2 * l)
                dve.wait_ge(h_new, 2 * TT * (l + 1))
                for t in range(TT):
                    link(V.scalar_tensor_tensor(acc[:, t, :], h[:, t, :], rstd[:, t:t + 1], a2b[:, :], ALU.mult, ALU.mult))
                    V.tensor_tensor(acc[:, t, :], acc[:, t, :], b2b[:, :], ALU.add).then_inc(s["f_done"], 1)
                dve.wait_ge(s["rw_hi"], at(l, "rw_hi", 1))
                V.tensor_tensor(rwl[:, :, :], rw[:, :, :], rwh[:, :, :].bitcast(f32), ALU.subtract).then_inc(s["rw_lo"], 1)
                cn = Counts(dve, l)

                def split(r, u, seen):
                    for piece in range(2):
                        cols = slice(piece * UNIT // 2, (piece + 1) * UNIT // 2)
                        dve.wait_ge(s["whd" if u == 2 else "whg"], seen + piece + 1)
                        ins = V.tensor_tensor(wl[:, u, cols], raw(r)[:, cols], wh[:, u, cols].bitcast(f32), ALU.subtract)
                    ins.then_inc(s["w_d" if u == 2 else "w_gu"], 1)

                for k in range(KC):
                    dve.wait_ge(s["fT_hi"], at(l, "fT_hi", k + 1))
                    V.tensor_tensor(fTl[:, k, :], bank(k % 2), fTh[:, k, :].bitcast(f32), ALU.subtract).then_inc(s["fT_out"], 1)
                for u in range(3):
                    split(u, u, 2 * cn.shared_split(u) - 2)

                def hidden(b, n):
                    dve.wait_ge(s["s"], n)
                    V.tensor_tensor(hh[:, b, :], bank(2 + b)[:, DE:2 * DE], sg[:, b, :], ALU.mult).then_inc(s["hm"], 1)

                def hidden_lo(b, n):
                    dve.wait_ge(s["h_hi"], n)
                    V.tensor_tensor(hTl[:, b, :, :].rearrange("p j n -> p (j n)"), bank(4 + b)[:, 0:2 * P],
                                    hTh[:, b, :, :].rearrange("p j n -> p (j n)").bitcast(f32), ALU.subtract).then_inc(s["ho"], 1)

                def shared_out(t):
                    hidden_lo(t % 2, cn.tile(t))
                    dve.wait_ge(s["yp1"], cn.tile(t))
                    if t == 0:
                        dve.wait_ge(s["f_stored"], at(l, "f_stored", 16 * TT))
                    V.tensor_copy(acc[:, t, HB:], bank(7)).then_inc(s["ye1"], 1)

                dve.wait_ge(s["rconst_in"], at(l, "rconst_in", 32))
                dve.wait_ge(s["sc_out"], at(l, "sc_out", 1))
                link(V.tensor_tensor(sel[:, :, :], score[:, :, :], bc(rbias[:, :].unsqueeze(1), [P, TT, EXPERTS]), ALU.add))
                for t in range(TT):
                    for g in range(GROUPS):
                        ins = V.max(out=g8[:, t, g, :], in_=sel[:, t, g * GE:(g + 1) * GE])
                link(ins)
                link(V.tensor_tensor(gsum[:, :, :], g8[:, :, :, 0], g8[:, :, :, 1], ALU.add))
                for t in range(TT):
                    ins = V.max(out=top8[:, t, :], in_=gsum[:, t, :])
                link(ins)
                for t in range(TT):
                    ins = V.max_index(out=idx8[:, t, :], in_max=top8[:, t, :], in_values=gsum[:, t, :])
                link(ins)
                link(V.tensor_copy(idxf[:, :, :], idx8[:, :, :]))
                link(V.tensor_tensor(geq[:, :, :, :], bc(iota_row[:, 0:GROUPS].unsqueeze(1).unsqueeze(3), [P, TT, GROUPS, TOPG]),
                                     bc(idxf[:, :, 0:TOPG].unsqueeze(2), [P, TT, GROUPS, TOPG]), ALU.is_equal))
                link(V.tensor_reduce(gmask[:, :, :], geq[:, :, :, :], AX.X, ALU.add))
                link(V.tensor_scalar(gmask[:, :, :], gmask[:, :, :], -1.0, 3.0e38, ALU.add, ALU.mult))
                sel4 = sel.rearrange("p t (g e) -> p (t g) e", e=GE)
                link(V.tensor_tensor(sel4, sel4, bc(gmask.rearrange("p t g -> p (t g)").unsqueeze(2), [P, TT * GROUPS, GE]), ALU.add))
                for t in range(TT):
                    ins = V.max(out=top8[:, t, :], in_=sel[:, t, :])
                link(ins)
                for t in range(TT):
                    ins = V.max_index(out=idx8[:, t, :], in_max=top8[:, t, :], in_values=sel[:, t, :])
                link(ins)
                link(V.tensor_copy(idxf[:, :, :], idx8[:, :, :]))
                full = [P, TT, TOPK, EXPERTS]
                for t in range(TT):
                    ins = V.tensor_tensor(eq[:, t, :, :], bc(iota_row[:, 0:EXPERTS].unsqueeze(1), full[:1] + full[2:]),
                                          bc(idxf[:, t, 0:TOPK].unsqueeze(2), full[:1] + full[2:]), ALU.is_equal)
                link(ins)
                for t in range(TT):
                    ins = V.tensor_reduce(mask[:, t, :], eq[:, t, :, :].rearrange("p k e -> p e k"), AX.X, ALU.add)
                ins.then_inc(s["rk_in"], 1)
                hidden(0, cn.tile(0))
                hidden(1, cn.tile(1))
                dve.wait_ge(s["rk_ps"], at(l, "rk_ps", 1))
                cnt = bank(0)[:, 0:EXPERTS]
                link(V.tensor_copy(pend[:, :], cnt))
                link(V.tensor_scalar(nblk[:, :], pend[:, :], 0.0, None, ALU.is_gt))
                for q in range(1, TT):
                    link(V.scalar_tensor_tensor(nblk[:, :], pend[:, :], float(q * P), nblk[:, :], ALU.is_gt, ALU.add))
                link(V.tensor_tensor_scan(pend[:, :], ones[:, 0:EXPERTS], nblk[:, :], 0.0, ALU.mult, ALU.add))
                link(V.tensor_scalar(junk_e[:, :], pend[:, :], iota_part[:, 0:1], None, ALU.is_le, ALU.add, accum_out=becol[:, :]))
                V.tensor_tensor(bst[:, :], pend[:, :], nblk[:, :], ALU.subtract).then_inc(s["rt"], 1)
                dve.wait_ge(s["rt"], at(l, "rt", 1))
                link(V.tensor_scalar(bst[:, :], bst[:, :], float(P), None, ALU.mult))
                V.tensor_tensor(sel[:, :, :], bank(1)[:, 0:TT * EXPERTS].rearrange("p (t e) -> p t e", e=EXPERTS),
                                bc(bst[:, :].unsqueeze(1), [P, TT, EXPERTS]), ALU.add).then_inc(s["places"], 1)
                dve.wait_ge(s["places"], at(l, "places", 1))
                for t in range(TT):
                    ins = V.tensor_tensor(eqw[:, t, :, :], eq[:, t, :, :], bc(sel[:, t, :].unsqueeze(1), full[:1] + full[2:]), ALU.mult)
                link(ins)
                link(V.tensor_reduce(code[:, :].rearrange("p (t k) -> p t k", k=TOPK), eqw[:, :, :, :], AX.X, ALU.add))
                link(V.tensor_copy(codei[:, 0, :], code[:, :]))
                link(V.tensor_scalar(codei[:, 1, :], codei[:, 0, :], P - 1, None, ALU.bitwise_and))
                link(V.tensor_copy(slotf[:, :], codei[:, 1, :]))
                link(V.tensor_scalar(codei[:, 1, :], codei[:, 0, :], 7, None, ALU.logical_shift_right))
                link(V.tensor_copy(blkf[:, :], codei[:, 1, :]))
                shared_out(0)
                shared_out(1)
                hidden(0, cn.tile(2))
                hidden(1, cn.tile(3))
                for t in range(TT):
                    ins = V.tensor_tensor(eqw[:, t, :, :], eq[:, t, :, :], bc(score[:, t, :].unsqueeze(1), full[:1] + full[2:]), ALU.mult)
                link(ins)
                link(V.tensor_reduce(wts[:, :, :], eqw[:, :, :, :], AX.X, ALU.add))
                link(V.tensor_reduce(wsum[:, :], wts[:, :, :], AX.X, ALU.add))
                link(V.reciprocal(wsum[:, :], wsum[:, :]))
                link(V.tensor_scalar(wsum[:, :], wsum[:, :], ROUTED_SCALE, None, ALU.mult))
                link(V.tensor_tensor(wts[:, :, :], wts[:, :, :], bc(wsum[:, :].unsqueeze(2), [P, TT, TOPK]), ALU.mult))
                for n in range(TT * TOPK):
                    if n >= 4:
                        dve.wait_ge(s["hot_used"], at(l, "hot_used", n - 3))
                    t, k = n // TOPK, n % TOPK
                    V.tensor_scalar(hot_s[:, n % 4, :], iota_row[:, :], slotf[:, n:n + 1], None, ALU.is_equal).then_inc(s["hot"], 1)
                    V.tensor_scalar(hot_b[:, n % 4, :], iota_row[:, 0:COLS], blkf[:, n:n + 1], pair_val[:, t, k:k + 1], ALU.is_equal, ALU.mult).then_inc(s["hot"], 1)
                dve.wait_ge(s["be_ps"], at(l, "be_ps", 1))
                V.tensor_scalar(etab[:, :], bank(1)[0:1, 256:256 + COLS], float(EXPERTS - 1), None, ALU.min).then_inc(s["tables"], 1)
                link(V.tensor_scalar(last_loop_pair[:, 2 * l + 1:2 * l + 2], pend[0:1, EXPERTS - 1:EXPERTS], -3.0, None, ALU.add))
                V.tensor_scalar(last_loop_pair[:, 2 * l:2 * l + 1], last_loop_pair[:, 2 * l + 1:2 * l + 2], 1, None, ALU.logical_shift_right).then_inc(s["tables"], 1)
                dve.wait_ge(s["hot_used"], at(l, "hot_used", TT * TOPK))
                V.tensor_scalar(vtab[:, :], bank(0)[:, 0:COLS], float(EMPTY), None, ALU.add).then_inc(s["tables"], 1)
                dve.wait_ge(s["tables"], at(l, "tables", 3))
                V.tensor_scalar(ttab[:, :], vtab[:, :], 3, None, ALU.logical_shift_right).then_inc(s["tables"], 1)

                shared_out(2)
                shared_out(3)
                dve.wait_ge(s["tables"], at(l, "tables", 4))
                last = dve.value_load(last_loop_pair[0:1, 2 * l:2 * l + 1], min_val=10, max_val=MAXP - 2) + 1

                def rows_lo(b, i):
                    for g in range(2):
                        dve.wait_ge(s["x_hi"], 2 * cn.n(b, i) + g + 1)
                        part = slice(g * KC // 2, (g + 1) * KC // 2)
                        V.tensor_tensor(xTl[:, b, part, :].rearrange("p k n -> p (k n)"), bank(g),
                                        xTh[:, b, part, :].rearrange("p k n -> p (k n)").bitcast(f32), ALU.subtract).then_inc(s["x_lo"], 1)

                def out_half(b, i):
                    if not (type(i) is int and i == 0):
                        dve.wait_ge(s[f"yw{b}"], 16 * (i + cn.off))
                    dve.wait_ge(s["yp1"], cn.block(b, i))
                    V.tensor_copy(yo[:, b, HB:], bank(7)).then_inc(s["ye1"], 1)

                def unit(b, i, u):
                    split(3 * b + u, u, 2 * cn.split(b, i, u) - 2)

                def step(b, i, first=False, last=False, last_pair=False):
                    if not first:
                        hidden_lo(prior(b, i)[0], cn.block(*prior(b, i)))
                    if not last:
                        unit(*after(b, i), 0)
                        rows_lo(*after(b, i))
                    hidden(b, cn.block(b, i))
                    if not last:
                        unit(*after(b, i), 1)
                    if not first:
                        out_half(*prior(b, i))
                    unit(b, i, 2)

                rows_lo(0, 0)
                for u in range(2):
                    unit(0, 0, u)
                run_blocks(dve, last, step)
                hidden_lo(1, cn.block(1, last))
                out_half(1, last)
                dve.wait_ge(s["ye0"], cn.tile(TT - 1))
                for t in range(TT):
                    dve.wait_ge(s[f"yl_in{t % 2}"], at(l, f"yl_in{t % 2}", 16 * (t // 2 + 1)))
                    for k in range(TOPK):
                        V.scalar_tensor_tensor(acc[:, t, :], yl[:, t % 2, k, :], wts[:, t, k:k + 1], acc[:, t, :], ALU.mult, ALU.add).then_inc(s["comb"], 1)
                        dve.wait_ge(s["comb"], at(l, "comb", TOPK * t + k + 1))
                    if t == 0:
                        dve.wait_ge(g2_in, 16 * (l + 1))
                    link(V.tensor_tensor(acc[:, t, :], acc[:, t, :], g2b[:, :], ALU.mult))
                    V.tensor_tensor(h[:, t, :], h[:, t, :], acc[:, t, :], ALU.add).then_inc(s["hfin"], 1)

            experts(0)
            stats(0, TT, D, 3 * TT + TC, var_done)
            dve.wait_ge(std_done, 3)
            for t in range(TT):
                V.tensor_scalar(rn1[:, t, :], h[:, t, :], rstd[:, t:t + 1], None, ALU.mult).then_inc(rn_done, 1)
            column_gains(1)
            link(V.memset(zz[:, :, :], 0.0))
            for ci in range(SCC):
                b = ci % 2
                dve.wait_ge(cg_out, ci + 1)
                dve.wait_ge(u3_ps, 3 * ci + 2)
                V.tensor_tensor(zz[:, b, 1:N + 1], bank(2 + 3 * b + 2), cgs[:, b, :], ALU.mult).then_inc(z_out, 1)
                dve.wait_ge(z_out, ci + 1)
                link(V.tensor_scalar(zt[:, b, :], zz[:, b, 0:N], odw[:, ci, 0:1], None, ALU.mult))
                for tap in (1, 2):
                    link(V.scalar_tensor_tensor(zt[:, b, :], zz[:, b, tap:tap + N], odw[:, ci, tap:tap + 1], zt[:, b, :], ALU.mult, ALU.add))
                dve.wait_ge(u3_ps, 3 * ci + 3)
                V.tensor_tensor(oT1[:, ci, :], bank(2 + 3 * b), zt[:, b, :], ALU.mult).then_inc(o1_out, 1)
            residual(1, zt, 0)
            experts(1)
            stats(0, TT, D, 5 * TT + TC, var_done)
            dve.wait_ge(std_done, 5)
            dve.wait_ge(fw_in, 16)
            for t in range(TT):
                V.scalar_tensor_tensor(h[:, t, :], h[:, t, :], rstd[:, t:t + 1], b2b[:, :], ALU.mult, ALU.mult).then_inc(fin_o, 1)


NAMES = ["x", "c", "ctx", "c_ctx", "ada_w", "ada_b", "norm_mix_w", "norm_ffn_w", "ev_w_in", "ev_conv_w", "ev_conv_b", "ev_ln_w",
         "ev_ln_b", "ev_q_norm_w", "ev_kv_norm_w", "ev_w_uq", "ev_w_ukv", "ev_w_out", "od_w_in", "od_conv_w", "od_w_out",
         "router_w", "router_bias", "exp_w_gate", "exp_w_up", "exp_w_down", "sh_w_gate", "sh_w_up", "sh_w_down", "final_norm_w"]
GRID_W, ROPE_BASE = 64, 10000.0


def constants():
    half = ROPE // 2
    inv = (1.0 / (np.float32(ROPE_BASE) ** (np.arange(0, half, 2, dtype=np.float32) / np.float32(half)))).astype(np.float32)
    n = np.arange(N)
    pos = np.stack([n // GRID_W, n % GRID_W]).astype(np.float32)
    ang = (pos[:, None, :] * inv[None, :, None]).astype(np.float32)
    cos, sin = np.cos(ang), np.sin(ang)
    rope = np.zeros((P, N), np.float32)
    rope[NOPE:NOPE + ROPE] = np.stack([cos, cos], 1).reshape(ROPE, N)
    rope[NOPE + ROPE:] = np.stack([-sin, sin], 1).reshape(ROPE, N)
    return {"k_ident": np.eye(P, dtype=np.float32), "k_before": np.triu(np.ones((P, P), np.float32), 1),
            "k_rope": rope}


def kernel(**inputs):
    import concourse.bacc as bacc
    from concourse.bass_utils import run_bass_kernel_spmd

    nc = bacc.Bacc("TRN2", target_bir_lowering=False, num_devices=1)
    arrays = {name: np.ascontiguousarray(inputs[name]) for name in NAMES}
    arrays.update(constants())
    aps = {name: nc.dram_tensor(f"in_{name}", v.shape, mybir.dt.from_np(v.dtype), kind="ExternalInput").ap() for name, v in arrays.items()}
    out = nc.dram_tensor("out", (1, N, D), mybir.dt.float32, kind="ExternalOutput").ap()
    scratch = [[nc.dram_tensor(f"{name}{l}", shape, mybir.dt.float32, kind="Internal").ap() for l in range(DEPTH)]
               for name, shape in (("rows_for_experts", (N, D)), ("rows_of_experts", (N * 8, D)), ("modulation", (2, 6 * D)))]
    build(nc, aps, out, scratch)
    result = run_bass_kernel_spmd(nc, [{f"in_{name}": v for name, v in arrays.items()}], core_ids=[0])
    return result.results[0]["out"]
```

```python
import concourse.bass as bass
from concourse import mybir
from contextlib import ExitStack
import numpy as np

P = 128
D = 1024
N = 512
NCTX = 256
KEYS = NCTX + N
KC = D // P
TT, TC = N // P, NCTX // P
CONV, TAPS = 512, 31
PAD = TAPS // 2
CC = CONV // P
HEADS, NOPE, ROPE, VH = 8, 64, 32, 64
QL, KVL = 256, 128
LAT = QL + KVL + ROPE
EXPERTS, TOPK, GROUPS, TOPG = 64, 6, 8, 4
GE = EXPERTS // GROUPS
DE = 256
ROUTED_SCALE = 2.5
EPS = 1e-6
ATT_SCALE = float(NOPE + ROPE) ** -0.5
SC = 1024
SCC = SC // P
MAXB = (N * TOPK + EXPERTS * (P - 1)) // P
MAXP = (MAXB + 1) // 2
COLS = 2 * MAXP + 4
EMPTY = 65536
HB = 512
DEPTH = 2
UNIT = KC // 2 * 2 * DE


def build(nc, a, out, scratch):
    f32, f32r, i32, u32 = mybir.dt.float32, mybir.dt.float32r, mybir.dt.int32, mybir.dt.uint32
    ALU, ACT, AX = mybir.AluOpType, mybir.ActivationFunctionType, mybir.AxisListType
    F_dram, Y_dram, M_dram = scratch
    x, c, ctx_in, c_ctx = a["x"], a["c"], a["ctx"], a["c_ctx"]

    stack = ExitStack()
    with stack:
        sem = lambda name: stack.enter_context(nc.semaphore(name))
        both = lambda name: [sem(f"{name}_{b}") for b in range(2)]
        keep = lambda name, shape, dt=f32: stack.enter_context(nc.sbuf_tensor(name, shape, dt))

        h = keep("h", [P, TT, D])
        ident = keep("ident", [P, P])
        ones = keep("ones", [P, P])
        before = keep("before", [P, P])
        iota_row = keep("iota_row", [P, P])
        iota_part = keep("iota_part", [P, 1])
        pair_val = keep("pair_val", [P, TT, 8])
        one_over = keep("one_over", [P, P])
        ccol = keep("ccol", [P, 2, KC])
        csil = keep("csil", [P, 2, KC])
        acol = keep("acol", [P, 2, 2, KC])
        nwcol = keep("nwcol", [P, DEPTH, KC])
        g1b = keep("g1b", [P, D])
        g2b = keep("g2b", [P, D])
        a2b = keep("a2b", [P, D])
        b2b = keep("b2b", [P, D])
        def region():
            return ExitStack()

        rr = region()
        mr = lambda name, shape, dt=f32: rr.enter_context(nc.sbuf_tensor(name, shape, dt))
        score = mr("score", [P, TT, EXPERTS])
        sel = mr("sel", [P, TT, EXPERTS])
        g8 = mr("g8", [P, TT, GROUPS, 8])
        gsum = mr("gsum", [P, TT, GROUPS])
        top8 = mr("top8", [P, TT, 8])
        idx8 = mr("idx8", [P, TT, 8], u32)
        idxf = mr("idxf", [P, TT, 8])
        geq = mr("geq", [P, TT, GROUPS, TOPG])
        gmask = mr("gmask", [P, TT, GROUPS])
        wsum = mr("wsum", [P, TT])
        mask = mr("mask", [P, TT, EXPERTS])
        rbias = mr("rbias", [P, EXPERTS])
        nblk = mr("nblk", [P, EXPERTS])
        pend = mr("pend", [P, EXPERTS])
        bst = mr("bst", [P, EXPERTS])
        code = mr("code", [P, TT * TOPK])
        codei = mr("codei", [P, 2, TT * TOPK], i32)
        slotf = mr("slotf", [P, TT * TOPK])
        blkf = mr("blkf", [P, TT * TOPK])
        below_e = mr("below_e", [P, EXPERTS])
        eq = mr("eq", [P, TT, TOPK, EXPERTS])
        eqs = mr("eqs", [P, TOPK, EXPERTS])
        rr.close()
        nrow = keep("nrow", [P, D])
        mrow = keep("mrow", [2, 2, HB])
        adab = keep("adab", [2, 2, HB])
        rt = keep("rt", [P, 2, HB])
        adaw = keep("adaw", [P, 2, KC, HB])
        last_loop_pair = keep("last_loop_pair", [1, 2 * DEPTH], i32)
        ssq = keep("ssq", [P, 24])
        rstd = keep("rstd", [P, 24])
        rope = keep("rope", [P, N])
        cvw = keep("cvw", [P, CC, TAPS + 3])
        odw = keep("odw", [P, SCC, 3])
        qnw = keep("qnw", [P, 2])
        kvw = keep("kvw", [P, 1])

        r0 = region()
        m0 = lambda name, shape, dt=f32: r0.enter_context(nc.sbuf_tensor(name, shape, dt))
        aT = m0("aT", [P, KC, KEYS])
        wlat = m0("wlat", [P, KC, LAT + ROPE])
        wab = m0("wab", [P, 2, KC, 2, P])
        vv = wab.rearrange("p b k j n -> p (b k j n)")[:, 0:(TT + TC) * HEADS * VH].rearrange("p (t n) -> p t n", n=HEADS * VH)
        wuq = m0("wuq", [P, 2, HEADS, P])
        wukv = m0("wukv", [P, HEADS, NOPE + VH])
        r0e = region()
        m0e = lambda name, shape, dt=f32: r0e.enter_context(nc.sbuf_tensor(name, shape, dt))
        r0l = region()
        m0l = lambda name, shape, dt=f32: r0l.enter_context(nc.sbuf_tensor(name, shape, dt))
        crow = m0e("crow", [TAPS + 3, CONV])
        orow = m0e("orow", [3, D])
        rn = m0e("rn", [P, TT + TC, D])
        hc = m0e("hc", [P, TC, D])
        r0e.close()
        pe_ = m0l("pe_", [P, 2, KEYS])
        pT = m0l("pT", [P, 2, KEYS])
        kT = m0l("kT", [P, 2, KEYS])
        qT = m0l("qT", [P, 2, N])
        vpad = m0l("vpad", [P, CC, N + 2 * PAD])
        cy = m0l("cy", [P, CC, N])
        csg = m0l("csg", [P, 2, N])
        cqT = m0l("cqT", [P, 2, N])
        ckvT = m0l("ckvT", [P, KEYS])
        krT = m0l("krT", [P, KEYS])
        stat = m0l("stat", [P, 4, 3])
        r0l.close()
        r0q = region()
        cqs = r0q.enter_context(nc.sbuf_tensor("cqs", [P, TT + TC, QL + KVL], f32))
        r0q.close()
        r0.close()
        r0b = region()
        m0b = lambda name, shape, dt=f32: r0b.enter_context(nc.sbuf_tensor(name, shape, dt))
        catT = m0b("catT", [P, 2, CC, N])
        oo = m0b("oo", [P, TT, HEADS * VH])
        r0b.close()
        wo0 = adaw

        r1 = region()
        m1 = lambda name, shape, dt=f32: r1.enter_context(nc.sbuf_tensor(name, shape, dt))
        r1n = region()
        rn1 = r1n.enter_context(nc.sbuf_tensor("rn1", [P, TT, D], f32))
        r1n.close()
        oT1 = m1("oT1", [P, SCC, N])
        aTh = m1("aTh", [P, KC, N], f32r)
        aTl = m1("aTl", [P, KC, N], f32r)
        zz = m1("zz", [P, 2, N + 2])
        cgs = m1("cgs", [P, 2, N])
        zt = m1("zt", [P, 2, N])
        gap1 = m1("gap1", [P, D - 4])
        w3 = m1("w3", [P, 2, KC, 3, P])
        w3h = m1("w3h", [P, 2, KC // 2, 3, P], f32r)
        w3l = m1("w3l", [P, 2, KC // 2, 3, P], f32r)
        aTf = m1("aTf", [P, 2, N])
        r1.close()
        wo1 = adaw

        rm = region()
        mm = lambda name, shape, dt=f32: rm.enter_context(nc.sbuf_tensor(name, shape, dt))
        wh = mm("wh", [P, 3, UNIT], f32r)
        wl = mm("wl", [P, 3, UNIT], f32r)
        acc = mm("acc", [P, TT, D])
        rr = region()
        mr = lambda name, shape, dt=f32: rr.enter_context(nc.sbuf_tensor(name, shape, dt))
        eqw = mr("eqw", [P, TT, TOPK, EXPERTS])
        scT = mr("scT", [EXPERTS, N])
        hot_s = mr("hot_s", [P, 4, P])
        hot_b = mr("hot_b", [P, 4, COLS])
        rr.close()
        xg = mm("xg", [P, 2, D])
        yo = mm("yo", [P, 2, D])
        rf = region()
        fTl = rf.enter_context(nc.sbuf_tensor("fTl", [P, KC, N], f32r))
        rf.close()
        xTh = mm("xTh", [P, 2, KC, P], f32r)
        xTl = mm("xTl", [P, 2, KC, P], f32r)
        rf = region()
        fTh = rf.enter_context(nc.sbuf_tensor("fTh", [P, KC, N], f32r))
        rf.close()
        raw45 = mm("raw45", [P, 2, UNIT])
        rf = region()
        rw = rf.enter_context(nc.sbuf_tensor("rw", [P, KC, EXPERTS], f32))
        rwh = rf.enter_context(nc.sbuf_tensor("rwh", [P, KC, EXPERTS], f32r))
        rwl = rf.enter_context(nc.sbuf_tensor("rwl", [P, KC, EXPERTS], f32r))
        rf.close()
        sg = mm("sg", [P, 2, DE])
        hTh = mm("hTh", [P, 2, 2, P], f32r)
        hTl = mm("hTl", [P, 2, 2, P], f32r)
        hh = mm("hh", [P, 2, DE])
        wts = mm("wts", [P, TT, TOPK])
        becol = mm("becol", [P, 1])
        vtab = mm("vtab", [P, COLS], i32)
        ttab = mm("ttab", [P, COLS], i32)
        etab = mm("etab", [1, COLS], i32)
        xid = mm("xid", [P, 2], u32)
        yid = mm("yid", [P, 2], u32)
        rm.close()
        ry = region()
        yl = ry.enter_context(nc.sbuf_tensor("yl", [P, 2, TOPK, D], f32))
        ry.close()

        raw4 = adaw.rearrange("p b k n -> p (b k n)").rearrange("p (r n) -> p r n", n=UNIT)
        raw = lambda r: raw4[:, r, :] if r < 4 else raw45[:, r - 4, :]

        pp = [stack.enter_context(nc.psum_tensor(f"pp{i}", [P, 2 * HB], f32)) for i in range(4)]
        bank = lambda i: pp[i // 2][:, (i % 2) * HB:(i % 2 + 1) * HB]

        c_in = sem("c_in"); x_in = sem("x_in"); hc_in = sem("hc_in"); const_in = sem("const_in"); rows_in = sem("rows_in")
        q_const = sem("q_const"); pool_set = sem("pool_set")
        ada_in = both("ada_in"); ada_ps = sem("ada_ps"); ada_row = sem("ada_row")
        mod_st = both("mod_st"); acol_in = sem("acol_in"); ada_col = sem("ada_col"); g1_in = sem("g1_in"); ab_in = sem("ab_in"); g2_in = sem("g2_in")
        csil_ok = sem("csil_ok")
        sq_done = sem("sq_done"); var_done = sem("var_done"); std_done = sem("std_done"); rn_done = sem("rn_done")
        t_ps = sem("t_ps"); t_out = sem("t_out")
        cw_ps = sem("cw_ps"); cw_out = sem("cw_out")
        wlat_in = sem("wlat_in"); wlat_swap = sem("wlat_swap"); wab_in = both("wab_in"); wab_used = sem("wab_used")
        wu_in = sem("wu_in"); wu_swap = sem("wu_swap"); wo_in = sem("wo_in"); woa_in = sem("woa_in")
        lat_ps = sem("lat_ps"); lat_out = sem("lat_out"); lat_sq = sem("lat_sq"); lat_var = sem("lat_var"); lat_std = sem("lat_std")
        lat_n = sem("lat_n"); latT_ps = sem("latT_ps"); latT_out = sem("latT_out")
        kr_ps = sem("kr_ps"); kr_out = sem("kr_out"); krc_out = sem("krc_out")
        u_ps = sem("u_ps"); sg_out = sem("sg_out"); v_out = sem("v_out")
        cv_done = sem("cv_done"); mean_ps = sem("mean_ps"); d_done = sem("d_done"); dsq = sem("dsq"); varc_ps = sem("varc_ps")
        cvar = sem("cvar"); cstd = sem("cstd"); dn = sem("dn"); ca_out = sem("ca_out")
        v_ps = sem("v_ps"); vv_out = sem("vv_out")
        kn_ps = sem("kn_ps"); kn_out = sem("kn_out"); kr_copy = sem("kr_copy")
        q_ps = sem("q_ps"); qn_out = sem("qn_out"); qr_out = sem("qr_out")
        s_ps = sem("s_ps"); mx = sem("mx"); ex = sem("ex"); pt_ps = sem("pt_ps"); pt_out = sem("pt_out"); pv_ps = sem("pv_ps")
        o_out = sem("o_out"); oT_ps = sem("oT_ps"); oT_out = sem("oT_out")
        y_ps = sem("y_ps"); y_g = sem("y_g"); h_new = sem("h_new")
        w3_in = both("w3_in"); w3_hi = sem("w3_hi"); w3_lo = sem("w3_lo"); aT_hi = sem("aT_hi"); aT_lo = sem("aT_lo"); u3_half = sem("u3_half")
        u3_ps = sem("u3_ps"); cg_out = sem("cg_out"); z_out = sem("z_out"); o1_out = sem("o1_out")
        PER = {"f_done": TT, "f_stored": 16 * TT, "fT_ps": KC, "fT_out": KC, "lg_ps": 1, "sc_out": 1, "st_ps": 1, "f_var": TT, "f_std": TT, "rt": 1,
               "rk_in": 1, "rk_ps": 1, "places": 1, "hot": 2 * TT * TOPK, "hot_used": TT * TOPK, "tables": 4, "be_ps": 1, "rconst_in": 32,
               "rw_hi": 1, "rw_lo": 1, "fT_hi": KC, "comb": TT * TOPK, "hfin": TT - 1, "hlast": 1, "n_var": TT, "n_std": TT, "gated": TT - 1,
               **{f"yl_in{b}{part}": 16 * TT // 2 for b in range(2) for part in range(2)}}
        L = {name: [sem(name)] * DEPTH for name in PER}
        at = lambda l, name, n: PER[name] * l + n
        for name in ("w_in0 w_in1 w_in2 w_in3 w_in4 w_in5 x_in0 x_in1 yw0 yw1 ye0 ye1 yp0 yp1 xp0 x_used x_hi x_lo x_id y_id "
                     "gu_h gu s hm hp h_hi ho whg whd w_gu w_d fence").split():
            L[name] = [sem(name)] * DEPTH
        fin_o = sem("fin_o"); stored = sem("stored"); fw_in = sem("fw_in")

        block = stack.enter_context(nc.Block())

        class Counts:

            def __init__(self, eng, l):
                self.l = l
                self.off = eng.value_load(last_loop_pair[0:1, 0:1], min_val=10, max_val=MAXP - 2) + 2 if l else 0

            def n(self, b, i):
                return 2 * (i + self.off) + b

            def tile(self, t):
                return TT * self.l + 2 * self.off + t + 1

            def block(self, b, i):
                return TT * (self.l + 1) + self.n(b, i) + 1

            def arrived(self, b, i, u):
                return (16 if u == 2 else 32) * (i + self.off + 1 + (self.l + 1 if b == 0 else 0))

            def shared_arrived(self, u):
                return (16 if u == 2 else 32) * (self.off + self.l + 1)

            def split(self, b, i, u):
                return (self.l + 1) + self.n(b, i) + 1 if u == 2 else 2 * (self.l + 1) + 2 * self.n(b, i) + u + 1

            def shared_split(self, u):
                return self.l + 2 * self.off + 1 if u == 2 else 2 * self.l + 4 * self.off + u + 1

        def run_blocks(eng, last, step):
            for b in range(2):
                step(b, 0, first=(b == 0))
            with eng.Fori(1, last) as i:
                for b in range(2):
                    step(b, i)
            for b in range(2):
                step(b, last, last=(b == 1), last_pair=True)

        after = lambda b, i: (1, i) if b == 0 else (0, i + 1)
        prior = lambda b, i: (1, i - 1) if b == 0 else (0, i)

        Y3 = [y.rearrange("(t p e) d -> p t e d", p=P, e=8) for y in Y_dram]
        F3 = [f.rearrange("(t p) d -> p t d", p=P) for f in F_dram]
        adaw_d = [a["ada_w"][l].rearrange("(p k) n -> p k n", k=KC) for l in range(DEPTH)]
        win_d = a["ev_w_in"][0].rearrange("(p k) n -> p k n", k=KC)
        w3_d = a["od_w_in"][0].rearrange("(p k) (j n) -> p k j n", k=KC, j=3)
        NSEC = 6
        SH1, SC1, G1, SH2, SC2, G2 = range(NSEC)
        CHUNKS = 2 * NSEC
        FIRST = 4
        MID = 4

        @block.sync
        def _(sp):
            sp.dma_start(ccol[:, 0, :], c.rearrange("a (p k) -> (a p) k", k=KC)).then_inc(c_in, 16)
            sp.dma_start(ccol[:, 1, :], c_ctx.rearrange("(p k) -> p k", k=KC)).then_inc(c_in, 16)
            def load_ada(m):
                l, n = m // CHUNKS, m % CHUNKS
                if m >= 2:
                    sp.wait_ge(ada_row, m - 1)
                sp.dma_start(adaw[:, m % 2, :, :], adaw_d[l][:, :, n * HB:(n + 1) * HB]).then_inc(ada_in[m % 2], 16)
                sp.dma_start(adab[:, m % 2, :], a["ada_b"][l:l + 1, n * HB:(n + 1) * HB].partition_broadcast(2).rearrange("p a d -> p (a d)")).then_inc(ada_in[m % 2], 16)

            for m in range(2):
                load_ada(m)
            sp.dma_start(h[:, :, :], x[0].rearrange("(t p) d -> p t d", p=P)).then_inc(x_in, 16)
            sp.dma_start(hc[:, :, :], ctx_in[0].rearrange("(t p) d -> p t d", p=P)).then_inc(hc_in, 16)
            for m in range(2, FIRST):
                load_ada(m)
            sp.dma_start(wlat[:, :, 0:LAT], win_d[:, :, 2 * CONV:]).then_inc(wlat_in, 16)
            sp.wait_ge(acol_in, 32)
            for ci in range(CC):
                if ci >= 2:
                    sp.wait_ge(wab_used, ci - 1)
                for j in range(2):
                    sp.dma_start(wab[:, ci % 2, :, j, :], win_d[:, :, j * CONV + ci * P:j * CONV + (ci + 1) * P]).then_inc(wab_in[ci % 2], 16)
                if ci == 1:
                    sp.dma_start(wuq[:, :, :, 0:NOPE + ROPE], a["ev_w_uq"][0].rearrange("(p j) h d -> p j h d", j=2)).then_inc(wu_in, 16)
                    sp.dma_start(wukv[:, :, :], a["ev_w_ukv"][0]).then_inc(wu_in, 16)
                    load_ada(FIRST)
                    load_ada(FIRST + 1)
            for m in range(FIRST + 2, DEPTH * CHUNKS):
                load_ada(m)
            wo0v = wo0.rearrange("p b k n -> p (b k n)").rearrange("p (c n) -> p c n", n=D)
            sp.wait_ge(ada_row, DEPTH * CHUNKS - 1)
            sp.dma_start(wo0v[:, 0:CC, :], a["ev_w_out"][0, CONV:, :].rearrange("(p c) n -> p c n", c=CC)).then_inc(woa_in, 16)
            sp.wait_ge(ada_row, DEPTH * CHUNKS)
            sp.dma_start(wo0v[:, CC:2 * CC, :], a["ev_w_out"][0, 0:CONV, :].rearrange("(c p) n -> p c n", p=P)).then_inc(wo_in, 16)

            def load_wo():
                wo1v = wo1.rearrange("p b k n -> p (b k n)").rearrange("p (c n) -> p c n", n=D)
                sp.dma_start(wo1v, a["od_w_out"][0].rearrange("(c p) n -> p c n", p=P)).then_inc(wo_in, 16)

            def load_short_conv():
                for ci in range(SCC):
                    if ci >= 2:
                        sp.wait_ge(w3_lo, 2 * (ci - 1))
                    for j in range(3):
                        sp.dma_start(w3[:, ci % 2, :, j, :], w3_d[:, :, j, ci * P:(ci + 1) * P]).then_inc(w3_in[ci % 2], 16)

            def experts(l):
                s = {k: v[l] for k, v in L.items()}
                sp.wait_ge(h_new, 2 * TT * (l + 1))
                sp.dma_start(rw[:, :, :], a["router_w"][l].rearrange("(p k) e -> p k e", k=KC)).then_inc(s["rconst_in"], 16)
                for b in range(2):
                    sp.wait_ge(mod_st[b], 16 * CHUNKS * DEPTH // 2)
                sp.dma_start(rbias[:, :], a["router_bias"][l:l + 1, :].partition_broadcast(P).rearrange("p a d -> p (a d)")).then_inc(s["rconst_in"], 16)

                def half(r, name, j, u, src):
                    sp.dma_start(raw(r)[:, j * (UNIT // 2):(j + 1) * (UNIT // 2)].rearrange("p (k n) -> p k n", n=DE),
                                 src.rearrange("(p k) n -> p k n", k=KC)[:, u * KC // 2:(u + 1) * KC // 2, :]).then_inc(s[f"w_in{r}"], 16)

                for u in range(2):
                    for j, name in enumerate(("sh_w_gate", "sh_w_up")):
                        half(u, name, j, u, a[name][l])
                sp.dma_start(raw(2), a["sh_w_down"][l].rearrange("(p j) n -> p (j n)", j=2)).then_inc(s["w_in2"], 16)
                for t in range(TT):
                    sp.wait_ge(s["f_done"], at(l, "f_done", t + 1))
                    sp.dma_start(F3[l][:, t, :], acc[:, t, :]).then_inc(s["f_stored"], 16)
                sp.wait_ge(s["tables"], at(l, "tables", 4))
                last = sp.value_load(last_loop_pair[0:1, 2 * l:2 * l + 1], min_val=10, max_val=MAXP - 2) + 1
                cn = Counts(sp, l)

                def load(b, i, u, e, behind):
                    r = 3 * b + u
                    if behind:
                        sp.wait_ge(s["w_d" if u == 2 else "w_gu"], cn.split(b, i - 1, u))
                    elif b == 0:
                        sp.wait_ge(s["w_d" if u == 2 else "w_gu"], cn.shared_split(u))
                    elif u:
                        sp.wait_ge(s["gu"], cn.tile(TT - 1))
                    if u == 2:
                        sp.dma_start(raw(r).rearrange("p (a n) -> p a n", a=1),
                                     a["exp_w_down"][l][bass.ds(e, 1), :, :].rearrange("a (p j) n -> p a (j n)", j=2)).then_inc(s[f"w_in{r}"], 16)
                    else:
                        for j, name in enumerate(("exp_w_gate", "exp_w_up")):
                            sp.dma_start(raw(r)[:, j * (UNIT // 2):(j + 1) * (UNIT // 2)].rearrange("p (a k n) -> p a k n", a=1, n=DE),
                                         a[name][l][bass.ds(e, 1), :, :].rearrange("a (p k) n -> p a k n", k=KC)[:, :, u * KC // 2:(u + 1) * KC // 2, :]).then_inc(s[f"w_in{r}"], 16)

                def expert(b, i):
                    return sp.value_load(etab[0:1, bass.ds(2 * i + b, 1)], min_val=0, max_val=EXPERTS - 1)

                def step(b, i, first=False, last=False, last_pair=False):
                    here = type(i) is int and i == 0
                    if not last:
                        nb, ni = after(b, i)
                        e = expert(nb, ni)
                        for u in range(2):
                            load(nb, ni, u, e, behind=not (here and b == 0))
                    load(b, i, 2, expert(b, i), behind=not here)

                e = expert(0, 0)
                for u in range(2):
                    load(0, 0, u, e, behind=False)
                run_blocks(sp, last, step)
                sp.wait_ge(s["w_gu"], cn.split(1, last, 1))
                sp.sem_inc(s["fence"], 1)
                sp.wait_ge(s["w_d"], cn.split(0, last, 2))
                sp.sem_inc(s["fence"], 1)
                if l == 0:
                    load_wo()
                else:
                    sp.dma_start(b2b[:, :], a["final_norm_w"].rearrange("(a n) -> a n", a=1).partition_broadcast(P).rearrange("p a d -> p (a d)")).then_inc(fw_in, 16)
                for b in range(2):
                    sp.wait_ge(s[f"yw{b}"], 16 * (last + 1 + cn.off))
                    sp.sem_inc(s["fence"], 1)
                sp.wait_ge(s["yp1"], TT * (l + 1) + 2 * (last + 1 + cn.off))
                sp.sem_inc(s["fence"], 1)
                for t in range(TT):
                    if t >= 2:
                        sp.wait_ge(s["comb"], at(l, "comb", TOPK * (t - 1)))
                    for part in range(2):
                        k3 = slice(part * TOPK // 2, (part + 1) * TOPK // 2)
                        sp.dma_start(yl[:, t % 2, k3, :], Y3[l][:, t, k3, :]).then_inc(s[f"yl_in{t % 2}{part}"], 16)

            experts(0)
            load_short_conv()
            experts(1)
            for t in range(TT):
                sp.wait_ge(fin_o, t + 1)
                sp.dma_start(out[0].rearrange("(t p) d -> p t d", p=P)[:, t, :], h[:, t, :]).then_inc(stored, 16)
            sp.wait_ge(stored, 16 * TT)

        @block.gpsimd
        def _(pool):
            for dst, name in ((ident, "k_ident"), (before, "k_before"), (rope, "k_rope")):
                pool.dma_start(dst[:, :], a[name]).then_inc(const_in, 16)
            pool.dma_start(crow[0:TAPS, :], a["ev_conv_w"][0].rearrange("t a n -> t (a n)")).then_inc(rows_in, 16)
            for j, name in enumerate(("ev_conv_b", "ev_ln_w", "ev_ln_b")):
                pool.dma_start(crow[TAPS + j:TAPS + j + 1, :], a[name]).then_inc(rows_in, 16)
            pool.dma_start(orow[:, :], a["od_conv_w"][0].rearrange("t a n -> t (a n)")).then_inc(rows_in, 16)
            pool.dma_start(qnw[:, :], a["ev_q_norm_w"].rearrange("a (p j) -> p (a j)", j=2)).then_inc(q_const, 16)
            pool.dma_start(kvw[:, :], a["ev_kv_norm_w"].rearrange("a p -> p a")).then_inc(q_const, 16)
            pool.dma_start(nwcol[:, :, :], a["norm_mix_w"].rearrange("l (p k) -> p l k", k=KC)).then_inc(q_const, 16)
            nc.gpsimd.memset(ones[:, :], 1.0).then_inc(pool_set, 1)
            nc.gpsimd.memset(one_over[:, :], 1.0 / CONV).then_inc(pool_set, 1)
            nc.gpsimd.iota(iota_row[:, :], pattern=[[1, P]], base=0, channel_multiplier=0, allow_small_or_imprecise_dtypes=True).then_inc(pool_set, 1)
            nc.gpsimd.iota(iota_part[:, :], pattern=[[0, 1]], base=0, channel_multiplier=1, allow_small_or_imprecise_dtypes=True).then_inc(pool_set, 1)
            nc.gpsimd.iota(pair_val[:, :, :], pattern=[[8 * P, TT], [1, 8]], base=-EMPTY, channel_multiplier=8, allow_small_or_imprecise_dtypes=True).then_inc(pool_set, 1)

            def store_rows(m0, m1):
                for m in range(m0, m1):
                    pool.wait_ge(ada_row, m + 1)
                    n = m % CHUNKS
                    pool.dma_start(M_dram[m // CHUNKS][:, n * HB:(n + 1) * HB], mrow[:, m % 2, :]).then_inc(mod_st[m % 2], 16)

            def rows_stored(m):
                for b in range(2):
                    pool.wait_ge(mod_st[b], 16 * m // 2)

            def load_columns(l):
                for sct in (SH1, SC1):
                    pool.dma_start(acol[:, sct, :, :], M_dram[l][:, sct * D:(sct + 1) * D].rearrange("r (p k) -> p r k", k=KC)).then_inc(acol_in, 16)

            def load_row(l, sct, dst, signal):
                pool.dma_start(dst[:, :], M_dram[l][0:1, sct * D:(sct + 1) * D].partition_broadcast(P).rearrange("p a d -> p (a d)")).then_inc(signal, 16)

            def load_ffn_rows(l):
                load_row(l, SH2, b2b, ab_in)
                load_row(l, SC2, a2b, ab_in)
                pool.dma_start(nrow[:, :], a["norm_ffn_w"][l:l + 1, :].partition_broadcast(P).rearrange("p a d -> p (a d)")).then_inc(ab_in, 16)

            store_rows(0, FIRST)
            rows_stored(FIRST)
            load_columns(0)
            pool.wait_ge(wlat_in, 16)
            q8 = ROPE // 4
            for ax in range(2):
                for half in range(2):
                    d0, s0 = LAT + (2 * ax + half) * q8, QL + KVL + (2 * ax + 1 - half) * q8
                    nc.gpsimd.tensor_copy(wlat[:, :, d0:d0 + q8], wlat[:, :, s0:s0 + q8]).then_inc(wlat_swap, 1)
            pool.wait_ge(wu_in, 32)
            wuqv = wuq.rearrange("p j h d -> p (j h) d")
            for ax in range(2):
                for half in range(2):
                    d0, s0 = NOPE + ROPE + (2 * ax + half) * q8, NOPE + (2 * ax + 1 - half) * q8
                    nc.gpsimd.tensor_copy(wuqv[:, :, d0:d0 + q8], wuqv[:, :, s0:s0 + q8]).then_inc(wu_swap, 1)
            pool.wait_ge(t_ps, 2 * KC)
            nc.gpsimd.memset(vpad[:, :, :], 0.0).then_inc(pool_set, 1)
            pool.wait_ge(kr_out, 1)
            pool.wait_ge(krc_out, 1)
            pool.wait_ge(wu_swap, 4)
            pool.wait_ge(pool_set, 6)
            for b in range(2):
                if b:
                    pool.wait_ge(kr_copy, b)
                nc.gpsimd.tensor_copy(kT[NOPE:NOPE + ROPE, b, :], krT[NOPE:NOPE + ROPE, :]).then_inc(kr_copy, 1)

            store_rows(FIRST, CHUNKS)
            rows_stored(CHUNKS)
            load_row(0, G1, g1b, g1_in)
            load_ffn_rows(0)
            load_row(0, G2, g2b, g2_in)
            store_rows(CHUNKS, DEPTH * CHUNKS)
            rows_stored(DEPTH * CHUNKS)
            pool.wait_ge(t_out, 2 * KC)
            load_columns(1)

            def experts(l):
                s = {k: v[l] for k, v in L.items()}
                pool.wait_ge(h_new, 2 * TT * (l + 1))
                if l + 1 < DEPTH:
                    load_row(l + 1, G1, g1b, g1_in)
                def settled(name, value):
                    pool.wait_ge(s[name], value)
                    pool.sem_inc(s["fence"], 1)

                pool.wait_ge(kr_copy, 2)
                cn = Counts(pool, l)
                for u in range(3):
                    settled("whd" if u == 2 else "whg", 2 * cn.shared_split(u))
                    nc.gpsimd.tensor_tensor(wl[:, u, :], raw(u), wh[:, u, :].bitcast(f32), ALU.subtract).then_inc(s["w_d" if u == 2 else "w_gu"], 1)
                pool.wait_ge(s["tables"], at(l, "tables", 4))
                pool.wait_ge(s["f_stored"], at(l, "f_stored", 16 * TT))
                last = pool.value_load(last_loop_pair[0:1, 2 * l:2 * l + 1], min_val=10, max_val=MAXP - 2) + 1

                def by_fill(b, i, move):
                    token = lambda q: pool.value_load(ttab[q * P // 4:q * P // 4 + 1, bass.ds(2 * i + b, 1)], min_val=0, max_val=EMPTY // 8)
                    with pool.If(token(2) < N):
                        with pool.If(token(3) < N):
                            move(P)
                        with pool.Else():
                            move(3 * P // 4)
                    with pool.Else():
                        with pool.If(token(1) < N):
                            move(P // 2)
                        with pool.Else():
                            move(P // 4)

                def gather(b, i, behind):
                    if behind:
                        settled("x_used", cn.n(b, i - 1) + 1)
                    nc.gpsimd.tensor_copy(xid[:, b:b + 1], ttab[:, bass.ds(2 * i + b, 1)]).then_inc(s["x_id"], 1)
                    settled("x_id", cn.n(b, i) + 1)

                    def rows(n):
                        nc.gpsimd.indirect_dma_start(
                            xg[0:n, b, :], None, F_dram[l][:, :], bass.IndirectOffsetOnAxis(ap=xid[0:n, b:b + 1], axis=0),
                            bounds_check=N - 1, oob_is_err=False).then_inc(s[f"x_in{b}"], 16)

                    if type(i) is int:
                        rows(P)
                    else:
                        by_fill(b, i, rows)

                def scatter(b, i, behind):
                    if behind:
                        settled(f"yw{b}", 16 * (i + cn.off))
                    nc.gpsimd.tensor_copy(yid[:, b:b + 1], vtab[:, bass.ds(2 * i + b, 1)]).then_inc(s["y_id"], 1)
                    settled("y_id", cn.n(b, i) + 1)
                    settled("ye0", cn.block(b, i))
                    settled("ye1", cn.block(b, i))
                    by_fill(b, i, lambda n: nc.gpsimd.indirect_dma_start(
                        Y_dram[l][:, :], bass.IndirectOffsetOnAxis(ap=yid[0:n, b:b + 1], axis=0), yo[0:n, b, :], None,
                        bounds_check=N * 8 - 1, oob_is_err=False).then_inc(s[f"yw{b}"], 16))

                def step(b, i, first=False, last=False, last_pair=False):
                    if not last_pair:
                        gather(b, i + 1, True)
                    if not first:
                        pb, pi = prior(b, i)
                        scatter(pb, pi, behind=not (type(pi) is int and pi == 0))

                for b in range(2):
                    gather(b, 0, False)
                run_blocks(pool, last, step)
                scatter(1, last, True)
                pool.wait_ge(g2_in, 16 * (l + 1))
                for t in range(TT - 1):
                    pool.wait_ge(s["comb"], at(l, "comb", TOPK * (t + 1)))
                    nc.gpsimd.tensor_tensor(acc[:, t, :], acc[:, t, :], g2b[:, :], ALU.mult).then_inc(s["gated"], 1)
                    pool.wait_ge(s["gated"], at(l, "gated", t + 1))
                    nc.gpsimd.tensor_tensor(h[:, t, :], h[:, t, :], acc[:, t, :], ALU.add).then_inc(s["hfin"], 1)

            experts(0)
            load_ffn_rows(1)
            pool.wait_ge(L["hlast"][0], 1)
            load_row(1, G2, g2b, g2_in)
            experts(1)

        @block.tensor
        def _(pe):
            mmul = nc.tensor.matmul

            def split_mm(o, lh, ll, rh, rl, start, stop):
                mmul(o, lh, rh, start=start, stop=False)
                mmul(o, lh, rl, start=False, stop=False)
                return mmul(o, ll, rh, start=False, stop=stop)

            def ada_part(m, k0, k1, o):
                if k0 == 0:
                    pe.wait_ge(ada_in[m % 2], 32 * (m // 2 + 1))
                for k in range(k0, k1):
                    ins = mmul(o[0:2, :], csil[:, :, k], adaw[:, m % 2, k, :], start=(k == 0), stop=(k == KC - 1))
                if k1 == KC:
                    ins.then_inc(ada_ps, 1)

            pe.wait_ge(csil_ok, 1)
            for m in range(FIRST):
                if m >= 2:
                    pe.wait_ge(ada_row, m - 1)
                ada_part(m, 0, KC, bank(m % 2))
            pe.wait_ge(ada_row, FIRST)
            pe.wait_ge(const_in, 48)
            pe.wait_ge(rows_in, 80)
            for ci in range(CC):
                ins = nc.tensor.transpose(bank(6)[:, ci * 40:ci * 40 + TAPS + 3], crow[:, ci * P:(ci + 1) * P], ident[0:TAPS + 3, 0:TAPS + 3])
            for ci in range(SCC):
                ins = nc.tensor.transpose(bank(6)[:, 256 + ci * 4:256 + ci * 4 + 3], orow[:, ci * P:(ci + 1) * P], ident[0:3, 0:3])
            ins.then_inc(cw_ps, 1)

            for k in range(KC):
                for part in range(2):
                    n = 2 * k + part
                    if n == 0:
                        pe.wait_ge(rn_done, TT + TC)
                    if n >= 2:
                        pe.wait_ge(t_out, n - 1)
                    for t in range(TT if part == 0 else TC):
                        ins = nc.tensor.transpose(bank(n % 2)[:, t * P:(t + 1) * P], rn[:, t + (TT if part else 0), k:D:KC], ident[:, :])
                    ins.then_inc(t_ps, 1)

            pe.wait_ge(t_out, 2 * KC)
            pe.wait_ge(wlat_in, 16)
            for t in range(TT + TC):
                if t >= 2:
                    pe.wait_ge(lat_out, t - 1)
                w = QL + KVL if t < TT else KVL
                key0 = NCTX + t * P if t < TT else (t - TT) * P
                for k in range(KC):
                    ins = mmul(bank(2 + t % 2)[:, 0:w], aT[:, k, key0:key0 + P], wlat[:, k, QL + KVL - w:QL + KVL], start=(k == 0), stop=(k == KC - 1))
                ins.then_inc(lat_ps, 1)
            pe.wait_ge(wlat_swap, 4)
            for j, (k0, kn) in enumerate(((NCTX, N), (0, NCTX))):
                for k in range(KC):
                    ins = mmul(bank(4 + j)[:, 0:kn], wlat[:, k, LAT - ROPE - NOPE:LAT + ROPE], aT[:, k, k0:k0 + kn], start=(k == 0), stop=(k == KC - 1))
                ins.then_inc(kr_ps, 1)
            pe.wait_ge(cw_out, 2)
            for ci in range(CC):
                pe.wait_ge(wab_in[ci % 2], 32 * (ci // 2 + 1))
                if ci >= 1:
                    pe.wait_ge(v_out, ci)
                for j in range(2):
                    for k in range(KC):
                        ins = mmul(bank(6 + j), wab[:, ci % 2, k, j, :], aT[:, k, NCTX:], start=(k == 0), stop=(k == KC - 1))
                    ins.then_inc(u_ps if j == 0 else wab_used, 1)
            pe.wait_ge(kr_out, 1)
            pe.wait_ge(krc_out, 1)
            for m in range(FIRST, FIRST + MID):
                if m >= FIRST + 2:
                    pe.wait_ge(ada_row, m - 1)
                ada_part(m, 0, KC, bank(4 + m % 2))
            pe.wait_ge(lat_n, 2 * TT + TC)
            for j in range(2):
                for t in range(TT):
                    ins = nc.tensor.transpose(bank(j)[:, t * P:(t + 1) * P], cqs[:, t, j:QL:2], ident[:, :])
                ins.then_inc(latT_ps, 1)
            pe.wait_ge(lat_out, TT + TC)
            for t in range(TC):
                ins = nc.tensor.transpose(bank(2)[:, t * P:(t + 1) * P], cqs[:, TT + t, QL:], ident[:, :])
            ins.then_inc(latT_ps, 1)
            for t in range(TT):
                ins = nc.tensor.transpose(bank(3)[:, t * P:(t + 1) * P], cqs[:, t, QL:], ident[:, :])
            ins.then_inc(latT_ps, 1)
            pe.wait_ge(wu_in, 32)
            pe.wait_ge(latT_out, 4)
            pe.wait_ge(ada_row, FIRST + MID)
            for t in range(TT + TC):
                if t >= 2:
                    pe.wait_ge(vv_out, t - 1)
                mmul(bank(4 + t % 2), ckvT[:, t * P:(t + 1) * P], wukv[:, :, NOPE:], start=True, stop=True).then_inc(v_ps, 1)
            pe.wait_ge(wu_swap, 4)
            pe.wait_ge(kr_copy, 2)
            pe.wait_ge(vv_out, TT + TC)
            pe.wait_ge(v_out, CC)
            S = [pp[0], pp[1]]
            def head(hd):
                if hd >= 1:
                    pe.wait_ge(pt_out, TT * (hd - 1) + 2)
                for n0, nn in ((0, HB), (HB, KEYS - HB)):
                    ins = mmul(pp[3][0:NOPE, n0:n0 + nn], wukv[:, hd, 0:NOPE], ckvT[:, n0:n0 + nn], start=True, stop=True)
                ins.then_inc(kn_ps, 1)
                if hd >= 1:
                    pe.wait_ge(ada_row, FIRST + MID + 2 * hd - 1)
                for j in range(2):
                    ins = mmul(bank(5), wuq[:, j, hd, :], cqT[:, j, :], start=(j == 0), stop=(j == 1))
                ins.then_inc(q_ps, 1)

            def head_ready(hd):
                pe.wait_ge(kn_out, hd + 1)
                pe.wait_ge(qn_out, hd + 1)
                pe.wait_ge(qr_out, hd + 1)

            def scores(n):
                hd, t = n // TT, n % TT
                if n >= 2:
                    pe.wait_ge(ex, n - 1)
                for n0, nn in ((0, HB), (HB, KEYS - HB)):
                    ins = mmul(S[n % 2][:, n0:n0 + nn], qT[0:NOPE + ROPE, hd % 2, t * P:(t + 1) * P], kT[0:NOPE + ROPE, hd % 2, n0:n0 + nn], start=True, stop=True)
                ins.then_inc(s_ps, 1)

            head(0)
            head_ready(0)
            scores(0)
            for n in range(TT * HEADS):
                hd, t = n // TT, n % TT
                if t == 2 and hd + 1 < HEADS:
                    head(hd + 1)
                if n + 1 < TT * HEADS:
                    scores(n + 1)
                m, k0 = FIRST + MID + n // 2, n % 2 * KC // 2
                early = KC // 4 if t != 2 else 0
                if n % 2 == 0 and early:
                    pe.wait_ge(ada_row, m)
                if early:
                    ada_part(m, k0, k0 + early, bank(5))
                pe.wait_ge(ex, n + 1)
                if n >= 1:
                    pe.wait_ge(pt_out, n)
                if t == 2:
                    head_ready(min(hd + 1, HEADS - 1))
                    if hd + 1 == HEADS:
                        pe.wait_ge(ada_row, m)
                for j in range(KEYS // P):
                    ins = nc.tensor.transpose(pp[3][:, j * P:(j + 1) * P], pe_[:, n % 2, j * P:(j + 1) * P], ident[:, :])
                ins.then_inc(pt_ps, 1)
                ada_part(m, k0 + early, k0 + KC // 2, bank(5))
                pe.wait_ge(pt_out, n + 1)
                if n >= 1:
                    pe.wait_ge(o_out, n)
                for j in range(KEYS // P):
                    ins = mmul(bank(4)[:, 0:VH], pT[:, n % 2, j * P:(j + 1) * P], vv[:, j, hd * VH:(hd + 1) * VH], start=(j == 0), stop=(j == KEYS // P - 1))
                ins.then_inc(pv_ps, 1)
            pe.wait_ge(cv_done, CC)
            pe.wait_ge(ex, TT * HEADS)
            for ci in range(CC):
                ins = mmul(bank(0), one_over[:, :], cy[:, ci, :], start=(ci == 0), stop=(ci == CC - 1))
            ins.then_inc(mean_ps, 1)
            pe.wait_ge(o_out, TT * HEADS)
            for ci in range(CC):
                if ci >= 2:
                    pe.wait_ge(oT_out, ci - 1)
                for t in range(TT):
                    ins = nc.tensor.transpose(bank(2 + ci % 2)[:, t * P:(t + 1) * P], oo[:, t, ci:HEADS * VH:CC], ident[:, :])
                ins.then_inc(oT_ps, 1)
            for ci in range(CC):
                pe.wait_ge(dsq, ci + 1)
                ins = mmul(bank(1), one_over[:, :], csg[:, ci % 2, :], start=(ci == 0), stop=(ci == CC - 1))
                ins.then_inc(varc_ps, 1)

            def mix_out(l, left, wv, base, behind=None):
                def part(n, k0, k1):
                    t, half = n // 2, n % 2
                    for k in range(k0, k1):
                        ins = mmul(bank(base + n % 2), left(k, t), wv[:, k, half * HB:(half + 1) * HB], start=(k == 0), stop=(k == KC - 1))
                    return ins

                for n in range(2):
                    part(n, 0, KC // 2)
                if behind:
                    behind()
                for n in range(2 * TT):
                    if n >= 2:
                        pe.wait_ge(y_g, 2 * TT * l + n - 1)
                    part(n, 0 if n >= 2 else KC // 2, KC).then_inc(y_ps, 1)

            def conv_half():
                pe.wait_ge(wo_in, 16)
                pe.wait_ge(ca_out, CC)

            pe.wait_ge(woa_in, 16)
            pe.wait_ge(oT_out, CC)
            wo0v = wo0.rearrange("p b k n -> p (b k n)").rearrange("p (c n) -> p c n", n=D)
            mix_out(0, lambda k, t: catT[:, 1 - k // CC, k % CC, t * P:(t + 1) * P], wo0v, 4, conv_half)

            def experts(l):
                s = {k: v[l] for k, v in L.items()}
                pe.wait_ge(s["f_done"], at(l, "f_done", TT))
                def router(k):
                    if k == 0:
                        pe.wait_ge(s["rw_lo"], at(l, "rw_lo", 1))
                    pe.wait_ge(s["fT_out"], at(l, "fT_out", k + 1))
                    return split_mm(bank(2)[0:EXPERTS, :], rwh[:, k, :], rwl[:, k, :], fTh[:, k, :], fTl[:, k, :], k == 0, k == KC - 1)

                for k in range(KC):
                    if k >= 2:
                        router(k - 2)
                    for t in range(TT):
                        ins = nc.tensor.transpose(bank(k % 2)[:, t * P:(t + 1) * P], acc[:, t, k:D:KC], ident[:, :])
                    ins.then_inc(s["fT_ps"], 1)
                router(KC - 2)
                router(KC - 1).then_inc(s["lg_ps"], 1)
                pe.wait_ge(s["sc_out"], at(l, "sc_out", 1))
                for t in range(TT):
                    ins = nc.tensor.transpose(bank(5)[:, t * EXPERTS:(t + 1) * EXPERTS], scT[:, t * P:(t + 1) * P], ident[0:EXPERTS, 0:EXPERTS])
                ins.then_inc(s["st_ps"], 1)
                cn = Counts(pe, l)

                def gate_up(b, left, split, signal=None):
                    for u in range(2):
                        pe.wait_ge(s["w_gu"], split(u))
                        for k in range(KC // 2):
                            hi, lo = left(u * KC // 2 + k)
                            cols = lambda w: w[:, u, :].rearrange("p (j k n) -> p j k n", j=2, n=DE)[:, :, k, :]
                            ins = split_mm(bank(2 + b), hi, lo, cols(wh), cols(wl), u + k == 0, u == 1 and k == KC // 2 - 1)
                        ins.then_inc(s["gu" if u else "gu_h"], 1)

                def hidden_T(b, n):
                    pe.wait_ge(s["hm"], n)
                    for j in range(2):
                        ins = nc.tensor.transpose(bank(4 + b)[:, j * P:(j + 1) * P], hh[:, b, j:DE:2], ident[:, :])
                    ins.then_inc(s["hp"], 1)

                def down(b, n, split, behind=True):
                    pe.wait_ge(s["ho"], n)
                    pe.wait_ge(s["w_d"], split)
                    if behind:
                        pe.wait_ge(s["ye0"], n - 1)
                        pe.wait_ge(s["ye1"], n - 1)
                    for half in range(2):
                        for j in range(2):
                            cols = lambda w: w[:, 2, j * D + half * HB:j * D + (half + 1) * HB]
                            ins = split_mm(bank(6 + half), hTh[:, b, j, :], hTl[:, b, j, :], cols(wh), cols(wl), j == 0, j == 1)
                        ins.then_inc(s[f"yp{half}"], 1)

                tile_gu = lambda t: gate_up(t % 2, lambda k: (fTh[:, k, t * P:(t + 1) * P], fTl[:, k, t * P:(t + 1) * P]), cn.shared_split)

                def tile_down(t):
                    down(t % 2, cn.tile(t), cn.shared_split(2), behind=l > 0 or t > 0)

                tile_gu(0)
                tile_gu(1)
                pe.wait_ge(s["rk_in"], at(l, "rk_in", 1))
                for t in range(TT):
                    for q in range(t + 1):
                        ins = mmul(bank(1)[:, t * EXPERTS:(t + 1) * EXPERTS], before[:, :] if q == t else ones[:, :], mask[:, q, :], start=(q == 0), stop=(q == t))
                for q in range(TT):
                    ins = mmul(bank(0)[:, 0:EXPERTS], ones[:, :], mask[:, q, :], start=(q == 0), stop=(q == TT - 1))
                ins.then_inc(s["rk_ps"], 1)
                hidden_T(0, cn.tile(0))
                hidden_T(1, cn.tile(1))
                tile_gu(2)
                tile_gu(3)
                pe.wait_ge(s["places"], at(l, "places", 1))
                mmul(bank(1)[0:1, 256:256 + COLS], becol[0:COLS, :], ident[0:COLS, 0:COLS], start=True, stop=True).then_inc(s["be_ps"], 1)
                for n in range(TT * TOPK):
                    pe.wait_ge(s["hot"], at(l, "hot", 2 * (n + 1)))
                    mmul(bank(0)[:, 0:COLS], hot_s[:, n % 4, :], hot_b[:, n % 4, :], start=(n == 0), stop=(n == TT * TOPK - 1)).then_inc(s["hot_used"], 1)
                tile_down(0)
                tile_down(1)
                hidden_T(0, cn.tile(2))
                hidden_T(1, cn.tile(3))
                tile_down(2)
                tile_down(3)
                pe.wait_ge(s["tables"], at(l, "tables", 4))
                last = pe.value_load(last_loop_pair[0:1, 2 * l:2 * l + 1], min_val=10, max_val=MAXP - 2) + 1

                def rows_T(b, i):
                    pe.wait_ge(s[f"x_in{b}"], 16 * (i + cn.off + 1))
                    for g in range(2):
                        for k in range(KC // 2):
                            kk = g * KC // 2 + k
                            ins = nc.tensor.transpose(bank(g)[:, k * P:(k + 1) * P], xg[:, b, kk:D:KC], ident[:, :])
                        ins.then_inc(s["x_used" if g else "xp0"], 1)

                def step(b, i, first=False, last=False, last_pair=False):
                    if not first:
                        hidden_T(prior(b, i)[0], cn.block(*prior(b, i)))
                    pe.wait_ge(s["x_lo"], 2 * cn.n(b, i) + 2)
                    gate_up(b, lambda k: (xTh[:, b, k, :], xTl[:, b, k, :]), lambda u: cn.split(b, i, u))
                    if not last:
                        rows_T(*after(b, i))
                    if not first:
                        down(prior(b, i)[0], cn.block(*prior(b, i)), cn.split(*prior(b, i), 2))

                rows_T(0, 0)
                run_blocks(pe, last, step)
                hidden_T(1, cn.block(1, last))
                down(1, cn.block(1, last), cn.split(1, last, 2))

            experts(0)
            for k in range(KC):
                if k == 0:
                    pe.wait_ge(rn_done, TT + TC + TT)
                if k >= 2:
                    pe.wait_ge(t_out, 2 * KC + k - 1)
                for t in range(TT):
                    ins = nc.tensor.transpose(bank(k % 2)[:, t * P:(t + 1) * P], rn1[:, t, k:D:KC], ident[:, :])
                ins.then_inc(t_ps, 1)
            pe.wait_ge(aT_lo, KC)
            for ci in range(SCC):
                if ci >= 2:
                    pe.wait_ge(o1_out, ci - 1)
                for half in range(2):
                    pe.wait_ge(w3_lo, 2 * ci + half + 1)
                    for j in (1, 2, 0):
                        for k in range(KC // 2):
                            kk = half * KC // 2 + k
                            ins = split_mm(bank(2 + 3 * (ci % 2) + j), w3h[:, half, k, j, :], w3l[:, half, k, j, :],
                                           aTh[:, kk, :], aTl[:, kk, :], kk == 0, kk == KC - 1)
                        if half:
                            ins.then_inc(u3_ps, 1)
                    if not half:
                        ins.then_inc(u3_half, 1)
            pe.wait_ge(wo_in, 32)
            pe.wait_ge(o1_out, SCC)
            wo1v = wo1.rearrange("p b k n -> p (b k n)").rearrange("p (c n) -> p c n", n=D)
            mix_out(1, lambda k, t: oT1[:, k, t * P:(t + 1) * P], wo1v, 0)
            experts(1)

        @block.scalar
        def _(act):
            act.wait_ge(c_in, 32)
            nc.scalar.activation(csil[:, :, :], ccol[:, :, :], ACT.Silu).then_inc(csil_ok, 1)

            act.wait_ge(x_in, 16)
            act.wait_ge(hc_in, 16)
            for t in range(TT + TC):
                nc.scalar.activation(rn[:, t, :], h[:, t, :] if t < TT else hc[:, t - TT, :], ACT.Square, accum_out=ssq[:, t:t + 1]).then_inc(sq_done, 1)
            act.wait_ge(var_done, 1)
            nc.scalar.activation(rstd[:, 0:TT + TC], rstd[:, 0:TT + TC], ACT.Sqrt).then_inc(std_done, 1)

            act.wait_ge(acol_in, 32)
            act.wait_ge(ada_col, 1)
            for k in range(KC):
                for part in range(2):
                    n = 2 * k + part
                    act.wait_ge(t_ps, n + 1)
                    o, width = (aT[:, k, 0:NCTX], NCTX) if part else (aT[:, k, NCTX:], N)
                    nc.scalar.activation(o, bank(n % 2)[:, 0:width], ACT.Identity,
                                         scale=acol[:, 1, part, k:k + 1], bias=acol[:, 0, part, k:k + 1]).then_inc(t_out, 1)
            for t in range(TT + TC):
                act.wait_ge(lat_ps, t + 1)
                w = QL + KVL if t < TT else KVL
                nc.scalar.activation(cqs[:, t, QL + KVL - w:], bank(2 + t % 2)[:, 0:w], ACT.Copy).then_inc(lat_out, 1)
            act.wait_ge(lat_out, TT + TC)
            cyf = cy.rearrange("p c n -> p (c n)")
            for t in range(TT + TC):
                nc.scalar.activation(cyf[:, t * KVL:(t + 1) * KVL], cqs[:, t, QL:], ACT.Square, accum_out=ssq[:, 8 + TT + t:9 + TT + t]).then_inc(lat_sq, 1)
                if t < TT:
                    nc.scalar.activation(cyf[:, 768 + t * QL:768 + (t + 1) * QL], cqs[:, t, 0:QL], ACT.Square, accum_out=ssq[:, 8 + t:9 + t]).then_inc(lat_sq, 1)
            act.wait_ge(kr_ps, 2)
            nc.scalar.activation(krT[NOPE:NOPE + ROPE, 0:NCTX], bank(5)[NOPE:NOPE + ROPE, 0:NCTX], ACT.Copy).then_inc(krc_out, 1)
            act.wait_ge(lat_var, 1)
            nc.scalar.activation(rstd[:, 8:8 + 2 * TT + TC], rstd[:, 8:8 + 2 * TT + TC], ACT.Sqrt).then_inc(lat_std, 1)
            for ci in range(CC):
                act.wait_ge(wab_used, ci + 1)
                if ci >= 2:
                    act.wait_ge(v_out, ci - 1)
                nc.scalar.activation(csg[:, ci % 2, :], bank(7), ACT.Sigmoid).then_inc(sg_out, 1)
            act.wait_ge(q_const, 48)
            for j in range(2):
                act.wait_ge(latT_ps, j + 1)
                nc.scalar.activation(cqT[:, j, :], bank(j), ACT.Copy, scale=qnw[:, j:j + 1]).then_inc(latT_out, 1)
            act.wait_ge(latT_ps, 4)
            nc.scalar.activation(ckvT[:, 0:NCTX], bank(2)[:, 0:NCTX], ACT.Copy, scale=kvw[:, 0:1]).then_inc(latT_out, 1)
            nc.scalar.activation(ckvT[:, NCTX:], bank(3), ACT.Copy, scale=kvw[:, 0:1]).then_inc(latT_out, 1)
            for t in range(TT + TC):
                act.wait_ge(v_ps, t + 1)
                nc.scalar.activation(vv[:, t, :], bank(4 + t % 2), ACT.Copy).then_inc(vv_out, 1)
            def head(hd):
                act.wait_ge(kn_ps, hd + 1)
                nc.scalar.activation(kT[0:NOPE, hd % 2, :], pp[3][0:NOPE, 0:KEYS], ACT.Copy).then_inc(kn_out, 1)
                act.wait_ge(q_ps, hd + 1)
                nc.scalar.activation(qT[0:NOPE, hd % 2, :], bank(5)[0:NOPE, :], ACT.Copy, scale=ATT_SCALE).then_inc(qn_out, 1)

            head(0)
            for n in range(TT * HEADS):
                if n % TT == 2 and n // TT + 1 < HEADS:
                    head(n // TT + 1)
                act.wait_ge(mx, n + 1)
                if n >= 2:
                    act.wait_ge(pt_ps, n - 1)
                nc.scalar.activation(pe_[:, n % 2, :], pp[n % 2][:, 0:KEYS], ACT.Exp, bias=stat[:, n % 4, 0:1],
                                     accum_out=stat[:, n % 4, 1:2]).then_inc(ex, 1)
                act.wait_ge(pt_ps, n + 1)
                if n >= 2:
                    act.wait_ge(pv_ps, n - 1)
                nc.scalar.activation(pT[:, n % 2, :], pp[3][:, 0:KEYS], ACT.Copy).then_inc(pt_out, 1)
            for ci in range(CC):
                act.wait_ge(oT_ps, ci + 1)
                nc.scalar.activation(catT[:, 1, ci, :], bank(2 + ci % 2), ACT.Copy).then_inc(oT_out, 1)
            for ci in range(CC):
                act.wait_ge(d_done, ci + 1)
                if ci >= 2:
                    act.wait_ge(varc_ps, ci - 1)
                nc.scalar.activation(csg[:, ci % 2, :], cy[:, ci, :], ACT.Square).then_inc(dsq, 1)
            act.wait_ge(cvar, 2)
            nc.scalar.activation(csg[:, 0, :], csg[:, 0, :], ACT.Sqrt).then_inc(cstd, 1)
            for ci in range(CC):
                act.wait_ge(dn, ci + 1)
                nc.scalar.activation(catT[:, 0, ci, :], cy[:, ci, :], ACT.Silu, scale=cvw[:, ci, TAPS + 1:TAPS + 2],
                                     bias=cvw[:, ci, TAPS + 2:TAPS + 3]).then_inc(ca_out, 1)

            def experts(l):
                s = {k: v[l] for k, v in L.items()}
                for t in range(TT):
                    act.wait_ge(h_new, 2 * (TT * l + t + 1))
                    row = TT + t if l else 2 * TT + t
                    nc.scalar.activation(yl[:, row // TOPK, row % TOPK, :], h[:, t, :], ACT.Square, accum_out=ssq[:, t:t + 1]).then_inc(sq_done, 1)
                    act.wait_ge(s["f_var"], at(l, "f_var", t + 1))
                    nc.scalar.activation(rstd[:, t:t + 1], rstd[:, t:t + 1], ACT.Sqrt).then_inc(s["f_std"], 1)
                act.wait_ge(s["rconst_in"], at(l, "rconst_in", 32))
                nc.scalar.activation(rwh[:, :, :], rw[:, :, :], ACT.Copy).then_inc(s["rw_hi"], 1)
                cn = Counts(act, l)

                def split(r, u, arrived, free):
                    act.wait_ge(s[f"w_in{r}"], arrived)
                    if free is not None:
                        act.wait_ge(s[("gu_h", "gu", "yp1")[u]], free)
                    for piece in range(2):
                        cols = slice(piece * UNIT // 2, (piece + 1) * UNIT // 2)
                        nc.scalar.activation(wh[:, u, cols], raw(r)[:, cols], ACT.Copy).then_inc(s["whd" if u == 2 else "whg"], 1)

                for k in range(KC):
                    act.wait_ge(s["fT_ps"], at(l, "fT_ps", k + 1))
                    nc.scalar.activation(fTh[:, k, :], bank(k % 2), ACT.Copy).then_inc(s["fT_hi"], 1)
                    if k == KC // 2:
                        split(0, 0, cn.shared_arrived(0), None)
                split(1, 1, cn.shared_arrived(1), None)
                act.wait_ge(s["lg_ps"], at(l, "lg_ps", 1))
                nc.scalar.activation(scT[:, :], bank(2)[0:EXPERTS, :], ACT.Sigmoid).then_inc(s["sc_out"], 1)
                split(2, 2, cn.shared_arrived(2), None)

                def silu(b, n):
                    act.wait_ge(s["gu"], n)
                    nc.scalar.activation(sg[:, b, :], bank(2 + b)[:, 0:DE], ACT.Silu).then_inc(s["s"], 1)

                def hidden_hi(b, n):
                    act.wait_ge(s["hp"], n)
                    nc.scalar.activation(hTh[:, b, :, :].rearrange("p j n -> p (j n)"), bank(4 + b)[:, 0:2 * P], ACT.Copy).then_inc(s["h_hi"], 1)

                def shared_out(t):
                    act.wait_ge(s["yp0"], cn.tile(t))
                    if t == 0:
                        act.wait_ge(s["f_stored"], at(l, "f_stored", 16 * TT))
                    nc.scalar.activation(acc[:, t, 0:HB], bank(6), ACT.Copy).then_inc(s["ye0"], 1)

                for b in range(2):
                    silu(b, cn.tile(b))
                for b in range(2):
                    hidden_hi(b, cn.tile(b))
                for b in range(2):
                    silu(b, cn.tile(2 + b))
                shared_out(0)
                shared_out(1)
                for b in range(2):
                    hidden_hi(b, cn.tile(2 + b))
                shared_out(2)
                shared_out(3)
                act.wait_ge(s["tables"], at(l, "tables", 4))
                last = act.value_load(last_loop_pair[0:1, 2 * l:2 * l + 1], min_val=10, max_val=MAXP - 2) + 1

                def rows_hi(b, i):
                    for g in range(2):
                        act.wait_ge(s["x_used" if g else "xp0"], cn.n(b, i) + 1)
                        nc.scalar.activation(xTh[:, b, g * KC // 2:(g + 1) * KC // 2, :].rearrange("p k n -> p (k n)"), bank(g), ACT.Copy).then_inc(s["x_hi"], 1)

                def out_rows(b, i):
                    if not (type(i) is int and i == 0):
                        act.wait_ge(s[f"yw{b}"], 16 * (i + cn.off))
                    act.wait_ge(s["yp0"], cn.block(b, i))
                    nc.scalar.activation(yo[:, b, 0:HB], bank(6), ACT.Copy).then_inc(s["ye0"], 1)
                    act.wait_ge(s["yp1"], cn.block(b, i))
                    nc.scalar.activation(yo[:, b, HB:], bank(7), ACT.Copy).then_inc(s["ye1"], 1)

                def unit(b, i, u):
                    split(3 * b + u, u, cn.arrived(b, i, u), cn.block(b, i) - 1)

                def step(b, i, first=False, last=False, last_pair=False):
                    if not first:
                        hidden_hi(prior(b, i)[0], cn.block(*prior(b, i)))
                    if not last:
                        unit(*after(b, i), 0)
                        rows_hi(*after(b, i))
                    silu(b, cn.block(b, i))
                    if not last:
                        unit(*after(b, i), 1)
                    if not first:
                        out_rows(*prior(b, i))
                    unit(b, i, 2)

                rows_hi(0, 0)
                for u in range(2):
                    unit(0, 0, u)
                run_blocks(act, last, step)
                hidden_hi(1, cn.block(1, last))
                out_rows(1, last)

            def next_norm(l):
                s = {k: v[l] for k, v in L.items()}
                for t in range(TT):
                    name = "hfin" if t + 1 < TT else "hlast"
                    act.wait_ge(s[name], at(l, name, t % (TT - 1) + 1))
                    nc.scalar.activation(acc[:, t, :], h[:, t, :], ACT.Square, accum_out=ssq[:, t:t + 1]).then_inc(sq_done, 1)
                    act.wait_ge(s["n_var"], at(l, "n_var", t + 1))
                    nc.scalar.activation(rstd[:, t:t + 1], rstd[:, t:t + 1], ACT.Sqrt).then_inc(s["n_std"], 1)

            experts(0)
            next_norm(0)

            def split_w3(n):
                ci, half = n // 2, n % 2
                act.wait_ge(w3_in[ci % 2], 48 * (ci // 2 + 1))
                if n >= 2:
                    act.wait_ge(*((u3_ps, 3 * ci) if half else (u3_half, ci)))
                nc.scalar.activation(w3h[:, half, :, :, :], w3[:, ci % 2, half * KC // 2:(half + 1) * KC // 2, :, :], ACT.Copy).then_inc(w3_hi, 1)

            split_w3(0)
            split_w3(1)
            act.wait_ge(acol_in, 64)
            act.wait_ge(ada_col, 2)
            for k in range(KC):
                act.wait_ge(t_ps, 2 * KC + k + 1)
                if k >= 2:
                    act.wait_ge(aT_lo, k - 1)
                nc.scalar.activation(aTf[:, k % 2, :], bank(k % 2), ACT.Identity,
                                     scale=acol[:, 1, 0, k:k + 1], bias=acol[:, 0, 0, k:k + 1]).then_inc(t_out, 1)
                act.wait_ge(t_out, 2 * KC + k + 1)
                nc.scalar.activation(aTh[:, k, :], aTf[:, k % 2, :], ACT.Copy).then_inc(aT_hi, 1)
            for ci in range(SCC):
                if ci + 1 < SCC:
                    split_w3(2 * ci + 2)
                act.wait_ge(u3_ps, 3 * ci + 1)
                if ci >= 2:
                    act.wait_ge(z_out, ci - 1)
                nc.scalar.activation(cgs[:, ci % 2, :], bank(2 + 3 * (ci % 2) + 1), ACT.Copy).then_inc(cg_out, 1)
                if ci + 1 < SCC:
                    split_w3(2 * ci + 3)
            experts(1)
            next_norm(1)

        @block.vector
        def _(dve):
            chain, steps = sem("dve_step"), [0]

            def mark(ins):
                steps[0] += 1
                ins.then_inc(chain, 1)

            def link(ins):
                mark(ins)
                dve.wait_ge(chain, steps[0])

            V = nc.vector

            def ada_row_of(m, src):
                dve.wait_ge(ada_ps, m + 1)
                if m >= 2:
                    dve.wait_ge(mod_st[m % 2], 16 * (m // 2))
                V.tensor_tensor(mrow[:, m % 2, :], src[0:2, :], adab[:, m % 2, :], ALU.add).then_inc(ada_row, 1)

            def column_gains(l):
                dve.wait_ge(q_const, 48)
                dve.wait_ge(acol_in, 32 * (l + 1))
                for r in range(2):
                    ins = V.scalar_tensor_tensor(acol[:, SC1, r, :], acol[:, SC1, r, :], 1.0, nwcol[:, l, :], ALU.add, ALU.mult)
                ins.then_inc(ada_col, 1)

            for m in range(2):
                ada_row_of(m, bank(m % 2))
            dve.wait_ge(sq_done, TT + TC)
            link(V.tensor_scalar(rstd[:, 0:TT + TC], ssq[:, 0:TT + TC], 1.0 / D, EPS, ALU.mult, ALU.add))
            V.reciprocal(rstd[:, 0:TT + TC], rstd[:, 0:TT + TC]).then_inc(var_done, 1)
            dve.wait_ge(std_done, 1)
            for t in range(TT + TC):
                V.tensor_scalar(rn[:, t, :], h[:, t, :] if t < TT else hc[:, t - TT, :], rstd[:, t:t + 1], None, ALU.mult).then_inc(rn_done, 1)
            for m in range(2, FIRST):
                ada_row_of(m, bank(m % 2))
            column_gains(0)
            dve.wait_ge(cw_ps, 1)
            V.tensor_copy(cvw[:, :, :], bank(6)[:, 0:CC * 40].rearrange("p (c n) -> p c n", n=40)[:, :, 0:TAPS + 3]).then_inc(cw_out, 1)
            V.tensor_copy(odw[:, :, :], bank(6)[:, 256:256 + SCC * 4].rearrange("p (c n) -> p c n", n=4)[:, :, 0:3]).then_inc(cw_out, 1)

            dve.wait_ge(lat_sq, 2 * TT + TC)
            q0, k0 = 8, 8 + TT
            mark(V.tensor_scalar(rstd[:, q0:k0], ssq[:, q0:k0], 1.0 / QL, EPS, ALU.mult, ALU.add))
            link(V.tensor_scalar(rstd[:, k0:k0 + TT + TC], ssq[:, k0:k0 + TT + TC], 1.0 / KVL, EPS, ALU.mult, ALU.add))
            V.reciprocal(rstd[:, q0:k0 + TT + TC], rstd[:, q0:k0 + TT + TC]).then_inc(lat_var, 1)
            dve.wait_ge(lat_std, 1)
            for t in range(TT + TC):
                V.tensor_scalar(cqs[:, t, QL:], cqs[:, t, QL:], rstd[:, k0 + t:k0 + t + 1], None, ALU.mult).then_inc(lat_n, 1)
                if t < TT:
                    V.tensor_scalar(cqs[:, t, 0:QL], cqs[:, t, 0:QL], rstd[:, q0 + t:q0 + t + 1], None, ALU.mult).then_inc(lat_n, 1)
            dve.wait_ge(kr_ps, 2)
            R0, R1, R2 = NOPE, NOPE + ROPE, NOPE + 2 * ROPE
            mark(V.tensor_tensor(rt[R0:R1, 0, :], bank(4)[R0:R1, :], rope[R0:R1, :], ALU.mult))
            link(V.tensor_tensor(rt[R0:R1, 1, :], bank(4)[R1:R2, :], rope[R1:R2, :], ALU.mult))
            V.tensor_tensor(krT[R0:R1, NCTX:], rt[R0:R1, 0, :], rt[R0:R1, 1, :], ALU.add).then_inc(kr_out, 1)
            dve.wait_ge(pool_set, 6)
            for ci in range(CC):
                dve.wait_ge(sg_out, ci + 1)
                V.tensor_tensor(vpad[:, ci, PAD:PAD + N], bank(6), csg[:, ci % 2, :], ALU.mult).then_inc(v_out, 1)
            for m in range(FIRST, FIRST + MID):
                ada_row_of(m, bank(4 + m % 2))

            def conv_steps():
                for ci in range(CC):
                    dve.wait_ge(v_out, ci + 1)
                    link(V.tensor_scalar(cy[:, ci, :], vpad[:, ci, 0:N], cvw[:, ci, 0:1], cvw[:, ci, TAPS:TAPS + 1], ALU.mult, ALU.add))
                    yield
                    for tap in range(1, TAPS):
                        ins = V.scalar_tensor_tensor(cy[:, ci, :], vpad[:, ci, tap:tap + N], cvw[:, ci, tap:tap + 1], cy[:, ci, :], ALU.mult, ALU.add)
                        if tap < TAPS - 1:
                            link(ins)
                        else:
                            ins.then_inc(cv_done, 1)
                        yield

            conv = conv_steps()
            def query(hd):
                dve.wait_ge(q_ps, hd + 1)
                mark(V.scalar_tensor_tensor(rt[R0:R1, 0, :], bank(5)[R0:R1, :], ATT_SCALE, rope[R0:R1, :], ALU.mult, ALU.mult))
                link(V.scalar_tensor_tensor(rt[R0:R1, 1, :], bank(5)[R1:R2, :], ATT_SCALE, rope[R1:R2, :], ALU.mult, ALU.mult))
                V.tensor_tensor(qT[R0:R1, hd % 2, :], rt[R0:R1, 0, :], rt[R0:R1, 1, :], ALU.add).then_inc(qr_out, 1)

            def head_max(n):
                dve.wait_ge(s_ps, n + 1)
                V.tensor_reduce(stat[:, n % 4, 0:1], pp[n % 2][:, 0:KEYS], AX.X, ALU.max, negate=True).then_inc(mx, 1)

            query(0)
            head_max(0)
            for n in range(TT * HEADS):
                hd, t = n // TT, n % TT
                if t == 2 and hd + 1 < HEADS:
                    query(hd + 1)
                if n + 1 < TT * HEADS:
                    head_max(n + 1)
                for _ in range(4):
                    next(conv, None)
                dve.wait_ge(ex, n + 1)
                link(V.reciprocal(stat[:, n % 4, 2:3], stat[:, n % 4, 1:2]))
                if n % 2:
                    ada_row_of(FIRST + MID + n // 2, bank(5))
                dve.wait_ge(pv_ps, n + 1)
                V.tensor_scalar(oo[:, t, hd * VH:(hd + 1) * VH], bank(4)[:, 0:VH], stat[:, n % 4, 2:3], None, ALU.mult).then_inc(o_out, 1)
            for _ in conv:
                pass
            dve.wait_ge(mean_ps, 1)
            dve.wait_ge(cv_done, CC)
            for ci in range(CC):
                V.tensor_tensor(cy[:, ci, :], cy[:, ci, :], bank(0), ALU.subtract).then_inc(d_done, 1)
            dve.wait_ge(varc_ps, CC)
            V.tensor_scalar(csg[:, 0, :], bank(1), EPS, None, ALU.add).then_inc(cvar, 1)
            dve.wait_ge(cvar, 1)
            V.reciprocal(csg[:, 0, :], csg[:, 0, :]).then_inc(cvar, 1)
            dve.wait_ge(cstd, 1)
            dve.wait_ge(d_done, CC)
            for ci in range(CC):
                V.tensor_tensor(cy[:, ci, :], cy[:, ci, :], csg[:, 0, :], ALU.mult).then_inc(dn, 1)

            def residual(l, tmp, base):
                s = {k: v[l] for k, v in L.items()}

                def variance(t):
                    dve.wait_ge(sq_done, TT + TC + 2 * TT * l + t + 1)
                    link(V.tensor_scalar(rstd[:, t:t + 1], ssq[:, t:t + 1], 1.0 / D, EPS, ALU.mult, ALU.add))
                    V.reciprocal(rstd[:, t:t + 1], rstd[:, t:t + 1]).then_inc(s["f_var"], 1)

                def rows(t):
                    dve.wait_ge(s["f_std"], at(l, "f_std", t + 1))
                    link(V.scalar_tensor_tensor(acc[:, t, :], h[:, t, :], rstd[:, t:t + 1], a2b[:, :], ALU.mult, ALU.mult))
                    V.tensor_tensor(acc[:, t, :], acc[:, t, :], b2b[:, :], ALU.add).then_inc(s["f_done"], 1)

                dve.wait_ge(ab_in, 48 * (l + 1))
                link(V.scalar_tensor_tensor(a2b[:, :], a2b[:, :], 1.0, nrow[:, :], ALU.add, ALU.mult))
                dve.wait_ge(g1_in, 16 * (l + 1))
                for n in range(2 * TT):
                    t, cols = n // 2, slice(n % 2 * HB, (n % 2 + 1) * HB)
                    dve.wait_ge(y_ps, 2 * TT * l + n + 1)
                    V.tensor_tensor(tmp[:, n % 2, :], bank(base + n % 2), g1b[:, cols], ALU.mult).then_inc(y_g, 1)
                    dve.wait_ge(y_g, 2 * TT * l + n + 1)
                    V.tensor_tensor(h[:, t, cols], h[:, t, cols], tmp[:, n % 2, :], ALU.add).then_inc(h_new, 1)
                    if n >= 2:
                        (rows if n % 2 else variance)(t - 1)
                variance(TT - 1)
                rows(TT - 1)

            residual(0, rt, 4)

            def bc(ap, shape):
                return ap.to_broadcast(shape)

            def experts(l):
                s = {k: v[l] for k, v in L.items()}
                dve.wait_ge(s["rw_hi"], at(l, "rw_hi", 1))
                V.tensor_tensor(rwl[:, :, :], rw[:, :, :], rwh[:, :, :].bitcast(f32), ALU.subtract).then_inc(s["rw_lo"], 1)
                cn = Counts(dve, l)

                def split(r, u, seen):
                    for piece in range(2):
                        cols = slice(piece * UNIT // 2, (piece + 1) * UNIT // 2)
                        dve.wait_ge(s["whd" if u == 2 else "whg"], seen + piece + 1)
                        ins = V.tensor_tensor(wl[:, u, cols], raw(r)[:, cols], wh[:, u, cols].bitcast(f32), ALU.subtract)
                    ins.then_inc(s["w_d" if u == 2 else "w_gu"], 1)

                for k in range(KC):
                    dve.wait_ge(s["fT_hi"], at(l, "fT_hi", k + 1))
                    V.tensor_tensor(fTl[:, k, :], bank(k % 2), fTh[:, k, :].bitcast(f32), ALU.subtract).then_inc(s["fT_out"], 1)

                def hidden(b, n):
                    dve.wait_ge(s["s"], n)
                    V.tensor_tensor(hh[:, b, :], bank(2 + b)[:, DE:2 * DE], sg[:, b, :], ALU.mult).then_inc(s["hm"], 1)

                def hidden_lo(b, n):
                    dve.wait_ge(s["h_hi"], n)
                    V.tensor_tensor(hTl[:, b, :, :].rearrange("p j n -> p (j n)"), bank(4 + b)[:, 0:2 * P],
                                    hTh[:, b, :, :].rearrange("p j n -> p (j n)").bitcast(f32), ALU.subtract).then_inc(s["ho"], 1)

                def shared_out(t):
                    dve.wait_ge(s["yp1"], cn.tile(t))
                    if t == 0:
                        dve.wait_ge(s["f_stored"], at(l, "f_stored", 16 * TT))
                    V.tensor_copy(acc[:, t, HB:], bank(7)).then_inc(s["ye1"], 1)

                dve.wait_ge(s["rconst_in"], at(l, "rconst_in", 32))
                dve.wait_ge(s["st_ps"], at(l, "st_ps", 1))
                mark(V.tensor_copy(score.rearrange("p t e -> p (t e)"), bank(5)[:, 0:TT * EXPERTS]))
                link(V.tensor_tensor(sel[:, :, :], bank(5)[:, 0:TT * EXPERTS].rearrange("p (t e) -> p t e", e=EXPERTS), bc(rbias[:, :].unsqueeze(1), [P, TT, EXPERTS]), ALU.add))
                for t in range(TT):
                    for g in range(GROUPS):
                        ins = V.max(out=g8[:, t, g, :], in_=sel[:, t, g * GE:(g + 1) * GE])
                link(ins)
                link(V.tensor_tensor(gsum[:, :, :], g8[:, :, :, 0], g8[:, :, :, 1], ALU.add))
                for t in range(TT):
                    ins = V.max(out=top8[:, t, :], in_=gsum[:, t, :])
                link(ins)
                for t in range(TT):
                    ins = V.max_index(out=idx8[:, t, :], in_max=top8[:, t, :], in_values=gsum[:, t, :])
                link(ins)
                link(V.tensor_copy(idxf[:, :, :], idx8[:, :, :]))
                link(V.tensor_tensor(geq[:, :, :, :], bc(iota_row[:, 0:GROUPS].unsqueeze(1).unsqueeze(3), [P, TT, GROUPS, TOPG]),
                                     bc(idxf[:, :, 0:TOPG].unsqueeze(2), [P, TT, GROUPS, TOPG]), ALU.is_equal))
                link(V.tensor_reduce(gmask[:, :, :], geq[:, :, :, :], AX.X, ALU.add))
                link(V.tensor_scalar(gmask[:, :, :], gmask[:, :, :], -1.0, 3.0e38, ALU.add, ALU.mult))
                sel4 = sel.rearrange("p t (g e) -> p (t g) e", e=GE)
                link(V.tensor_tensor(sel4, sel4, bc(gmask.rearrange("p t g -> p (t g)").unsqueeze(2), [P, TT * GROUPS, GE]), ALU.add))
                for t in range(TT):
                    ins = V.max(out=top8[:, t, :], in_=sel[:, t, :])
                link(ins)
                for t in range(TT):
                    ins = V.max_index(out=idx8[:, t, :], in_max=top8[:, t, :], in_values=sel[:, t, :])
                link(ins)
                link(V.tensor_copy(idxf[:, :, :], idx8[:, :, :]))
                full = [P, TT, TOPK, EXPERTS]
                for t in range(TT):
                    ins = V.tensor_tensor(eq[:, t, :, :], bc(iota_row[:, 0:EXPERTS].unsqueeze(1), full[:1] + full[2:]),
                                          bc(idxf[:, t, 0:TOPK].unsqueeze(2), full[:1] + full[2:]), ALU.is_equal)
                link(ins)
                for t in range(TT):
                    ins = V.tensor_reduce(mask[:, t, :], eq[:, t, :, :].rearrange("p k e -> p e k"), AX.X, ALU.add)
                ins.then_inc(s["rk_in"], 1)
                hidden(0, cn.tile(0))
                hidden(1, cn.tile(1))
                dve.wait_ge(s["rk_ps"], at(l, "rk_ps", 1))
                cnt = bank(0)[:, 0:EXPERTS]
                link(V.tensor_copy(pend[:, :], cnt))
                link(V.tensor_scalar(nblk[:, :], pend[:, :], 0.0, None, ALU.is_gt))
                for q in range(1, TT):
                    link(V.scalar_tensor_tensor(nblk[:, :], pend[:, :], float(q * P), nblk[:, :], ALU.is_gt, ALU.add))
                link(V.tensor_tensor_scan(pend[:, :], ones[:, 0:EXPERTS], nblk[:, :], 0.0, ALU.mult, ALU.add))
                link(V.tensor_scalar(below_e[:, :], pend[:, :], iota_part[:, 0:1], None, ALU.is_le, ALU.add, accum_out=becol[:, :]))
                V.tensor_tensor(bst[:, :], pend[:, :], nblk[:, :], ALU.subtract).then_inc(s["rt"], 1)
                dve.wait_ge(s["rt"], at(l, "rt", 1))
                hidden_lo(0, cn.tile(0))
                hidden_lo(1, cn.tile(1))
                link(V.tensor_scalar(bst[:, :], bst[:, :], float(P), None, ALU.mult))
                V.tensor_tensor(sel[:, :, :], bank(1)[:, 0:TT * EXPERTS].rearrange("p (t e) -> p t e", e=EXPERTS),
                                bc(bst[:, :].unsqueeze(1), [P, TT, EXPERTS]), ALU.add).then_inc(s["places"], 1)
                dve.wait_ge(s["places"], at(l, "places", 1))
                for t in range(TT):
                    ins = V.tensor_tensor(eqw[:, t, :, :], eq[:, t, :, :], bc(sel[:, t, :].unsqueeze(1), full[:1] + full[2:]), ALU.mult)
                link(ins)
                link(V.tensor_reduce(code[:, :].rearrange("p (t k) -> p t k", k=TOPK), eqw[:, :, :, :], AX.X, ALU.add))
                link(V.tensor_copy(codei[:, 0, :], code[:, :]))
                link(V.tensor_scalar(codei[:, 1, :], codei[:, 0, :], P - 1, None, ALU.bitwise_and))
                link(V.tensor_copy(slotf[:, :], codei[:, 1, :]))
                link(V.tensor_scalar(codei[:, 1, :], codei[:, 0, :], 7, None, ALU.logical_shift_right))
                link(V.tensor_copy(blkf[:, :], codei[:, 1, :]))
                for n in range(TT * TOPK):
                    if n >= 4:
                        dve.wait_ge(s["hot_used"], at(l, "hot_used", n - 3))
                    t, k = n // TOPK, n % TOPK
                    V.tensor_scalar(hot_s[:, n % 4, :], iota_row[:, :], slotf[:, n:n + 1], None, ALU.is_equal).then_inc(s["hot"], 1)
                    V.tensor_scalar(hot_b[:, n % 4, :], iota_row[:, 0:COLS], blkf[:, n:n + 1], pair_val[:, t, k:k + 1], ALU.is_equal, ALU.mult).then_inc(s["hot"], 1)
                hidden(0, cn.tile(2))
                hidden(1, cn.tile(3))
                dve.wait_ge(s["be_ps"], at(l, "be_ps", 1))
                V.tensor_scalar(etab[:, :], bank(1)[0:1, 256:256 + COLS], float(EXPERTS - 1), None, ALU.min).then_inc(s["tables"], 1)
                link(V.tensor_scalar(last_loop_pair[:, 2 * l + 1:2 * l + 2], pend[0:1, EXPERTS - 1:EXPERTS], -3.0, None, ALU.add))
                V.tensor_scalar(last_loop_pair[:, 2 * l:2 * l + 1], last_loop_pair[:, 2 * l + 1:2 * l + 2], 1, None, ALU.logical_shift_right).then_inc(s["tables"], 1)
                dve.wait_ge(s["hot_used"], at(l, "hot_used", TT * TOPK))
                V.tensor_scalar(vtab[:, :], bank(0)[:, 0:COLS], float(EMPTY), None, ALU.add).then_inc(s["tables"], 1)
                dve.wait_ge(s["tables"], at(l, "tables", 3))
                V.tensor_scalar(ttab[:, :], vtab[:, :], 3, None, ALU.logical_shift_right).then_inc(s["tables"], 1)

                shared_out(0)
                shared_out(1)
                hidden_lo(0, cn.tile(2))
                hidden_lo(1, cn.tile(3))
                for t in range(TT):
                    link(V.tensor_tensor(eqs[:, :, :], eq[:, t, :, :], bc(score[:, t, :].unsqueeze(1), full[:1] + full[2:]), ALU.mult))
                    link(V.tensor_reduce(wts[:, t, :], eqs[:, :, :], AX.X, ALU.add))
                link(V.tensor_reduce(wsum[:, :], wts[:, :, :], AX.X, ALU.add))
                link(V.reciprocal(wsum[:, :], wsum[:, :]))
                link(V.tensor_scalar(wsum[:, :], wsum[:, :], ROUTED_SCALE, None, ALU.mult))
                link(V.tensor_tensor(wts[:, :, :], wts[:, :, :], bc(wsum[:, :].unsqueeze(2), [P, TT, TOPK]), ALU.mult))
                shared_out(2)
                shared_out(3)
                dve.wait_ge(s["tables"], at(l, "tables", 4))
                last = dve.value_load(last_loop_pair[0:1, 2 * l:2 * l + 1], min_val=10, max_val=MAXP - 2) + 1

                def rows_lo(b, i):
                    for g in range(2):
                        dve.wait_ge(s["x_hi"], 2 * cn.n(b, i) + g + 1)
                        part = slice(g * KC // 2, (g + 1) * KC // 2)
                        V.tensor_tensor(xTl[:, b, part, :].rearrange("p k n -> p (k n)"), bank(g),
                                        xTh[:, b, part, :].rearrange("p k n -> p (k n)").bitcast(f32), ALU.subtract).then_inc(s["x_lo"], 1)

                def unit(b, i, u):
                    split(3 * b + u, u, 2 * cn.split(b, i, u) - 2)

                def step(b, i, first=False, last=False, last_pair=False):
                    if not first:
                        hidden_lo(prior(b, i)[0], cn.block(*prior(b, i)))
                    if not last:
                        unit(*after(b, i), 0)
                        rows_lo(*after(b, i))
                    hidden(b, cn.block(b, i))
                    if not last:
                        unit(*after(b, i), 1)
                    unit(b, i, 2)

                rows_lo(0, 0)
                for u in range(2):
                    unit(0, 0, u)
                run_blocks(dve, last, step)
                hidden_lo(1, cn.block(1, last))
                def variance(t):
                    dve.wait_ge(sq_done, 2 * TT + TC + 2 * TT * l + t + 1)
                    link(V.tensor_scalar(rstd[:, t:t + 1], ssq[:, t:t + 1], 1.0 / D, EPS, ALU.mult, ALU.add))
                    V.reciprocal(rstd[:, t:t + 1], rstd[:, t:t + 1]).then_inc(s["n_var"], 1)
                    if l + 1 == DEPTH:
                        dve.wait_ge(s["n_std"], at(l, "n_std", t + 1))
                        dve.wait_ge(fw_in, 16)
                        V.scalar_tensor_tensor(h[:, t, :], h[:, t, :], rstd[:, t:t + 1], b2b[:, :], ALU.mult, ALU.mult).then_inc(fin_o, 1)

                dve.wait_ge(s["ye0"], cn.tile(TT - 1))
                for t in range(TT):
                    for k in range(TOPK):
                        if k % (TOPK // 2) == 0:
                            name = f"yl_in{t % 2}{k // (TOPK // 2)}"
                            dve.wait_ge(s[name], at(l, name, 16 * (t // 2 + 1)))
                        V.scalar_tensor_tensor(acc[:, t, :], yl[:, t % 2, k, :], wts[:, t, k:k + 1], acc[:, t, :], ALU.mult, ALU.add).then_inc(s["comb"], 1)
                        dve.wait_ge(s["comb"], at(l, "comb", TOPK * t + k + 1))
                    if t:
                        variance(t - 1)
                dve.wait_ge(g2_in, 16 * (l + 1))
                link(V.tensor_tensor(acc[:, TT - 1, :], acc[:, TT - 1, :], g2b[:, :], ALU.mult))
                V.tensor_tensor(h[:, TT - 1, :], h[:, TT - 1, :], acc[:, TT - 1, :], ALU.add).then_inc(s["hlast"], 1)
                variance(TT - 1)

            experts(0)
            dve.wait_ge(L["n_std"][0], TT)
            for t in range(TT):
                V.tensor_scalar(rn1[:, t, :], h[:, t, :], rstd[:, t:t + 1], None, ALU.mult).then_inc(rn_done, 1)
            column_gains(1)

            def split_w3(n):
                ci, half = n // 2, n % 2
                dve.wait_ge(w3_hi, n + 1)
                V.tensor_tensor(w3l[:, half, :, :, :], w3[:, ci % 2, half * KC // 2:(half + 1) * KC // 2, :, :],
                                w3h[:, half, :, :, :].bitcast(f32), ALU.subtract).then_inc(w3_lo, 1)

            split_w3(0)
            split_w3(1)
            for k in range(KC):
                dve.wait_ge(aT_hi, k + 1)
                V.tensor_tensor(aTl[:, k, :], aTf[:, k % 2, :], aTh[:, k, :].bitcast(f32), ALU.subtract).then_inc(aT_lo, 1)
            mark(V.memset(zz[:, :, 0:1], 0.0))
            link(V.memset(zz[:, :, N + 1:], 0.0))
            for ci in range(SCC):
                b = ci % 2
                if ci + 1 < SCC:
                    split_w3(2 * ci + 2)
                dve.wait_ge(cg_out, ci + 1)
                dve.wait_ge(u3_ps, 3 * ci + 2)
                V.tensor_tensor(zz[:, b, 1:N + 1], bank(2 + 3 * b + 2), cgs[:, b, :], ALU.mult).then_inc(z_out, 1)
                dve.wait_ge(z_out, ci + 1)
                link(V.tensor_scalar(zt[:, b, :], zz[:, b, 0:N], odw[:, ci, 0:1], None, ALU.mult))
                for tap in (1, 2):
                    link(V.scalar_tensor_tensor(zt[:, b, :], zz[:, b, tap:tap + N], odw[:, ci, tap:tap + 1], zt[:, b, :], ALU.mult, ALU.add))
                dve.wait_ge(u3_ps, 3 * ci + 3)
                V.tensor_tensor(oT1[:, ci, :], bank(2 + 3 * b), zt[:, b, :], ALU.mult).then_inc(o1_out, 1)
                if ci + 1 < SCC:
                    split_w3(2 * ci + 3)
            residual(1, rt, 0)
            experts(1)


NAMES = ["x", "c", "ctx", "c_ctx", "ada_w", "ada_b", "norm_mix_w", "norm_ffn_w", "ev_w_in", "ev_conv_w", "ev_conv_b", "ev_ln_w",
         "ev_ln_b", "ev_q_norm_w", "ev_kv_norm_w", "ev_w_uq", "ev_w_ukv", "ev_w_out", "od_w_in", "od_conv_w", "od_w_out",
         "router_w", "router_bias", "exp_w_gate", "exp_w_up", "exp_w_down", "sh_w_gate", "sh_w_up", "sh_w_down", "final_norm_w"]
GRID_W, ROPE_BASE = 64, 10000.0


def constants():
    half = ROPE // 2
    inv = (1.0 / (np.float32(ROPE_BASE) ** (np.arange(0, half, 2, dtype=np.float32) / np.float32(half)))).astype(np.float32)
    n = np.arange(N)
    pos = np.stack([n // GRID_W, n % GRID_W]).astype(np.float32)
    ang = (pos[:, None, :] * inv[None, :, None]).astype(np.float32)
    cos, sin = np.cos(ang), np.sin(ang)
    rope = np.zeros((P, N), np.float32)
    rope[NOPE:NOPE + ROPE] = np.stack([cos, cos], 1).reshape(ROPE, N)
    rope[NOPE + ROPE:] = np.stack([-sin, sin], 1).reshape(ROPE, N)
    return {"k_ident": np.eye(P, dtype=np.float32), "k_before": np.triu(np.ones((P, P), np.float32), 1),
            "k_rope": rope}


def kernel(**inputs):
    import concourse.bacc as bacc
    from concourse.bass_utils import run_bass_kernel_spmd

    nc = bacc.Bacc("TRN2", target_bir_lowering=False, num_devices=1)
    arrays = {name: np.ascontiguousarray(inputs[name]) for name in NAMES}
    arrays.update(constants())
    aps = {name: nc.dram_tensor(f"in_{name}", v.shape, mybir.dt.from_np(v.dtype), kind="ExternalInput").ap() for name, v in arrays.items()}
    out = nc.dram_tensor("out", (1, N, D), mybir.dt.float32, kind="ExternalOutput").ap()
    scratch = [[nc.dram_tensor(f"{name}{l}", shape, mybir.dt.float32, kind="Internal").ap() for l in range(DEPTH)]
               for name, shape in (("rows_for_experts", (N, D)), ("rows_of_experts", (N * 8, D)), ("modulation", (2, 6 * D)))]
    build(nc, aps, out, scratch)
    result = run_bass_kernel_spmd(nc, [{f"in_{name}": v for name, v in arrays.items()}], core_ids=[0])
    return result.results[0]["out"]
```
